# Optimizing a Trainium2 kernel written in Bass

```python
import math
import jax, jax.numpy as jnp
from jax import lax
import numpy as np

D_MODEL = 1024
BATCH = 1
SEQ = 256
DEPTH = 1

GRID_W = 64
D_MIX = D_MODEL
EPS = 1e-6
CONV_W = 256
CONV_K = 3
NA_HEADS = 4
NA_DH = 64
NA_W = NA_HEADS * NA_DH
NA_KH = 8
NA_KW = 16
GDN_HEADS = 4
GDN_DK = 128
GDN_DV = 128
GDN_W = GDN_HEADS * GDN_DV
GDN_CONV_K = 3
GDN_CHUNK = 64
GDN_QKV = 2 * GDN_HEADS * GDN_DK + GDN_W
IN_SPLITS = (CONV_W, CONV_W, CONV_W, NA_W, NA_W, NA_W, GDN_QKV, GDN_W, 2 * GDN_HEADS, 2 * GDN_HEADS)
D_IN = 3 * CONV_W + 3 * NA_W + GDN_QKV + GDN_W + 4 * GDN_HEADS
N_GROUPS = 4
EXPERTS_PER_GROUP = 8
N_EXPERTS = N_GROUPS * EXPERTS_PER_GROUP
TOP_K = 2
D_EXPERT = 512
MOE_BLOCK = 256


def _rmsnorm(x, w):
    xf = x.astype(jnp.float32)
    y = xf * lax.rsqrt(jnp.mean(xf * xf, axis=-1, keepdims=True) + EPS)
    return (y * w.astype(jnp.float32)).astype(x.dtype)

def _l2norm(x):
    xf = x.astype(jnp.float32)
    return xf * lax.rsqrt(jnp.sum(xf * xf, axis=-1, keepdims=True) + EPS)

def _dwconv(x, w):
    ch = x.shape[-1]
    return lax.conv_general_dilated(x, w[:, None, :].astype(x.dtype), window_strides=(1,), padding='SAME',
                                    dimension_numbers=('NWC', 'WIO', 'NWC'), feature_group_count=ch)

def _neighbourhood_attention(q, k, v, rpb):
    bsz, t, h, dh = q.shape
    rows = t // GRID_W
    kh = min(NA_KH, rows)
    qg = q.reshape(bsz, rows, GRID_W, h, dh)
    kg = k.reshape(bsz, rows, GRID_W, h, dh)
    vg = v.reshape(bsz, rows, GRID_W, h, dh)
    col = jnp.arange(GRID_W)
    col_idx = jnp.clip(col - NA_KW // 2, 0, GRID_W - NA_KW)[:, None] + jnp.arange(NA_KW)[None, :]
    dc = col_idx - col[:, None] + (NA_KW - 1)
    row_start = jnp.clip(jnp.arange(rows) - kh // 2, 0, rows - kh)
    scale = dh ** -0.5

    def one_row(r):
        rs = row_start[r]
        q_r = lax.dynamic_index_in_dim(qg, r, axis=1, keepdims=False)
        k_rows = lax.dynamic_slice_in_dim(kg, rs, kh, axis=1)
        v_rows = lax.dynamic_slice_in_dim(vg, rs, kh, axis=1)
        k_win = k_rows[:, :, col_idx]
        v_win = v_rows[:, :, col_idx]
        dr = rs + jnp.arange(kh) - r + (NA_KH - 1)
        bias = rpb[:, dr][:, :, dc]
        s = jnp.einsum('bchd,brckhd->bhcrk', q_r, k_win).astype(jnp.float32) * scale
        s = s + jnp.transpose(bias, (0, 2, 1, 3)).astype(jnp.float32)[None]
        p = jax.nn.softmax(s.reshape(bsz, h, GRID_W, kh * NA_KW), axis=-1).reshape(s.shape).astype(v.dtype)
        return jnp.einsum('bhcrk,brckhd->bchd', p, v_win)

    out = lax.map(one_row, jnp.arange(rows))
    return jnp.transpose(out, (1, 0, 2, 3, 4)).reshape(bsz, t, h * dh)

def _gated_delta_chunked(q, k, v, g, beta):
    bsz, h, t, dk = q.shape
    dv = v.shape[-1]
    n = t // GDN_CHUNK
    cs = lambda a: a.reshape((bsz, h, n, GDN_CHUNK) + a.shape[3:])
    q, k, v, g, beta = cs(q), cs(k), cs(v), cs(g), cs(beta)
    g = jnp.cumsum(g, axis=-1)
    idx = jnp.arange(GDN_CHUNK)
    strict = idx[:, None] > idx[None, :]
    incl = idx[:, None] >= idx[None, :]
    diff = g[..., :, None] - g[..., None, :]
    dec_strict = jnp.exp(jnp.where(strict, diff, -jnp.inf))
    dec_incl = jnp.exp(jnp.where(incl, diff, -jnp.inf))
    kb = k * beta[..., None]
    lower = jnp.einsum('bhncd,bhnsd->bhncs', kb, k) * dec_strict
    rhs = jnp.concatenate([v * beta[..., None], kb * jnp.exp(g)[..., None]], axis=-1)
    sol = lax.linalg.triangular_solve(lower, rhs, left_side=True, lower=True, unit_diagonal=True)
    u, w = sol[..., :dv], sol[..., dv:]
    intra = jnp.einsum('bhncd,bhnsd->bhncs', q, k) * dec_incl
    q_dec = q * jnp.exp(g)[..., None]
    g_last = g[..., -1]
    k_dec = k * jnp.exp(g_last[..., None] - g)[..., None]

    def step(state, xs):
        u_c, w_c, intra_c, q_c, k_c, gl_c = xs
        v_new = u_c - jnp.einsum('bhcd,bhde->bhce', w_c, state)
        o_c = jnp.einsum('bhcd,bhde->bhce', q_c, state) + jnp.einsum('bhcs,bhse->bhce', intra_c, v_new)
        state = state * jnp.exp(gl_c)[..., None, None] + jnp.einsum('bhcd,bhce->bhde', k_c, v_new)
        return state, o_c

    xs = tuple(jnp.moveaxis(a, 2, 0) for a in (u, w, intra, q_dec, k_dec, g_last))
    s0 = jnp.zeros((bsz, h, dk, dv), jnp.float32)
    _, o = lax.scan(step, s0, xs)
    return jnp.moveaxis(o, 0, 2).reshape(bsz, h, t, dv)

def _gdn_mixer(qkv, z, a, b, conv_w, a_log, dt_bias, norm_w):
    bsz, t, _ = qkv.shape
    qkv = jax.nn.silu(_dwconv(qkv, conv_w))
    q = qkv[..., :GDN_HEADS * GDN_DK].reshape(bsz, t, GDN_HEADS, GDN_DK)
    k = qkv[..., GDN_HEADS * GDN_DK:2 * GDN_HEADS * GDN_DK].reshape(bsz, t, GDN_HEADS, GDN_DK)
    v = qkv[..., 2 * GDN_HEADS * GDN_DK:].reshape(bsz, t, GDN_HEADS, GDN_DV)
    q = jnp.transpose(_l2norm(q) * (GDN_DK ** -0.5), (0, 2, 1, 3))
    k = jnp.transpose(_l2norm(k), (0, 2, 1, 3))
    v = jnp.transpose(v.astype(jnp.float32), (0, 2, 1, 3))
    a = a.astype(jnp.float32).reshape(bsz, t, 2, GDN_HEADS)
    b = b.astype(jnp.float32).reshape(bsz, t, 2, GDN_HEADS)
    g = -jnp.exp(a_log.astype(jnp.float32)) * jax.nn.softplus(a + dt_bias.astype(jnp.float32))
    beta = jax.nn.sigmoid(b)
    g = jnp.transpose(g, (2, 0, 3, 1))
    beta = jnp.transpose(beta, (2, 0, 3, 1))
    flip = lambda a_: jnp.flip(a_, axis=2)
    o_fwd = _gated_delta_chunked(q, k, v, g[0], beta[0])
    o_bwd = flip(_gated_delta_chunked(flip(q), flip(k), flip(v), flip(g[1]), flip(beta[1])))
    o = jnp.transpose(o_fwd + o_bwd, (0, 2, 1, 3))
    o = o * lax.rsqrt(jnp.mean(o * o, axis=-1, keepdims=True) + EPS) * norm_w.astype(jnp.float32)
    o = o * jax.nn.silu(z.astype(jnp.float32).reshape(bsz, t, GDN_HEADS, GDN_DV))
    return o.reshape(bsz, t, GDN_W).astype(qkv.dtype)

def _hier_moe(h, wg, bg, we, be, w1, w3, w2):
    bsz, t, d = h.shape
    xt = h.reshape(bsz * t, d)
    n = xt.shape[0]
    pg = jax.nn.softmax((xt @ wg + bg).astype(jnp.float32), axis=-1)
    grp = jnp.argmax(pg, axis=-1)
    pg_top = jnp.take_along_axis(pg, grp[:, None], axis=-1)
    el = (xt @ we + be).astype(jnp.float32).reshape(n, N_GROUPS, EXPERTS_PER_GROUP)
    el_grp = jnp.take_along_axis(el, grp[:, None, None], axis=1)[:, 0]
    top_logit, top_e = lax.top_k(el_grp, TOP_K)
    gate = pg_top * jax.nn.softmax(top_logit, axis=-1)
    expert = (grp[:, None] * EXPERTS_PER_GROUP + top_e).reshape(-1)
    n_slots = n * TOP_K
    order = jnp.argsort(expert)
    sorted_e = expert[order]
    tok = order // TOP_K
    sizes = jnp.bincount(expert, length=N_EXPERTS)
    padded = (sizes + MOE_BLOCK - 1) // MOE_BLOCK * MOE_BLOCK
    pad_end = jnp.cumsum(padded)
    pad_start = pad_end - padded
    seg_start = jnp.cumsum(sizes) - sizes
    dest = pad_start[sorted_e] + jnp.arange(n_slots) - seg_start[sorted_e]
    padded_rows = (n_slots + N_EXPERTS * (MOE_BLOCK - 1) + MOE_BLOCK - 1) // MOE_BLOCK * MOE_BLOCK
    n_blocks = padded_rows // MOE_BLOCK
    buf = jnp.zeros((padded_rows, d), xt.dtype).at[dest].set(xt[tok])
    block_e = jnp.minimum(jnp.searchsorted(pad_end, jnp.arange(n_blocks) * MOE_BLOCK, side='right'), N_EXPERTS - 1)

    def expert_block(args):
        xb, e = args
        return (jax.nn.silu(xb @ w1[e]) * (xb @ w3[e])) @ w2[e]

    ys = lax.map(expert_block, (buf.reshape(n_blocks, MOE_BLOCK, d), block_e)).reshape(padded_rows, d)[dest]
    ys = ys * gate.reshape(-1)[order][:, None].astype(ys.dtype)
    return jnp.zeros_like(xt).at[tok].add(ys).reshape(bsz, t, d)

def first_inputs(seed: int = 0) -> dict:
    key = jax.random.key(seed)
    ks = jax.random.split(key, 22)
    f32 = jnp.float32
    nrm = lambda k_, shape, s: jax.random.normal(k_, shape, f32) * s
    x = nrm(ks[0], (BATCH, SEQ, D_MODEL), 1.0)
    c = nrm(ks[1], (BATCH, D_MODEL), 1.0)
    norm_mix_w = 1.0 + nrm(ks[2], (DEPTH, D_MODEL), 0.02)
    norm_ffn_w = 1.0 + nrm(ks[3], (DEPTH, D_MODEL), 0.02)
    w_ada = nrm(ks[4], (DEPTH, D_MODEL, 6 * D_MODEL), 0.5 * D_MODEL ** -0.5)
    b_ada = nrm(ks[5], (DEPTH, 6 * D_MODEL), 0.02)
    w_in = nrm(ks[6], (DEPTH, D_MODEL, D_IN), D_MODEL ** -0.5)
    conv_a_w = nrm(ks[7], (DEPTH, CONV_K, CONV_W), CONV_K ** -0.5)
    na_rpb = nrm(ks[8], (DEPTH, NA_HEADS, 2 * NA_KH - 1, 2 * NA_KW - 1), 0.1)
    gdn_conv_w = nrm(ks[9], (DEPTH, GDN_CONV_K, GDN_QKV), GDN_CONV_K ** -0.5)
    gdn_a_log = jnp.log(jax.random.uniform(ks[10], (DEPTH, 2, GDN_HEADS), f32, 1.0, 16.0))
    dt = jnp.exp(jax.random.uniform(ks[11], (DEPTH, 2, GDN_HEADS), f32, math.log(1e-3), math.log(1e-1)))
    gdn_dt_bias = dt + jnp.log(-jnp.expm1(-dt))
    gdn_norm_w = 1.0 + nrm(ks[12], (DEPTH, GDN_DV), 0.02)
    w_out = nrm(ks[13], (DEPTH, D_MIX, D_MODEL), D_MIX ** -0.5)
    router_group_w = nrm(ks[14], (DEPTH, D_MODEL, N_GROUPS), D_MODEL ** -0.5)
    router_group_b = nrm(ks[15], (DEPTH, N_GROUPS), 0.01)
    router_expert_w = nrm(ks[16], (DEPTH, D_MODEL, N_EXPERTS), D_MODEL ** -0.5)
    router_expert_b = nrm(ks[17], (DEPTH, N_EXPERTS), 0.01)
    expert_w1 = nrm(ks[18], (DEPTH, N_EXPERTS, D_MODEL, D_EXPERT), D_MODEL ** -0.5)
    expert_w3 = nrm(ks[19], (DEPTH, N_EXPERTS, D_MODEL, D_EXPERT), D_MODEL ** -0.5)
    expert_w2 = nrm(ks[20], (DEPTH, N_EXPERTS, D_EXPERT, D_MODEL), D_EXPERT ** -0.5)
    final_norm_w = 1.0 + nrm(ks[21], (D_MODEL,), 0.02)
    return {"x": x, "c": c, "norm_mix_w": norm_mix_w, "norm_ffn_w": norm_ffn_w, "w_ada": w_ada, "b_ada": b_ada,
            "w_in": w_in, "conv_a_w": conv_a_w, "na_rpb": na_rpb, "gdn_conv_w": gdn_conv_w,
            "gdn_a_log": gdn_a_log, "gdn_dt_bias": gdn_dt_bias, "gdn_norm_w": gdn_norm_w, "w_out": w_out,
            "router_group_w": router_group_w, "router_group_b": router_group_b,
            "router_expert_w": router_expert_w, "router_expert_b": router_expert_b,
            "expert_w1": expert_w1, "expert_w3": expert_w3, "expert_w2": expert_w2, "final_norm_w": final_norm_w}

def first_block(x, c, norm_mix_w, norm_ffn_w, w_ada, b_ada, w_in, conv_a_w, na_rpb, gdn_conv_w, gdn_a_log,
              gdn_dt_bias, gdn_norm_w, w_out, router_group_w, router_group_b, router_expert_w, router_expert_b,
              expert_w1, expert_w3, expert_w2, final_norm_w):
    bsz, t, _ = x.shape
    cond = jax.nn.silu(c)
    split_at = np.cumsum(IN_SPLITS)[:-1].tolist()
    for l in range(DEPTH):
        mod = cond @ w_ada[l] + b_ada[l]
        shift1, scale1, gate1, shift2, scale2, gate2 = [m[:, None, :] for m in jnp.split(mod, 6, axis=-1)]
        hmix = _rmsnorm(x, norm_mix_w[l]) * (1.0 + scale1) + shift1
        proj = hmix @ w_in[l]
        cb, cc, cx, nq, nk, nv, gqkv, gz, ga, gb = jnp.split(proj, split_at, axis=-1)
        y_conv = cb * _dwconv(cc * cx, conv_a_w[l])
        y_na = _neighbourhood_attention(nq.reshape(bsz, t, NA_HEADS, NA_DH), nk.reshape(bsz, t, NA_HEADS, NA_DH),
                                        nv.reshape(bsz, t, NA_HEADS, NA_DH), na_rpb[l])
        y_gdn = _gdn_mixer(gqkv, gz, ga, gb, gdn_conv_w[l], gdn_a_log[l], gdn_dt_bias[l], gdn_norm_w[l])
        mixed = jnp.concatenate([y_conv, y_na, y_gdn], axis=-1) @ w_out[l]
        x = x + gate1 * mixed
        hffn = _rmsnorm(x, norm_ffn_w[l]) * (1.0 + scale2) + shift2
        y_moe = _hier_moe(hffn, router_group_w[l], router_group_b[l], router_expert_w[l], router_expert_b[l],
                          expert_w1[l], expert_w3[l], expert_w2[l])
        x = x + gate2 * y_moe
    return _rmsnorm(x, final_norm_w)


GLA_HEADS = 4
GLA_DK = 64
GLA_DV = 128
GLA_RANK = 16
GLA_TAU = 16.0
GLA_CHUNK = 64
MOBA_HEADS = 8
MOBA_HD = 64
MOBA_BLOCK = 256
MOBA_TOPK = 3
MOBA_QCHUNK = 64
ROPE_THETA = 10000.0
MIX_WIDTH = GLA_HEADS * GLA_DV + MOBA_HEADS * MOBA_HD
IN_SPLITS_2 = (GLA_HEADS * GLA_DK, GLA_HEADS * GLA_DK, GLA_HEADS * GLA_DV, GLA_HEADS * GLA_DV,
             GLA_RANK, MOBA_HEADS * MOBA_HD, MOBA_HEADS * MOBA_HD, MOBA_HEADS * MOBA_HD)
IN_WIDTH = sum(IN_SPLITS_2)
PEER_HEADS = 8
PEER_NKEYS = 128
PEER_N = PEER_NKEYS * PEER_NKEYS
PEER_QDIM = 256
PEER_TOPK = 16
PEER_TOKCHUNK = 128


def rmsnorm(x, w):
    xf = x.astype(jnp.float32)
    y = xf * lax.rsqrt(jnp.mean(xf * xf, axis=-1, keepdims=True) + EPS)
    return (y * w.astype(jnp.float32)).astype(x.dtype)

def rope(x, pos):
    hd = x.shape[-1]
    half = hd // 2
    inv = ROPE_THETA ** (-jnp.arange(half, dtype=jnp.float32) / half)
    ang = pos.astype(jnp.float32)[:, None] * inv[None, :]
    cos, sin = jnp.cos(ang), jnp.sin(ang)
    xf = x.astype(jnp.float32)
    x1, x2 = xf[..., :half], xf[..., half:]
    return jnp.concatenate([x1 * cos - x2 * sin, x2 * cos + x1 * sin], axis=-1).astype(x.dtype)

def to_heads(t, h):
    b, s, _ = t.shape
    return t.reshape(b, s, h, -1).transpose(0, 2, 1, 3)

def from_heads(t):
    b, h, s, d = t.shape
    return t.transpose(0, 2, 1, 3).reshape(b, s, h * d)

def gla_chunked(q, k, v, log_a):
    B, H, S, dk = q.shape
    dv = v.shape[-1]
    C = GLA_CHUNK
    nc = S // C
    q, k, g = (t.reshape(B, H, nc, C, dk) for t in (q, k, log_a))
    v = v.reshape(B, H, nc, C, dv)
    b = jnp.cumsum(g, axis=3)
    b_last = b[:, :, :, -1:, :]
    q_d = q * jnp.exp(b) * (dk ** -0.5)
    k_in = k * jnp.exp(-b)
    k_st = k * jnp.exp(b_last - b)
    causal = jnp.tril(jnp.ones((C, C), dtype=bool))
    A = jnp.where(causal, jnp.einsum('bhnid,bhnjd->bhnij', q_d, k_in), 0.0)
    o_intra = jnp.einsum('bhnij,bhnje->bhnie', A, v)
    upd = jnp.einsum('bhncd,bhnce->bhnde', k_st, v)
    decay = jnp.exp(b_last[:, :, :, 0, :])

    def step(state, inp):
        dec, u = inp
        return dec[..., None] * state + u, state

    init = jnp.zeros((B, H, dk, dv), jnp.float32)
    _, s_before = lax.scan(step, init, (jnp.moveaxis(decay, 2, 0), jnp.moveaxis(upd, 2, 0)))
    s_before = jnp.moveaxis(s_before, 0, 2)
    o_inter = jnp.einsum('bhncd,bhnde->bhnce', q_d, s_before)
    return (o_intra + o_inter).reshape(B, H, S, dv)

def moba_attention(q, k, v):
    B, H, S, hd = q.shape
    Sp = ((S + MOBA_BLOCK - 1) // MOBA_BLOCK) * MOBA_BLOCK
    padw = ((0, 0), (0, 0), (0, Sp - S), (0, 0))
    q, k, v = (jnp.pad(t, padw) for t in (q, k, v))
    nb = Sp // MOBA_BLOCK
    K = min(MOBA_TOPK, nb)
    kb = k.reshape(B, H, nb, MOBA_BLOCK, hd)
    vb = v.reshape(B, H, nb, MOBA_BLOCK, hd)
    kbar = jnp.mean(kb.astype(jnp.float32), axis=3)
    scale = hd ** -0.5
    bi = jnp.arange(B)[:, None, None, None]
    hi = jnp.arange(H)[None, :, None, None]
    nq = Sp // MOBA_QCHUNK

    def one_chunk(c):
        q0 = c * MOBA_QCHUNK
        qc = lax.dynamic_slice_in_dim(q, q0, MOBA_QCHUNK, axis=2)
        blk = q0 // MOBA_BLOCK
        bscore = jnp.einsum('bhqd,bhnd->bhqn', qc.astype(jnp.float32), kbar)
        bscore = jnp.where(jnp.arange(nb) < blk, bscore, -jnp.inf)
        _, idx = lax.top_k(bscore, K)
        valid = jnp.arange(K) < blk
        kg = kb[bi, hi, idx]
        vg = vb[bi, hi, idx]
        s_sel = jnp.einsum('bhqd,bhqkld->bhqkl', qc, kg).astype(jnp.float32) * scale
        s_sel = jnp.where(valid[:, None], s_sel, -jnp.inf)
        k_own = lax.dynamic_index_in_dim(kb, blk, axis=2, keepdims=False)
        v_own = lax.dynamic_index_in_dim(vb, blk, axis=2, keepdims=False)
        s_own = jnp.einsum('bhqd,bhld->bhql', qc, k_own).astype(jnp.float32) * scale
        qpos = q0 + jnp.arange(MOBA_QCHUNK)
        kpos = blk * MOBA_BLOCK + jnp.arange(MOBA_BLOCK)
        s_own = jnp.where(kpos[None, :] <= qpos[:, None], s_own, -jnp.inf)
        logits = jnp.concatenate([s_sel.reshape(B, H, MOBA_QCHUNK, K * MOBA_BLOCK), s_own], axis=-1)
        p = jax.nn.softmax(logits, axis=-1).astype(v.dtype)
        p_sel = p[..., :K * MOBA_BLOCK].reshape(B, H, MOBA_QCHUNK, K, MOBA_BLOCK)
        p_own = p[..., K * MOBA_BLOCK:]
        return (jnp.einsum('bhqkl,bhqkld->bhqd', p_sel, vg)
                + jnp.einsum('bhql,bhld->bhqd', p_own, v_own))

    out = lax.map(one_chunk, jnp.arange(nq))
    out = jnp.moveaxis(out, 0, 2).reshape(B, H, Sp, hd)
    return out[:, :, :S]

def peer_ffn(xn, w_query, subkeys, u_tab, v_tab):
    B, S, D = xn.shape
    T = B * S
    xt = xn.reshape(T, D)
    q = (xt @ w_query).reshape(T, PEER_HEADS, 2, PEER_QDIM // 2)
    s = jnp.einsum('thpd,hpkd->thpk', q, subkeys).astype(jnp.float32)
    sv, si = lax.top_k(s, PEER_TOPK)
    cand = (sv[:, :, 0, :, None] + sv[:, :, 1, None, :]).reshape(T, PEER_HEADS, PEER_TOPK * PEER_TOPK)
    cand_id = (si[:, :, 0, :, None] * PEER_NKEYS + si[:, :, 1, None, :]).reshape(T, PEER_HEADS, PEER_TOPK * PEER_TOPK)
    top_s, pos = lax.top_k(cand, PEER_TOPK)
    expert = jnp.take_along_axis(cand_id, pos, axis=-1)
    gate = jax.nn.softmax(top_s, axis=-1)
    nchunk = T // PEER_TOKCHUNK

    def apply(args):
        xc, ec, gc = args
        ug = u_tab[ec]
        vg = v_tab[ec]
        act = jax.nn.gelu(jnp.einsum('thkd,td->thk', ug, xc).astype(jnp.float32), approximate=False)
        w = (gc * act).astype(vg.dtype)
        return jnp.einsum('thk,thkd->td', w, vg)

    out = lax.map(apply, (xt.reshape(nchunk, PEER_TOKCHUNK, D),
                          expert.reshape(nchunk, PEER_TOKCHUNK, PEER_HEADS, PEER_TOPK),
                          gate.reshape(nchunk, PEER_TOKCHUNK, PEER_HEADS, PEER_TOPK)))
    return out.reshape(B, S, D)

def second_inputs(seed: int = 0) -> dict:
    key = jax.random.key(seed)
    ks = jax.random.split(key, 15)
    L, D = DEPTH, D_MODEL
    nrm = jax.random.normal
    return {
        "x": nrm(ks[0], (BATCH, SEQ, D), jnp.float32),
        "norm1_w": 1.0 + 0.02 * nrm(ks[1], (L, D), jnp.float32),
        "w_in": nrm(ks[2], (L, D, IN_WIDTH), jnp.float32) * D ** -0.5,
        "gla_w_alpha": nrm(ks[3], (L, GLA_RANK, GLA_HEADS * GLA_DK), jnp.float32) * GLA_RANK ** -0.5,
        "gla_b_alpha": 0.1 * nrm(ks[4], (L, GLA_HEADS * GLA_DK), jnp.float32),
        "gla_out_norm_w": 1.0 + 0.02 * nrm(ks[5], (L, GLA_DV), jnp.float32),
        "moba_q_norm_w": 1.0 + 0.02 * nrm(ks[6], (L, MOBA_HD), jnp.float32),
        "moba_k_norm_w": 1.0 + 0.02 * nrm(ks[7], (L, MOBA_HD), jnp.float32),
        "mix_scale": 1.0 + 0.02 * nrm(ks[8], (L, MIX_WIDTH), jnp.float32),
        "w_out": nrm(ks[9], (L, MIX_WIDTH, D), jnp.float32) * MIX_WIDTH ** -0.5,
        "norm2_w": 1.0 + 0.02 * nrm(ks[10], (L, D), jnp.float32),
        "peer_w_query": nrm(ks[11], (L, D, PEER_HEADS * PEER_QDIM), jnp.float32) * D ** -0.5,
        "peer_subkeys": nrm(ks[12], (L, PEER_HEADS, 2, PEER_NKEYS, PEER_QDIM // 2), jnp.float32) * (PEER_QDIM // 2) ** -0.5,
        "peer_u": nrm(ks[13], (L, PEER_N, D), jnp.float32) * D ** -0.5,
        "peer_v": nrm(ks[14], (L, PEER_N, D), jnp.float32) * (PEER_HEADS * PEER_TOPK) ** -0.5,
    }

def second_block(x, norm1_w, w_in, gla_w_alpha, gla_b_alpha, gla_out_norm_w, moba_q_norm_w,
              moba_k_norm_w, mix_scale, w_out, norm2_w, peer_w_query, peer_subkeys, peer_u, peer_v):
    B, S, _ = x.shape
    pos = jnp.arange(S)
    offsets = []
    acc = 0
    for w in IN_SPLITS_2[:-1]:
        acc += w
        offsets.append(acc)
    for l in range(DEPTH):
        xn = rmsnorm(x, norm1_w[l])
        proj = xn @ w_in[l]
        gq, gk, gv, ggate, gr, mq, mk, mv = jnp.split(proj, offsets, axis=-1)
        log_a = jax.nn.log_sigmoid((gr @ gla_w_alpha[l] + gla_b_alpha[l]).astype(jnp.float32)) / GLA_TAU
        o_gla = gla_chunked(to_heads(gq, GLA_HEADS).astype(jnp.float32),
                            to_heads(gk, GLA_HEADS).astype(jnp.float32),
                            to_heads(gv, GLA_HEADS).astype(jnp.float32),
                            to_heads(log_a, GLA_HEADS))
        o_gla = from_heads(rmsnorm(o_gla, gla_out_norm_w[l])).astype(x.dtype)
        o_gla = o_gla * jax.nn.silu(ggate)
        qh = rope(rmsnorm(to_heads(mq, MOBA_HEADS), moba_q_norm_w[l]), pos)
        kh = rope(rmsnorm(to_heads(mk, MOBA_HEADS), moba_k_norm_w[l]), pos)
        o_moba = from_heads(moba_attention(qh, kh, to_heads(mv, MOBA_HEADS)))
        mixed = jnp.concatenate([o_gla, o_moba], axis=-1) * mix_scale[l]
        x = x + mixed @ w_out[l]
        x = x + peer_ffn(rmsnorm(x, norm2_w[l]), peer_w_query[l], peer_subkeys[l], peer_u[l], peer_v[l])
    return x


def setup_inputs(seed=0):
    out = dict(first_inputs(seed))
    for name, value in second_inputs(seed + 1).items():
        if name != "x":
            out[name + "_2"] = value
    return out


def reference(
    x, c, norm_mix_w, norm_ffn_w, w_ada, b_ada, w_in, conv_a_w, na_rpb, gdn_conv_w, gdn_a_log,
    gdn_dt_bias, gdn_norm_w, w_out, router_group_w, router_group_b, router_expert_w,
    router_expert_b, expert_w1, expert_w3, expert_w2, final_norm_w, norm1_w_2, w_in_2,
    gla_w_alpha_2, gla_b_alpha_2, gla_out_norm_w_2, moba_q_norm_w_2, moba_k_norm_w_2,
    mix_scale_2, w_out_2, norm2_w_2, peer_w_query_2, peer_subkeys_2, peer_u_2, peer_v_2,
):
    x = first_block(
        x, c, norm_mix_w, norm_ffn_w, w_ada, b_ada, w_in, conv_a_w, na_rpb, gdn_conv_w,
        gdn_a_log, gdn_dt_bias, gdn_norm_w, w_out, router_group_w, router_group_b,
        router_expert_w, router_expert_b, expert_w1, expert_w3, expert_w2, final_norm_w,
    )
    return second_block(
        x, norm1_w_2, w_in_2, gla_w_alpha_2, gla_b_alpha_2, gla_out_norm_w_2, moba_q_norm_w_2,
        moba_k_norm_w_2, mix_scale_2, w_out_2, norm2_w_2, peer_w_query_2, peer_subkeys_2,
        peer_u_2, peer_v_2,
    )


_drawn_inputs = setup_inputs


def setup_inputs(seed=0):
    import zlib

    import numpy as np

    out = dict(_drawn_inputs(seed))
    spreads = {}
    factors = {'norm_mix_w': 4.188,
     'norm_ffn_w': 3.7,
     'na_rpb': 7.917,
     'gdn_a_log': 2.82,
     'gdn_norm_w': 8.0,
     'router_group_b': 8.0,
     'router_expert_b': 28.648,
     'norm1_w_2': 3.247,
     'gla_b_alpha_2': 3.115,
     'gla_out_norm_w_2': 6.069,
     'moba_q_norm_w_2': 8.0,
     'moba_k_norm_w_2': 8.0,
     'mix_scale_2': 16.398,
     'norm2_w_2': 64.0,
     'peer_w_query_2': 3.62,
     'peer_subkeys_2': 3.635,
     'peer_u_2': 4.283,
     'peer_v_2': 3.717}
    for name, (base, spread) in spreads.items():
        noise = np.random.default_rng([zlib.crc32(name.encode()), seed]).standard_normal(out[name].shape)
        drawn = base * np.exp(spread * noise) if base else spread * noise
        out[name] = __import__('jax').numpy.asarray(drawn.astype(out[name].dtype))
    for name, factor in factors.items():
        out[name] = (out[name] * factor).astype(out[name].dtype)
    return out
```

```python
from contextlib import ExitStack

import numpy as np
import concourse.bass as bass
from concourse import mybir

F32 = mybir.dt.float32
U32 = mybir.dt.uint32
ALU = mybir.AluOpType
ACT = mybir.ActivationFunctionType
AX = mybir.AxisListType

P = 128
T = 256
TT = T // P
D = 1024
KC = D // P
EPS = 1e-6
NEG = -1e30
N_MOD = 6 * D // 512
CONV_W = 256
NA_H, NA_DH = 4, 64
ROW_W, N_ROWS = 64, T // 64
NA_KW, NA_KH = 16, 8
N_DR, N_DC = 2 * NA_KH - 1, 2 * NA_KW - 1
GH, GD = 4, 128
LEVELS = 7
W_IN_TILES = 7
N_EXP, N_GRP, EPG = 32, 4, 8
F_OPS = 2 + 2 * 19
S_OPS = 13
CAP = 64
D_EXP = 512
LH, LDK, LDV, CH = 4, 64, 128, 64
AH, AD = 8, 64
PH, PK, PTOP = 8, 128, 16
U_RING, V_RING = 8, 16
RING = 6

_off = 0


def _take(n):
    global _off
    a = _off
    _off += n
    return a


C_ID = _take(P)
C_UINC = _take(P)
C_LINC = _take(P)
C_NEGF = _take(P)
C_NEGB = _take(P)
C_LVL = _take(2 * LEVELS * P)
C_IOTA = _take(P)
C_BLK = _take(P)
C_ONE = _take(P)
C_DN4 = _take(N_GRP)
C_ROPE = _take(4 * 32)
NCONST = _off


def shape_constants():
    c = np.zeros((P, NCONST), np.float32)
    i = np.arange(P)
    c[:, C_ID:C_ID + P] = np.eye(P)
    le = (i[:, None] <= i[None, :])
    ge = le.T
    c[:, C_UINC:C_UINC + P] = le
    c[:, C_LINC:C_LINC + P] = ge
    c[:, C_NEGF:C_NEGF + P] = np.where(le, 0, NEG)
    c[:, C_NEGB:C_NEGB + P] = np.where(ge, 0, NEG)
    for lv in range(LEVELS):
        same = (i[:, None] >> (lv + 1)) == (i[None, :] >> (lv + 1))
        m = same & (((i[:, None] >> lv) & 1) == 0) & (((i[None, :] >> lv) & 1) == 1)
        c[:, C_LVL + lv * P:C_LVL + (lv + 1) * P] = m
        c[:, C_LVL + (LEVELS + lv) * P:C_LVL + (LEVELS + lv + 1) * P] = m.T
    c[:, C_IOTA:C_IOTA + P] = i[None, :]
    c[:, C_BLK:C_BLK + P] = le & ((i[:, None] // 64) == (i[None, :] // 64))
    c[:, C_ONE:C_ONE + P] = 1.0
    c[:, C_DN4:C_DN4 + N_GRP] = 8 - np.arange(N_GRP)
    inv = (np.float32(10000.0) ** (-np.arange(32, dtype=np.float32) / np.float32(32))).astype(np.float32)
    ang = (np.arange(T, dtype=np.float32)[:, None] * inv[None, :]).astype(np.float32)
    for t in range(TT):
        c[:, C_ROPE + t * 32:C_ROPE + (t + 1) * 32] = np.cos(ang[t * P:(t + 1) * P])
        c[:, C_ROPE + 64 + t * 32:C_ROPE + 64 + (t + 1) * 32] = np.sin(ang[t * P:(t + 1) * P])
    return c


def window_selector():
    col = np.arange(ROW_W)
    start = np.clip(col - NA_KW // 2, 0, ROW_W - NA_KW)
    e = np.zeros((N_DC + 1, ROW_W, ROW_W), np.float32)
    for c in range(ROW_W):
        for k in range(ROW_W):
            if start[c] <= k < start[c] + NA_KW:
                e[k - c + NA_KW - 1, c, k] = 1.0
            else:
                e[N_DC, c, k] = NEG
    return e.reshape(N_DC + 1, ROW_W * ROW_W)


class Count:

    def __init__(self, eng, sem, base=0):
        self.eng, self.sem, self.base, self.n = eng, sem, base, 0

    def at(self, base):
        self.base, self.n = base, 0

    def value(self, more=0):
        return self.base + (self.n + more)

    def wait(self, more=0):
        if isinstance(self.base, int) and self.base + self.n + more <= 0:
            return
        self.eng.wait_ge(self.sem, self.base + (self.n + more))


def two_blocks(nc, io):
    ctx = ExitStack()
    with ctx:
        def sb(name, shape, dt=F32):
            return ctx.enter_context(nc.sbuf_tensor(name, shape, dt))

        def sem(name):
            return ctx.enter_context(nc.semaphore(name))

        ring = sb("ring", [P, RING, 4096])
        x = sb("x", [P, TT, D])
        hT = sb("hT", [P, KC, T])
        mod = sb("mod", [P, 4, D])
        nw = sb("nw", [P, D])
        consts = sb("consts_sb", [P, NCONST])
        tail_w = sb("tail_w", [P, KC, 36])
        small = sb("small", [P, 512])
        WORK = 15664
        work = sb("work", [P, WORK])
        ident = consts[:, C_ID:C_ID + P]
        u_inc = consts[:, C_UINC:C_UINC + P]
        l_inc = consts[:, C_LINC:C_LINC + P]

        def W(at, *shape):
            n = 1
            for s in shape:
                n *= s
            assert at + n <= WORK
            v = work[:, at:at + n]
            if len(shape) == 2:
                v = v.rearrange("p (a b) -> p a b", a=shape[0])
            if len(shape) == 3:
                v = v.rearrange("p (a b c) -> p a b c", a=shape[0], b=shape[1])
            return v

        _s = [0]

        def S(n):
            a = _s[0]
            _s[0] += n
            assert _s[0] <= 512
            return small[:, a:a + n]

        sel_w = W(0, 4096)
        bias_rows = W(4096, 4096)
        b_ada = W(8192, 6 * D)
        ab1 = W(3072, 2, D)
        h_tok = W(0, TT, D)
        cond_b = W(14336, KC, P)
        g_raw = W(0, 12, T)
        g_cv = W(3072, 12, T)
        c3 = W(6144, 6, T)
        z = W(7680, TT, 512)
        gab = W(8704, TT, 16)
        NA0 = 9216
        na_q = W(NA0, 4, T)
        na_k = W(NA0 + 1024, 4, T)
        na_v = W(NA0 + 2048, TT, 256)
        na_bias = W(NA0 + 2560, TT, 4, T)
        na_p = W(NA0 + 4608, 4, T)
        na_pT = W(6144, 4, 2, P)
        na_o = W(8768, 4, NA_DH)
        k_tok = W(0, TT, 4, P)
        v_tok = W(1024, TT, 4, P)
        o_acc = W(2048, TT, 4, P)
        sq = W(NA0, 8, T)
        rn = W(NA0 + 2048, 8, T)
        GD0 = NA0
        LT = W(GD0, TT, 4, P)
        X = W(GD0 + 1024, TT, 4, P)
        XT = W(GD0 + 2048, TT, 4, P)
        inT = W(GD0 + 3072, TT, 4, P)
        tB = W(GD0 + 4096, TT, 4, P)
        tU = W(GD0 + 5120, TT, 4, P)
        tD = W(6144, 4, P)
        acc = W(2048, TT, D)
        xeT = W(4096, KC, P)
        pm = W(5120, TT, P)
        pg = W(5376, 2, TT, P)
        pgT = W(5888, TT, P)
        sil = W(6144, D_EXP)
        act_p = W(6656, D_EXP)
        actT = W(7168, 4, P)
        y_sb = W(9984, D)
        sil_d = W(7936, 4, T)
        act_d = W(8960, 4, T)
        _r = [11008]

        def R(*shape):
            n = int(np.prod(shape))
            a = _r[0]
            _r[0] += n
            return W(a, *shape)

        lg = R(TT, 36)
        rb = R(36)
        gmx = R(TT)
        oh4 = R(TT, N_GRP)
        e4 = R(TT, N_GRP)
        pen = R(TT, N_GRP)
        pgt = R(TT)
        elm = R(TT, N_EXP)
        v8 = R(TT, 8)
        i8 = R(TT, 8).bitcast(U32)
        i8f = R(TT, 8)
        gt = R(TT, 4)
        G = R(TT, 36)
        M = R(TT, 36)
        rk = R(TT, 36)
        cnt = R(36)
        rk4 = R(TT, 4)
        g4 = R(TT, 4)
        flag = R(4).bitcast(mybir.dt.int32)
        y2 = W(0, TT, D)
        gq = W(2048, LH, T)
        gk = W(3072, LH, T)
        gv = W(4096, TT, 512)
        ggate = W(5120, TT, 512)
        gb_ = W(6144, LH, T)
        ge = W(7168, LH, T)
        mq = W(8192, TT, 512)
        mk = W(9216, TT, 512)
        mv = W(10240, TT, 512)
        kin = W(11264, LH, T)
        qz = W(12288, LH, 4, P)
        grT = W(12288, T)
        walpha = W(12544, 256)
        AT = W(14336, TT, LH, P)
        kst = W(6656, TT, LH, LDK)
        st = [None, W(7168, LH, LDV), W(7680, LH, LDV), W(6144, LH, LDV)]
        qT = W(12288, AH, T)
        kT = W(2048, AH, T)
        sc = W(4096, AH, T)
        pT = W(6144, AH, 2, P)
        rt = W(14336, 1024)
        NG = PH // 2
        qpT = W(2048, 16, T)
        s_all = W(6144, TT, 16 * PK).rearrange("p t (c k) -> p t c k", k=PK)
        subT = W(10240, 16, PK)
        cand = W(12288, 2 * TT, 16, 16)
        oh = W(13312, 2 * TT, 16, 16)
        sv = W(14336, 4 * TT, 16)
        si = W(14464, 4 * TT, 16).bitcast(U32)
        sif = W(14592, 4 * TT, 16)
        tv = W(14720, 2 * TT, 16)
        ti = W(14784, 2 * TT, 16).bitcast(U32)
        tj = W(14848, 2 * TT, 16).bitcast(U32)
        tif = W(14912, 2 * TT, 16)
        tjf = W(14976, 2 * TT, 16)
        e0 = W(15040, 2 * TT, 16)
        e1 = W(15104, 2 * TT, 16)
        gates = W(15168, 2, TT, 32)
        idx_all = W(15296, 2, TT, 32).bitcast(U32)
        idx_cur = W(15424, TT, 16).bitcast(U32)
        dots = W(15456, TT, 16)
        gel = W(15488, TT, 16)
        w_cur = W(15520, TT, 16)
        gsum = W(15552, 2 * TT)
        junk = W(2048, 2, D)
        diag = W(4096, 4, P)
        zeros = W(4608, P)
        mixT = hT
        gn_w = W(9024, P)
        ones = consts[:, C_ONE:C_ONE + P]
        conv_a = S(6)
        conv_g = S(36)
        cT = S(8)
        a_log = S(8)
        dt_b = S(8)
        rpb = small[:, 448:508]

        ms = S(8)
        rstd = S(8)
        g_e = S(8)
        g_t = S(16)
        g_t2 = S(16)
        g_t3 = S(16)
        g_g = S(16)
        g_be = S(16)
        g_c = S(16)
        g_nc = S(16)
        g_tot = S(16)
        g_eg = S(16)
        g_kd = S(16)
        na_m = S(8)
        na_nm = S(8)
        na_s = S(8)
        na_r = S(8)
        ps = [ctx.enter_context(nc.psum_tensor(f"ps{i}", [P, 512], F32)) for i in range(8)]

        scratch_bias = nc.dram_tensor("bias_scratch", [NA_H * N_DR, ROW_W * ROW_W], F32).ap()

        landed = [sem(f"landed{i}") for i in range(RING)]
        w_used = sem("w_used")
        pe_done = sem("pe_done")
        evac = sem("evac")
        dve_n = sem("dve_n")
        act_n = sem("act_n")
        in_start = sem("in_start")
        in_small = sem("in_small")
        in_bias0 = sem("in_bias0")
        in_nw = sem("in_nw")
        nw_used = sem("nw_used")
        in_tail = sem("in_tail")
        in_ada = sem("in_ada")
        bias_out = sem("bias_out")
        bias_in = sem("bias_in")
        tail_used = sem("tail_used")
        cond_act = sem("cond_act")
        cond_ready = sem("cond_ready")
        bias_ready = sem("bias_ready")
        mod_ready = sem("mod_ready")
        ms_ready = sem("ms_ready")
        rt_ready = sem("rt_ready")
        h_ready = sem("h_ready")
        hT_ready = sem("hT_ready")
        conv_ready = sem("conv_ready")
        silu_ready = sem("silu_ready")
        sq_ready = sem("sq_ready")
        na_sc = sem("na_sc")
        na_exp = sem("na_exp")
        na_pt = sem("na_pt")
        na_out = sem("na_out")
        gab_in = sem("gab_in")
        gab_act = sem("gab_act")
        g_ready = sem("g_ready")
        l2_in = sem("l2_in")
        l2_rt = sem("l2_rt")
        qk_ready = sem("qk_ready")
        d_in = sem("d_in")
        d_out = sem("d_out")
        gd_op = sem("gd_op")
        y_ready = sem("y_ready")
        mix_ready = sem("mix_ready")
        x1_ready = sem("x1_ready")
        out_done = sem("out_done")
        in_route = sem("in_route")
        zeros_ready = sem("zeros_ready")
        gathers = sem("gathers")
        in_nw2 = sem("in_nw2")
        in_tail2 = sem("in_tail2")
        acc_ready = sem("acc_ready")
        rt_logits = sem("rt_logits")
        rt_exp = sem("rt_exp")
        masks_ready = sem("masks_ready")
        flag_ready = sem("flag_ready")
        f_done = sem("f_done")
        f_free = sem("f_free")
        f_dve = sem("f_dve")
        f_act = sem("f_act")
        p_ready = sem("p_ready")
        s_done = sem("s_done")
        s_free = sem("s_free")
        s_dve = sem("s_dve")
        s_act = sem("s_act")
        moe_done = sem("moe_done")
        b2_small = sem("b2_small")
        z_in = sem("z_in")
        z_act = sem("z_act")
        b_in = sem("b_in")
        b_act = sem("b_act")
        gla_op = sem("gla_op")
        o_in = sem("o_in")
        a_in = sem("a_in")
        a_rt = sem("a_rt")
        a_op = sem("a_op")
        a_exp = sem("a_exp")
        mix2_ready = sem("mix2_ready")
        x3_ready = sem("x3_ready")
        in_sub = sem("in_sub")
        e_in = sem("e_in")
        e_act = sem("e_act")
        idx_ready = sem("idx_ready")
        idx_copied = sem("idx_copied")
        u_landed = [sem(f"u_landed{i}") for i in range(U_RING)]
        v_landed = [sem(f"v_landed{i}") for i in range(V_RING)]
        u_free = sem("u_free")
        v_free = sem("v_free")
        gelu_done = sem("gelu_done")
        w_ready = sem("w_ready")
        diag_ready = sem("diag_ready")
        p_done = sem("p_done")
        p_taken = sem("p_taken")

        block = ctx.enter_context(nc.Block())

        w_in_v = io["w_in"].rearrange("(k p) n -> p k n", p=P)
        w_ada_v = io["w_ada"].rearrange("(k p) n -> p k n", p=P)
        w_out_v = io["w_out"].rearrange("(k p) n -> p k n", p=P)
        tiles = [w_ada_v[:, :, n * 512:(n + 1) * 512] for n in range(N_MOD)]
        tiles += [w_in_v[:, :, n * 512:(n + 1) * 512] for n in range(W_IN_TILES)]
        tiles += [w_out_v[:, :, n * 512:(n + 1) * 512] for n in range(2)]

        N_HEAD = len(tiles)
        N_MOE = 3 * N_EXP
        w1_v, w3_v = (io[n].rearrange("e (k p) n -> e p k n", p=P) for n in ("expert_w1", "expert_w3"))
        w2_v = io["expert_w2"].rearrange("e (k p) n -> e p k n", p=P)
        w_in2_v = io["w_in_2"].rearrange("(k p) n -> p k n", p=P)
        w_out2_v = io["w_out_2"].rearrange("(k p) n -> p k n", p=P)
        w_q_v = io["peer_w_query"].rearrange("(k p) n -> p k n", p=P)
        tiles2 = [w_in2_v[:, :, a:a + 512] for a in (0, 512, 1024, 1552, 2064, 2576)]
        tiles2 += [w_out2_v[:, :, n * 512:(n + 1) * 512] for n in range(2)]
        tiles2 += [w_q_v[:, :, n * 512:(n + 1) * 512] for n in range(4)]

        def slot(i, cols=512):
            return ring[:, i % RING, :].rearrange("p (k n) -> p k n", n=cols)

        def u_ring(k):
            return ring[:, 3 + k % U_RING // 4, k % 4 * D:(k % 4 + 1) * D]

        def v_ring(k):
            return ring[:, (5 + k // 4) % RING, k % 4 * D:(k % 4 + 1) * D]

        @block.sync
        def _(sp):
            sp.dma_start(x[:, :, :], io["x"].rearrange("(a p) d -> p a d", p=P)).then_inc(in_start, 16)
            sp.dma_start(cT, io["c"]).then_inc(in_start, 16)
            sp.dma_start(consts[:, :], io["consts"]).then_inc(in_start, 16)
            sp.dma_start(b_ada, io["b_ada"].to_broadcast([P, 6 * D])).then_inc(in_ada, 16)
            sp.dma_start(sel_w[0:32, :], io["window"]).then_inc(in_bias0, 16)
            sp.dma_start(rpb[0:N_DC + 1, :], io["na_rpb"]).then_inc(in_bias0, 16)
            sp.dma_start(nw[:, :], io["norm_mix_w"].to_broadcast([P, D])).then_inc(in_nw, 16)
            for i, src in enumerate(tiles[:N_MOD]):
                if i >= RING:
                    sp.wait_ge(w_used, i - RING + 1)
                sp.dma_start(slot(i), src).then_inc(landed[i % RING], 16)
            sp.dma_start(conv_a, io["conv_a_w"]).then_inc(in_small, 16)
            sp.dma_start(conv_g, io["gdn_conv_w"]).then_inc(in_small, 16)
            sp.dma_start(a_log, io["gdn_a_log"].to_broadcast([P, 8])).then_inc(in_small, 16)
            sp.dma_start(dt_b, io["gdn_dt_bias"].to_broadcast([P, 8])).then_inc(in_small, 16)
            sp.dma_start(tail_w[:, :, 0:16], w_in_v[:, :, 3584:3600]).then_inc(in_tail, 16)
            sp.wait_ge(bias_ready, 1)
            sp.dma_start(scratch_bias, bias_rows[0:NA_H * N_DR, :]).then_inc(bias_out, 16)
            sp.wait_ge(bias_out, 16)
            sp.wait_ge(mod_ready, 1)
            sp.dma_start(gn_w[:, :], io["gdn_norm_w"].to_broadcast([P, P])).then_inc(in_small, 16)
            for r in range(N_ROWS):
                src = scratch_bias.rearrange("(h a) (c k) -> c h a k", h=NA_H, c=ROW_W)[
                    :, :, NA_KH - 1 - r:NA_KH - 1 - r + N_ROWS, :]
                for h in range(NA_H):
                    dst = na_bias[(r % 2) * ROW_W:(r % 2 + 1) * ROW_W, r // 2, h, :]
                    sp.dma_start(dst.rearrange("p (a k) -> p a k", a=N_ROWS), src[:, h, :, :]).then_inc(bias_in, 16)
            for i in range(N_MOD, len(tiles)):
                sp.wait_ge(w_used, i - RING + 1)
                sp.dma_start(slot(i), tiles[i]).then_inc(landed[i % RING], 16)
            with sp.Fori(0, N_EXP // 2) as i:
                for l in range(6):
                    sp.wait_ge(w_used, i * 6 + (N_HEAD + l - RING + 1))
                    e = i * 2 + l % 2
                    v = (w1_v, w3_v, w2_v)[l // 2]
                    sl = (N_HEAD + l) % RING
                    sp.dma_start(slot(sl, 1024 if l >= 4 else 512), v[e, :, :, :]).then_inc(landed[sl], 16)
            for i in range(len(tiles2)):
                n2 = N_HEAD + N_MOE + i
                sp.wait_ge(w_used, n2 - RING + 1)
                sp.dma_start(slot(n2), tiles2[i]).then_inc(landed[n2 % RING], 16)
            out_v = io["out"].rearrange("(a p) d -> p a d", p=P)
            for t in range(TT):
                sp.wait_ge(p_taken, t + 1)
                sp.dma_start(out_v[:, t, :], x[:, t, :]).then_inc(out_done, 16)
            sp.wait_ge(out_done, 32)

        @block.scalar
        def _(act):
            n = [0]

            def o(ins):
                n[0] += 1
                ins.then_inc(act_n, 1)

            def sync():
                act.wait_ge(act_n, n[0])

            norms = [0]

            def norm_roots():
                norms[0] += 1
                act.wait_ge(ms_ready, norms[0])
                act.activation(rstd[:, 0:TT], ms[:, 0:TT], ACT.Sqrt).then_inc(rt_ready, 1)

            act.wait_ge(in_start, 48)
            act.activation(g_e[:, :], cT, ACT.Silu).then_inc(cond_act, 1)
            norm_roots()
            act.wait_ge(gab_in, 1)
            a2 = g_t.rearrange("p (t c) -> p t c", t=TT)
            o(act.activation(g_t2[:, :], g_t, ACT.Abs))
            sync()
            o(act.activation(g_t3[:, :], g_t2, ACT.Exp, scale=-1.0))
            o(act.activation(g_e[:, :], a_log, ACT.Exp))
            sync()
            o(act.activation(g_t2[:, :], g_t3, ACT.Ln, bias=1.0))
            o(act.activation(g_be.rearrange("p (t c) -> p t c", t=TT), gab[:, :, 8:16], ACT.Sigmoid))
            sync()
            act.sem_inc(gab_act, 1)
            act.wait_ge(conv_ready, 1)
            o(act.activation(g_cv[:, :, :], g_cv[:, :, :], ACT.Silu))
            sync()
            act.sem_inc(silu_ready, 1)
            for t in range(TT):
                act.wait_ge(na_sc, t + 1)
                for h in range(NA_H):
                    o(act.activation(na_p[:, h, :], na_p[:, h, :], ACT.Exp, bias=na_nm[:, h:h + 1],
                                     accum_out=na_s[:, h:h + 1]))
                sync()
                act.sem_inc(na_exp, 1)
            act.wait_ge(na_out, 1)
            o(act.activation(sq[:, :, :], g_cv[:, 0:8, :], ACT.Square))
            sync()
            act.sem_inc(sq_ready, 1)
            for j in range(4):
                act.wait_ge(l2_in, j + 1)
                act.activation(rn[:, 2 * j:2 * j + 2, :], rn[:, 2 * j:2 * j + 2, :], ACT.Sqrt).then_inc(l2_rt, 1)
            o(act.activation(z[:, :, :], z[:, :, :], ACT.Silu))
            act.wait_ge(qk_ready, 1)
            o(act.activation(g_eg[:, :], g_c, ACT.Exp))
            o(act.activation(g_kd[:, :], g_kd, ACT.Exp))
            sync()
            act.sem_inc(gab_act, 1)
            m = 0
            for d in range(2):
                for t in range(TT):
                    m += 1
                    act.wait_ge(d_in, m)
                    for h in range(GH):
                        col = t * 8 + d * 4 + h
                        o(act.activation(tD[:, h, :], tD[:, h, :], ACT.Exp, bias=g_nc[:, col:col + 1]))
                    sync()
                    act.sem_inc(d_out, 1)
            act.wait_ge(y_ready, 1)
            act.activation(rstd[:, 0:8], ms[:, 0:8], ACT.Sqrt).then_inc(rt_ready, 1)
            norm_roots()
            act.wait_ge(rt_logits, 1)
            act.activation(e4, e4, ACT.Exp).then_inc(rt_exp, 1)
            act.wait_ge(rt_logits, 2)
            act.activation(gt[:, :, 0:1], gt[:, :, 0:1], ACT.Exp).then_inc(rt_exp, 1)
            act.wait_ge(flag_ready, 1)
            many = act.value_load(flag[0:1, 0:1], min_val=0, max_val=1)
            with act.If(many == 0):
                with act.Fori(0, N_EXP // 4) as i:
                    for p in range(2):
                        jb = 2 + 12 * p
                        act.wait_ge(f_done, i * 24 + (jb + 1))
                        act.activation(sil, ps[jb % 8][:, :], ACT.Silu).then_inc(f_act, 1)
            with act.Else():
                with act.Fori(0, N_EXP // 2) as i:
                    for u in range(2):
                        for c in range(2):
                            act.wait_ge(s_done, i * 16 + (8 * u + c + 1))
                            act.activation(sil_d[:, 2 * c:2 * c + 2, :],
                                           ps[c][:, :].rearrange("p (a b) -> p a b", a=2), ACT.Silu).then_inc(s_act, 1)
            norm_roots()
            norm_roots()
            act.wait_ge(z_in, 1)
            act.activation(ge[0:64], ge[0:64], ACT.Exp, scale=-1.0).then_inc(z_act, 1)
            act.wait_ge(z_act, 1)
            act.activation(ge[0:64], ge[0:64], ACT.Ln, bias=1.0).then_inc(z_act, 1)
            act.wait_ge(b_in, 1)
            act.activation(ge[0:64], gb_[0:64], ACT.Exp).then_inc(b_act, 1)
            act.wait_ge(b_in, 2)
            act.activation(ge[0:64], gb_[0:64], ACT.Exp, scale=-1.0).then_inc(b_act, 1)
            act.wait_ge(b_in, 3)
            act.activation(ge[0:64], ge[0:64], ACT.Exp).then_inc(b_act, 1)
            act.activation(ggate, ggate, ACT.Silu).then_inc(b_act, 1)
            act.wait_ge(o_in, 1)
            act.activation(rstd[:, 0:8], ms[:, 0:8], ACT.Sqrt).then_inc(rt_ready, 1)
            for m in range(2):
                act.wait_ge(a_in, m + 1)
                act.activation(g_t2, g_t2, ACT.Sqrt).then_inc(a_rt, 1)
            for t in range(TT):
                act.wait_ge(a_op, t + 1)
                kw = (t + 1) * P
                for h in range(AH):
                    ins = act.activation(sc[:, h, 0:kw], sc[:, h, 0:kw], ACT.Exp, bias=na_nm[:, h:h + 1],
                                         accum_out=na_s[:, h:h + 1])
                    o(ins)
                sync()
                act.sem_inc(a_exp, 1)
            norm_roots()
            for n2 in range(NG):
                act.wait_ge(e_in, n2 + 1)
                act.activation(gates[:, n2 % 2, :, :], gates[:, n2 % 2, :, :], ACT.Exp).then_inc(e_act, 1)
                with act.Fori(0, 2) as q:
                    for t in range(TT):
                        step = q * TT + (2 * TT * n2 + t)
                        act.wait_ge(u_free, step * 16 + (U_RING + 16))
                        act.activation(gel[:, t, :], dots[:, t, :], ACT.Gelu).then_inc(gelu_done, 1)
                        act.wait_ge(w_ready, step + 1)
                        for k in range(16):
                            act.wait_ge(v_free, step * 16 + (V_RING + k - 3))
                            act.activation(diag[:, k % 4, :], ident, ACT.Copy,
                                           scale=w_cur[:, t, k:k + 1]).then_inc(diag_ready, 1)

        @block.tensor
        def _(pe):
            j = [0]
            w = [0]

            def bank():
                if j[0] >= 8:
                    pe.wait_ge(evac, j[0] - 7)
                return ps[j[0] % 8]

            def full(ins):
                ins.then_inc(pe_done, 1)
                j[0] += 1

            def emptied():
                pe.wait_ge(evac, j[0])

            def weight_tile():
                i = w[0]
                pe.wait_ge(landed[i % RING], 16 * (i // RING + 1))
                w[0] += 1
                return slot(i)

            def transposes_to_hT():
                for t in range(TT):
                    for g in range(2):
                        b = bank()
                        for c in range(4):
                            k = 4 * g + c
                            last = pe.transpose(b[:, c * P:(c + 1) * P], h_tok[:, t, k * P:(k + 1) * P], ident)
                        full(last)

            def feature_major(b, at, wt, c0, n, last_of_tile=False):
                for k in range(KC):
                    last = pe.matmul(b[0:n, at:at + T], wt[:, k, c0:c0 + n], hT[:, k, :],
                                     start=(k == 0), stop=(k == KC - 1))
                return last

            def token_major(b, at, t, wt, c0, n):
                for k in range(KC):
                    last = pe.matmul(b[:, at:at + n], hT[:, k, t * P:(t + 1) * P], wt[:, k, c0:c0 + n],
                                     start=(k == 0), stop=(k == KC - 1))
                return last

            pe.wait_ge(in_start, 48)
            pe.wait_ge(in_bias0, 32)
            pe.wait_ge(cond_ready, 1)
            for n in range(8):
                full(pe.matmul(bank()[0:60, :], rpb[0:32, :], sel_w[0:32, n * 512:(n + 1) * 512],
                               start=True, stop=True))
            for n in range(N_MOD):
                wt = weight_tile()
                b = bank()
                for k in range(KC):
                    last = pe.matmul(b[:, :], cond_b[:, k, :], wt[:, k, :], start=(k == 0), stop=(k == KC - 1))
                full(last)
                pe.wait_ge(pe_done, j[0])
                pe.sem_inc(w_used, 1)
            pe.wait_ge(h_ready, 1)
            transposes_to_hT()
            pe.wait_ge(hT_ready, 1)

            def used():
                pe.wait_ge(pe_done, j[0])
                pe.sem_inc(w_used, 1)

            wt = weight_tile()
            for c in range(2):
                b = bank()
                feature_major(b, 0, wt, c * 256, P)
                full(feature_major(b, T, wt, c * 256 + P, P))
            used()
            wt = weight_tile()
            b = bank()
            feature_major(b, 0, wt, 0, P)
            full(feature_major(b, T, wt, P, P))
            for c in range(2):
                b = bank()
                feature_major(b, 0, wt, 256 + c * P, NA_DH)
                full(feature_major(b, T, wt, 256 + c * P + NA_DH, NA_DH))
            used()
            wt = weight_tile()
            for c in range(2):
                b = bank()
                feature_major(b, 0, wt, c * P, NA_DH)
                full(feature_major(b, T, wt, c * P + NA_DH, NA_DH))
            b = bank()
            token_major(b, 0, 0, wt, 256, 256)
            full(token_major(b, 256, 1, wt, 256, 256))
            used()
            pe.wait_ge(in_tail, 16)
            b = bank()
            token_major(b, 0, 0, tail_w, 0, 16)
            full(token_major(b, 16, 1, tail_w, 0, 16))
            pe.wait_ge(pe_done, j[0])
            pe.sem_inc(tail_used, 1)
            for n in range(3):
                wt = weight_tile()
                for c in range(2):
                    b = bank()
                    feature_major(b, 0, wt, c * 256, P)
                    full(feature_major(b, T, wt, c * 256 + P, P))
                used()
            wt = weight_tile()
            for t in range(TT):
                full(token_major(bank(), 0, t, wt, 0, 512))
            used()
            emptied()
            for t in range(TT):
                for g in range(2):
                    b = bank()
                    for h in (2 * g, 2 * g + 1):
                        last = pe.matmul(b[:, (h % 2) * T:(h % 2 + 1) * T], na_q[0:64, h, t * P:(t + 1) * P],
                                         na_k[0:64, h, :], start=True, stop=True)
                    full(last)
                pe.wait_ge(na_exp, t + 1)
                for g in range(2):
                    b = bank()
                    for h in (2 * g, 2 * g + 1):
                        for kt in range(2):
                            last = pe.transpose(b[:, ((h % 2) * 2 + kt) * P:((h % 2) * 2 + kt + 1) * P],
                                                na_p[:, h, kt * P:(kt + 1) * P], ident)
                    full(last)
                emptied()
                b = bank()
                for h in range(NA_H):
                    for kt in range(2):
                        last = pe.matmul(b[:, h * NA_DH:(h + 1) * NA_DH], na_pT[:, h, kt, :],
                                         na_v[:, kt, h * NA_DH:(h + 1) * NA_DH], start=(kt == 0), stop=(kt == 1))
                full(last)
                emptied()
                b = bank()
                for c in range(2):
                    last = pe.transpose(b[:, c * P:(c + 1) * P],
                                        na_o.rearrange("p a b -> p (a b)")[:, c * P:(c + 1) * P], ident)
                full(last)
            pe.wait_ge(sq_ready, 1)
            for c in range(4):
                b = bank()
                full(pe.matmul(b[:, :], ones[:, :], sq[:, 2 * c:2 * c + 2, :].rearrange("p a b -> p (a b)"),
                               start=True, stop=True))
            b = bank()
            pe.wait_ge(g_ready, 1)
            gg = g_g.rearrange("p (t c) -> p t c", t=TT)
            for t in range(TT):
                pe.matmul(b[:, t * 8:t * 8 + 4], u_inc, gg[:, t, 0:4], start=True, stop=True)
                pe.matmul(b[:, t * 8 + 4:t * 8 + 8], l_inc, gg[:, t, 4:8], start=True, stop=True)
                last = pe.matmul(b[:, 16 + t * 8:24 + t * 8], ones[:, :], gg[:, t, :], start=True, stop=True)
            full(last)
            pe.wait_ge(qk_ready, 1)
            for base in (4, 8):
                for t in range(TT):
                    b = bank()
                    for h in range(GH):
                        last = pe.transpose(b[:, h * P:(h + 1) * P], g_cv[:, base + h, t * P:(t + 1) * P], ident)
                    full(last)
            op = [0]

            def operand():
                op[0] += 1
                pe.wait_ge(gd_op, op[0])

            def heads(lhsT, rhs):
                b = bank()
                for h in range(GH):
                    last = pe.matmul(b[:, h * P:(h + 1) * P], lhsT(h), rhs(h), start=True, stop=True)
                full(last)

            gb = g_be.rearrange("p (t c) -> p t c", t=TT)
            for d in range(2):
                tri = u_inc if d == 0 else l_inc
                for t in range(TT):
                    q = lambda h: g_cv[:, h, t * P:(t + 1) * P]
                    k = lambda h: g_cv[:, 4 + h, t * P:(t + 1) * P]
                    heads(lambda h: gg[:, t, d * 4 + h:d * 4 + h + 1].to_broadcast([P, P]), lambda h: tri)
                    heads(k, q)
                    heads(lambda h: gb[:, t, d * 4 + h:d * 4 + h + 1].to_broadcast([P, P]), lambda h: ident)
                    heads(k, k)
                for lv in range(LEVELS):
                    for t in range(TT):
                        operand()
                        heads(lambda h: tB[:, t, h, :], lambda h: X[:, t, h, :])
                    for t in range(TT):
                        operand()
                        heads(lambda h: XT[:, t, h, :], lambda h: tU[:, t, h, :])
                        heads(lambda h: tU[:, t, h, :], lambda h: XT[:, t, h, :])
                A, B = (0, 1) if d == 0 else (1, 0)
                operand()
                heads(lambda h: XT[:, A, h, :], lambda h: tB[:, A, h, :])
                operand()
                heads(lambda h: tB[:, B, h, :], lambda h: tU[:, A, h, :])
                heads(lambda h: inT[:, A, h, :], lambda h: tU[:, A, h, :])
                operand()
                heads(lambda h: g_cv[:, 4 + h, B * P:(B + 1) * P], lambda h: X[:, 0, h, :])
                heads(lambda h: g_cv[:, h, B * P:(B + 1) * P], lambda h: X[:, 0, h, :])
                operand()
                heads(lambda h: XT[:, B, h, :], lambda h: tB[:, B, h, :])
                operand()
                heads(lambda h: inT[:, B, h, :], lambda h: tU[:, B, h, :])
            pe.wait_ge(y_ready, 2)
            for t in range(TT):
                heads_b = bank()
                for h in range(GH):
                    last = pe.transpose(heads_b[:, h * P:(h + 1) * P], o_acc[:, t, h, :], ident)
                full(last)
            pe.wait_ge(mix_ready, 1)
            for n in range(2):
                wt = weight_tile()
                for t in range(TT):
                    b = bank()
                    for k in range(KC):
                        last = pe.matmul(b[:, :], mixT[:, k, t * P:(t + 1) * P], wt[:, k, :],
                                         start=(k == 0), stop=(k == KC - 1))
                    full(last)
                used()
            pe.wait_ge(h_ready, 2)
            transposes_to_hT()
            pe.wait_ge(hT_ready, 2)
            pe.wait_ge(in_tail2, 16)
            b = bank()
            token_major(b, 0, 0, tail_w, 0, 36)
            full(token_major(b, 36, 1, tail_w, 0, 36))
            pe.wait_ge(pe_done, j[0])
            pe.sem_inc(tail_used, 1)
            pe.wait_ge(masks_ready, 1)
            b = bank()
            pe.matmul(b[:, 0:36], u_inc, M[:, 0, :], start=True, stop=True)
            pe.matmul(b[:, 36:72], ones, M[:, 0, :], start=True, stop=False)
            pe.matmul(b[:, 36:72], u_inc, M[:, 1, :], start=False, stop=True)
            pe.matmul(b[:, 72:108], ones, M[:, 0, :], start=True, stop=False)
            full(pe.matmul(b[:, 72:108], ones, M[:, 1, :], start=False, stop=True))
            emptied()
            pe.wait_ge(flag_ready, 1)
            many = pe.value_load(flag[0:1, 0:1], min_val=0, max_val=1)
            with pe.If(many == 0):
                done = Count(pe, f_done)

                def fbank():
                    pe.wait_ge(f_free, done.value(1))
                    return ps[(fj[0]) % 8]

                fj = [0]

                def ffull(ins):
                    ins.then_inc(f_done, 1)
                    done.n += 1
                    fj[0] += 1

                def gathered(pair):
                    pe.wait_ge(p_ready, pair + 1)
                    for g in range(2):
                        b = fbank()
                        for c in range(4):
                            k = 4 * g + c
                            for t in range(TT):
                                last = pe.matmul(b[:, c * P:(c + 1) * P], h_tok[:, t, k * P:(k + 1) * P],
                                                 pm[:, t, :], start=(t == 0), stop=(t == TT - 1))
                        ffull(last)

                gathered(0)
                pe.wait_ge(f_free, 8 + 2)
                with pe.Fori(0, N_EXP // 4) as i:
                    done.at(i * 24 + 2)
                    for p in range(2):
                        for r in range(2):
                            b = fbank()
                            for u in range(2):
                                wi = N_HEAD + 6 * p + 2 * r + u
                                pe.wait_ge(landed[wi % RING], i * 32 + 16 * (wi // RING + 1))
                            for k in range(KC):
                                for u in range(2):
                                    last = pe.matmul(b[u * CAP:(u + 1) * CAP, :], xeT[:, k, u * CAP:(u + 1) * CAP],
                                                     slot(N_HEAD + 6 * p + 2 * r + u)[:, k, :],
                                                     start=(k == 0), stop=(k == KC - 1), skip_group_check=True)
                            ffull(last)
                            pe.wait_ge(f_done, done.value())
                            pe.sem_inc(w_used, 2)
                        gathered(i * 2 + (p + 1))
                        pe.wait_ge(f_free, done.value(8 - 2))
                        b = fbank()
                        for c in range(4):
                            last = pe.transpose(b[:, c * P:(c + 1) * P], act_p[:, c * P:(c + 1) * P], ident)
                        ffull(last)
                        b = fbank()
                        for t in range(TT):
                            last = pe.transpose(b[:, t * P:(t + 1) * P], pg[:, p, t, :], ident)
                        ffull(last)
                        pe.wait_ge(f_free, done.value(8 - 1))
                        for n in range(2):
                            b = fbank()
                            for u in range(2):
                                wi = N_HEAD + 6 * p + 4 + u
                                pe.wait_ge(landed[wi % RING], i * 32 + 16 * (wi // RING + 1))
                            for c in range(4):
                                for u in range(2):
                                    last = pe.matmul(b[u * CAP:(u + 1) * CAP, :], actT[:, c, u * CAP:(u + 1) * CAP],
                                                     slot(N_HEAD + 6 * p + 4 + u, 1024)[:, c, n * 512:(n + 1) * 512],
                                                     start=(c == 0), stop=(c == 3), skip_group_check=True)
                            ffull(last)
                        pe.wait_ge(f_done, done.value())
                        pe.sem_inc(w_used, 2)
                        pe.wait_ge(f_free, done.value(8))
                        for t in range(TT):
                            for n in range(2):
                                b = fbank()
                                ffull(pe.matmul(b[:, :], pgT[:, t, :], y_sb[:, n * 512:(n + 1) * 512],
                                                start=True, stop=True))
                pe.wait_ge(f_free, 8 + 2 + 24 * (N_EXP // 4))
            with pe.Else():
                with pe.Fori(0, N_EXP // 2) as i:
                    for u in range(2):
                        for r in range(2):
                            wi = N_HEAD + 2 * r + u
                            pe.wait_ge(landed[wi % RING], i * 16 + 16 * (wi // RING + 1))
                            wt = slot(wi)
                            for c2 in range(2):
                                jb = 8 * u + 2 * r + c2
                                pe.wait_ge(s_free, i * 16 + (jb + 1))
                                b = ps[jb % 8]
                                for c in range(2):
                                    last = feature_major(b, c * T, wt, (2 * c2 + c) * P, P)
                                last.then_inc(s_done, 1)
                        wi = N_HEAD + 4 + u
                        pe.wait_ge(landed[wi % RING], i * 16 + 16 * (wi // RING + 1))
                        wt = slot(wi, 1024)
                        pe.wait_ge(s_free, i * 16 + (8 * u + 4 + 8))
                        for t in range(TT):
                            for n in range(2):
                                jb = 8 * u + 4 + 2 * t + n
                                pe.wait_ge(s_free, i * 16 + (jb + 1))
                                for c in range(4):
                                    last = pe.matmul(ps[jb % 8][:, :], act_d[:, c, t * P:(t + 1) * P],
                                                     wt[:, c, n * 512:(n + 1) * 512], start=(c == 0), stop=(c == 3))
                                last.then_inc(s_done, 1)
                        if u:
                            pe.wait_ge(s_done, i * 16 + (jb + 1))
                            pe.sem_inc(w_used, 6)
                pe.wait_ge(s_free, 8 + 8 * N_EXP)
            w[0] += N_MOE
            pe.wait_ge(h_ready, 3)
            transposes_to_hT()
            pe.wait_ge(hT_ready, 3)
            wt = weight_tile()
            for c in range(4):
                b = bank()
                feature_major(b, 0, wt, c * P, LDK)
                full(feature_major(b, T, wt, c * P + LDK, LDK))
            used()
            pe.wait_ge(in_tail2, 32)
            b = bank()
            full(feature_major(b, 0, tail_w, 0, 16))
            for n in range(2):
                wt = weight_tile()
                for t in range(TT):
                    full(token_major(bank(), 0, t, wt, 0, 512))
                used()
            emptied()
            pe.wait_ge(b2_small, 80)
            for g in range(2):
                b = bank()
                for h in (2 * g, 2 * g + 1):
                    last = pe.matmul(b[0:64, (h % 2) * T:(h % 2 + 1) * T], walpha[0:16, h * LDK:(h + 1) * LDK],
                                     grT[0:16, :], start=True, stop=True)
                full(last)
            for n in range(3):
                wt = weight_tile()
                for t in range(TT):
                    full(token_major(bank(), 0, t, wt, 0, 512))
                used()
            pe.wait_ge(gla_op, 1)
            for t in range(TT):
                b = bank()
                for h in range(LH):
                    last = pe.transpose(b[:, h * LDK:(h + 1) * LDK], gk[0:64, h, t * P:(t + 1) * P], ident[0:64, 0:64])
                full(last)
            for t in range(TT):
                b = bank()
                for h in range(LH):
                    last = pe.matmul(b[:, h * P:(h + 1) * P], kin[0:64, h, t * P:(t + 1) * P],
                                     gq[0:64, h, t * P:(t + 1) * P], start=True, stop=True)
                full(last)
            emptied()
            for c in range(3):
                b = bank()
                r0 = (c % 2) * CH
                for h in range(LH):
                    last = pe.matmul(b[0:64, h * LDV:(h + 1) * LDV], kst[r0:r0 + CH, c // 2, h, :],
                                     gv[r0:r0 + CH, c // 2, h * LDV:(h + 1) * LDV], start=True, stop=True)
                full(last)
            pe.wait_ge(gla_op, 2)
            for t in range(TT):
                b = bank()
                for h in range(LH):
                    out = b[:, h * LDV:(h + 1) * LDV]
                    pe.matmul(out, AT[:, t, h, :], gv[:, t, h * LDV:(h + 1) * LDV], start=True, stop=False)
                    for c in (2 * t, 2 * t + 1):
                        if c:
                            last = pe.matmul(out, qz[0:64, h, c, :], st[c][0:64, h, :], start=False, stop=(c == 2 * t + 1))
                full(last)
            for m in range(2):
                pe.wait_ge(a_rt, m + 1)
                pe.wait_ge(gla_op, 3 + m)
                src = (mq, mk)[m]
                for t in range(TT):
                    for g in range(2):
                        b = bank()
                        for h in range(4):
                            a = (4 * g + h) * AD
                            last = pe.transpose(b[0:64, h * P:(h + 1) * P], src[:, t, a:a + AD], ident)
                        full(last)
            emptied()
            for t in range(TT):
                kw = (t + 1) * P
                for g in range(4):
                    b = bank()
                    for h in (2 * g, 2 * g + 1):
                        last = pe.matmul(b[:, (h % 2) * T:(h % 2) * T + kw], qT[0:64, h, t * P:(t + 1) * P],
                                         kT[0:64, h, 0:kw], start=True, stop=True)
                    full(last)
                pe.wait_ge(a_exp, t + 1)
                for g in range(4):
                    b = bank()
                    for h in (2 * g, 2 * g + 1):
                        for kt in range(t + 1):
                            a = ((h % 2) * 2 + kt) * P
                            last = pe.transpose(b[:, a:a + P], sc[:, h, kt * P:(kt + 1) * P], ident)
                    full(last)
                emptied()
                b = bank()
                for h in range(AH):
                    for kt in range(t + 1):
                        last = pe.matmul(b[:, h * AD:(h + 1) * AD], pT[:, h, kt, :], mv[:, kt, h * AD:(h + 1) * AD],
                                         start=(kt == 0), stop=(kt == t))
                full(last)
            pe.wait_ge(h_ready, 4)
            transposes_to_hT()
            pe.wait_ge(hT_ready, 4)
            for n in range(2):
                wt = weight_tile()
                for t in range(TT):
                    full(token_major(bank(), 0, t, wt, 0, 512))
                used()
            pe.wait_ge(h_ready, 5)
            transposes_to_hT()
            pe.wait_ge(hT_ready, 5)

            def queries():
                wt = weight_tile()
                for c in range(2):
                    b = bank()
                    feature_major(b, 0, wt, c * 256, P)
                    full(feature_major(b, T, wt, c * 256 + P, P))
                used()

            def key_scores(g, behind):
                pe.wait_ge(evac, j[0] - behind)
                for t in range(TT):
                    b = bank()
                    for c in range(4):
                        k = 4 * g + c
                        last = pe.matmul(b[:, c * P:(c + 1) * P], qpT[:, k, t * P:(t + 1) * P], subT[:, k, :],
                                         start=True, stop=True)
                    full(last)

            queries()
            queries()
            pe.wait_ge(in_sub, 16)
            key_scores(0, 2)
            queries()
            key_scores(1, 4)
            queries()
            key_scores(2, 4)
            key_scores(3, 2)
            pe.wait_ge(pe_done, j[0])
            pe.sem_inc(v_free, V_RING)
            emptied()
            pe.wait_ge(zeros_ready, 1)
            for n in range(2 * TT):
                pe.matmul(ps[n][:, :], zeros, h_tok[:, 0, 0:512], start=True, stop=False, skip_group_check=True)
            for n2 in range(NG):
                with pe.Fori(0, 2) as q:
                    for t in range(TT):
                        step = q * TT + (2 * TT * n2 + t)
                        for k in range(16):
                            pe.wait_ge(diag_ready, step * 16 + (k + 1))
                            pe.wait_ge(v_landed[k], step * 16 + 16)
                            for n in range(2):
                                last = pe.matmul(ps[2 * t + n][:, :], diag[:, k % 4, :],
                                                 v_ring(k)[:, n * 512:(n + 1) * 512],
                                                 start=False, stop=False, skip_group_check=True)
                            last.then_inc(v_free, 1)
            for n in range(2 * TT):
                last = pe.matmul(ps[n][:, :], zeros, h_tok[:, 0, 0:512], start=False, stop=True, skip_group_check=True)
            last.then_inc(p_done, 1)

        @block.gpsimd
        def _(pool):
            pool.wait_ge(nw_used, 1)
            pool.dma_start(nw[:, :], io["norm_ffn_w"].to_broadcast([P, D])).then_inc(in_nw2, 16)
            pool.wait_ge(tail_used, 1)
            pool.dma_start(tail_w[:, :, :], io["router_w"].rearrange("(k p) n -> p k n", p=P)).then_inc(in_tail2, 16)
            pool.wait_ge(x1_ready, 1)
            pool.dma_start(rb, io["router_b"].to_broadcast([P, 36])).then_inc(in_route, 16)
            pool.wait_ge(nw_used, 2)
            pool.dma_start(nw[:, :], io["final_norm_w"].to_broadcast([P, D])).then_inc(in_nw2, 16)
            pool.wait_ge(tail_used, 2)
            pool.dma_start(tail_w[:, :, 0:16], w_in2_v[:, :, 1536:1552]).then_inc(in_tail2, 16)
            pool.wait_ge(moe_done, 1)
            pool.dma_start(walpha[0:16, :], io["gla_w_alpha"]).then_inc(b2_small, 16)
            pool.dma_start(conv_g[0:64, 0:4], io["gla_b_alpha"]).then_inc(b2_small, 16)
            pool.dma_start(small[:, 320:448], io["gla_out_norm_w"].to_broadcast([P, P])).then_inc(b2_small, 16)
            pool.dma_start(small[:, 448:512], io["moba_q_norm_w"].to_broadcast([P, AD])).then_inc(b2_small, 16)
            pool.dma_start(mod[:, 0, 0:AD], io["moba_k_norm_w"].to_broadcast([P, AD])).then_inc(b2_small, 16)
            pool.wait_ge(nw_used, 3)
            pool.dma_start(nw[:, :], io["norm1_w_2"].to_broadcast([P, D])).then_inc(in_nw2, 16)
            pool.wait_ge(nw_used, 4)
            pool.dma_start(nw[:, :], io["mix_scale"].to_broadcast([P, D])).then_inc(in_nw2, 16)
            pool.wait_ge(nw_used, 5)
            pool.dma_start(nw[:, :], io["norm2_w"].to_broadcast([P, D])).then_inc(in_nw2, 16)
            pool.wait_ge(x3_ready, 1)
            pool.dma_start(subT, io["subkeys"]).then_inc(in_sub, 16)
            for n2 in range(NG):
                pool.wait_ge(idx_ready, n2 + 1)
                with pool.Fori(0, 2) as q:
                    for t in range(TT):
                        step = q * TT + (2 * TT * n2 + t)
                        pool.tensor_copy(idx_cur[:, t, :], idx_all[:, n2 % 2, t, bass.ds(q * 16, 16)])\
                            .then_inc(idx_copied, 1)
                        pool.wait_ge(idx_copied, step + 1)
                        for k in range(16):
                            pool.wait_ge(u_free, step * 16 + (k + 1))
                            pool.sem_inc(gathers, 1)
                            pool.indirect_dma_start(
                                out=u_ring(k), out_offset=None, in_=io["peer_u"],
                                in_offset=bass.IndirectOffsetOnAxis(ap=idx_cur[:, t, k:k + 1], axis=0),
                            ).then_inc(u_landed[k % U_RING], 16)
                        for k in range(16):
                            pool.wait_ge(v_free, step * 16 + (k + 1))
                            pool.sem_inc(gathers, 1)
                            pool.indirect_dma_start(
                                out=v_ring(k), out_offset=None, in_=io["peer_v"],
                                in_offset=bass.IndirectOffsetOnAxis(ap=idx_cur[:, t, k:k + 1], axis=0),
                            ).then_inc(v_landed[k], 16)

        @block.vector
        def _(dve):
            n = [0]
            j = [0]
            norms = [0]

            def o(ins):
                n[0] += 1
                ins.then_inc(dve_n, 1)

            def sync():
                if n[0]:
                    dve.wait_ge(dve_n, n[0])

            def post(s):
                sync()
                dve.sem_inc(s, 1)

            def job():
                dve.wait_ge(pe_done, j[0] + 1)
                return ps[j[0] % 8]

            def empty(*_):
                sync()
                j[0] += 1
                dve.sem_inc(evac, 1)

            def bc(ap, shape):
                return ap.to_broadcast(shape)

            def rms_scale():
                for t in range(TT):
                    o(dve.tensor_tensor_reduce(out=h_tok[:, t, :], in0=x[:, t, :], in1=x[:, t, :], scale=1.0 / D,
                                               scalar=0.0, op0=ALU.mult, op1=ALU.add, accum_out=ms[:, t:t + 1]))
                sync()
                o(dve.tensor_scalar(ms[:, 0:TT], ms[:, 0:TT], EPS, None, ALU.add))
                post(ms_ready)
                norms[0] += 1
                dve.wait_ge(rt_ready, norms[0])
                o(dve.reciprocal(rstd[:, 0:TT], rstd[:, 0:TT]))
                sync()

            def to_hT():
                for t in range(TT):
                    for g in range(2):
                        b = job()
                        o(dve.tensor_copy(hT[:, 4 * g:4 * g + 4, t * P:(t + 1) * P],
                                          b[:, :].rearrange("p (c n) -> p c n", c=4)))
                        empty()
                post(hT_ready)

            def norm_mod(scale, shift):
                for t in range(TT):
                    o(dve.scalar_tensor_tensor(h_tok[:, t, :], x[:, t, :], rstd[:, t:t + 1], scale,
                                               ALU.mult, ALU.mult))
                sync()
                for t in range(TT):
                    o(dve.tensor_tensor(h_tok[:, t, :], h_tok[:, t, :], shift, ALU.add))
                post(h_ready)

            dve.wait_ge(in_bias0, 32)
            dve.wait_ge(in_start, 48)
            dve.wait_ge(cond_act, 1)
            o(dve.tensor_copy(cond_b, bc(g_e.unsqueeze(2), [P, KC, P])))
            post(cond_ready)
            for i in range(8):
                b = job()
                o(dve.tensor_copy(bias_rows[0:60, i * 512:(i + 1) * 512], b[0:60, :]))
                empty()
            post(bias_ready)
            dve.wait_ge(in_ada, 16)
            dve.wait_ge(bias_out, 16)
            for i in range(N_MOD):
                b = job()
                dst = ab1[:, i // 2, (i % 2) * 512:(i % 2 + 1) * 512] if i < 4 else \
                    mod[:, i // 2 - 2, (i % 2) * 512:(i % 2 + 1) * 512]
                o(dve.tensor_tensor(dst, b[:, :], b_ada[:, i * 512:(i + 1) * 512], ALU.add))
                empty()
            dve.wait_ge(in_nw, 16)
            o(dve.scalar_tensor_tensor(ab1[:, 1, :], ab1[:, 1, :], 1.0, nw[:, :], ALU.add, ALU.mult))
            post(nw_used)
            dve.sem_inc(mod_ready, 1)
            rms_scale()
            norm_mod(ab1[:, 1, :], ab1[:, 0, :])
            to_hT()
            dve.wait_ge(in_nw2, 16)
            o(dve.scalar_tensor_tensor(mod[:, 2, :], mod[:, 2, :], 1.0, nw[:, :], ALU.add, ALU.mult))

            for c in range(3):
                b = job()
                o(dve.tensor_copy(c3[:, 2 * c:2 * c + 2, :], b[:, :].rearrange("p (a b) -> p a b", a=2)))
                empty()
            for dst in (na_q, na_k):
                for c in range(2):
                    b = job()
                    o(dve.tensor_copy(dst[0:64, 2 * c:2 * c + 2, :], b[0:64, :].rearrange("p (a b) -> p a b", a=2)))
                    empty()
            b = job()
            o(dve.tensor_copy(na_v, b[:, :].rearrange("p (a b) -> p a b", a=2)))
            empty()
            b = job()
            o(dve.tensor_copy(gab, b[:, 0:32].rearrange("p (a b) -> p a b", a=2)))
            empty()
            dve.wait_ge(in_small, 80)
            t3 = lambda ap: ap.rearrange("p (t c) -> p t c", t=TT)
            o(dve.tensor_tensor(t3(g_t), gab[:, :, 0:8], bc(dt_b.unsqueeze(1), [P, TT, 8]), ALU.add))
            post(gab_in)
            for c in range(6):
                b = job()
                o(dve.tensor_copy(g_raw[:, 2 * c:2 * c + 2, :], b[:, :].rearrange("p (a b) -> p a b", a=2)))
                empty()
            for t in range(TT):
                b = job()
                o(dve.tensor_copy(z[:, t, :], b[:, :]))
                empty()

            def conv(dst, src, taps, m):
                for c in range(m):
                    o(dve.tensor_scalar(dst(c), src(c), taps(c, 1), None, ALU.mult))
                sync()
                for c in range(m):
                    o(dve.scalar_tensor_tensor(dst(c)[:, 1:T], src(c)[:, 0:T - 1], taps(c, 0), dst(c)[:, 1:T],
                                               ALU.mult, ALU.add))
                sync()
                for c in range(m):
                    o(dve.scalar_tensor_tensor(dst(c)[:, 0:T - 1], src(c)[:, 1:T], taps(c, 2), dst(c)[:, 0:T - 1],
                                               ALU.mult, ALU.add))
                sync()

            conv(lambda c: g_cv[:, c, :], lambda c: g_raw[:, c, :],
                 lambda c, i: conv_g[:, 3 * c + i:3 * c + i + 1], 12)
            post(conv_ready)
            o(dve.tensor_tensor(c3[:, 2:4, :], c3[:, 2:4, :], c3[:, 4:6, :], ALU.mult))
            sync()
            conv(lambda c: c3[:, 4 + c, :], lambda c: c3[:, 2 + c, :],
                 lambda c, i: conv_a[:, 3 * c + i:3 * c + i + 1], 2)
            o(dve.tensor_tensor(mixT[:, 0:2, :], c3[:, 4:6, :], c3[:, 0:2, :], ALU.mult))
            dve.wait_ge(gab_act, 1)
            o(dve.scalar_tensor_tensor(g_t2, g_t, 0.0, g_t2, ALU.max, ALU.add))
            sync()
            o(dve.scalar_tensor_tensor(t3(g_g), t3(g_t2), -1.0, bc(g_e.unsqueeze(1), [P, TT, 8]),
                                       ALU.mult, ALU.mult))
            post(g_ready)
            dve.wait_ge(bias_in, 16 * N_ROWS * NA_H)
            for t in range(TT):
                for g in range(2):
                    b = job()
                    o(dve.scalar_tensor_tensor(na_p[:, 2 * g:2 * g + 2, :], b[:, :].rearrange("p (a b) -> p a b", a=2),
                                               NA_DH ** -0.5, na_bias[:, t, 2 * g:2 * g + 2, :], ALU.mult, ALU.add))
                    empty()
                o(dve.tensor_reduce(na_m[:, 0:4], na_p[:, :, :], AX.X, ALU.max))
                sync()
                o(dve.tensor_scalar(na_nm[:, 0:4], na_m[:, 0:4], -1.0, None, ALU.mult))
                post(na_sc)
                dve.wait_ge(na_exp, t + 1)
                o(dve.reciprocal(na_r[:, 0:4], na_s[:, 0:4]))
                for g in range(2):
                    b = job()
                    o(dve.tensor_copy(na_pT[:, 2 * g:2 * g + 2, :, :].rearrange("p a b c -> p (a b c)"), b[:, :]))
                    empty()
                b = job()
                o(dve.tensor_tensor(na_o, b[:, 0:256].rearrange("p (a b) -> p a b", a=4),
                                    bc(na_r[:, 0:4].unsqueeze(2), [P, 4, NA_DH]), ALU.mult))
                empty()
                b = job()
                o(dve.tensor_copy(mixT[:, 2:4, t * P:(t + 1) * P], b[:, 0:256].rearrange("p (a b) -> p a b", a=2)))
                empty()
            post(na_out)
            for c in range(4):
                b = job()
                o(dve.tensor_scalar(rn[:, 2 * c:2 * c + 2, :], b[:, :].rearrange("p (a b) -> p a b", a=2),
                                    EPS, None, ALU.add))
                empty()
                dve.sem_inc(l2_in, 1)
            for c in range(4):
                dve.wait_ge(l2_rt, c + 1)
                o(dve.reciprocal(rn[:, 2 * c:2 * c + 2, :], rn[:, 2 * c:2 * c + 2, :]))
            sync()
            o(dve.scalar_tensor_tensor(g_cv[:, 0:4, :], g_cv[:, 0:4, :], GD ** -0.5, rn[:, 0:4, :], ALU.mult, ALU.mult))
            o(dve.tensor_tensor(g_cv[:, 4:8, :], g_cv[:, 4:8, :], rn[:, 4:8, :], ALU.mult))
            b = job()
            o(dve.tensor_copy(g_c, b[:, 0:16]))
            o(dve.tensor_scalar(g_nc, b[:, 0:16], -1.0, None, ALU.mult))
            o(dve.tensor_copy(g_tot, b[:, 16:32]))
            empty()
            o(dve.tensor_tensor(g_kd, g_tot, g_nc, ALU.add))
            post(qk_ready)
            for dst in (k_tok, v_tok):
                for t in range(TT):
                    b = job()
                    o(dve.tensor_copy(dst[:, t, :, :].rearrange("p a b -> p (a b)"), b[:, :]))
                    empty()
            dve.wait_ge(gab_act, 2)
            b4 = lambda b: b[:, :].rearrange("p (a b) -> p a b", a=4)
            tok = lambda ap, t, d: bc(ap[:, t * 8 + d * 4:t * 8 + d * 4 + 4].unsqueeze(2), [P, 4, P])
            m = 0
            for d in range(2):
                neg = consts[:, (C_NEGF if d == 0 else C_NEGB):(C_NEGF if d == 0 else C_NEGB) + P]
                for t in range(TT):
                    b = job()
                    o(dve.tensor_tensor(tD, b4(b), bc(neg.unsqueeze(1), [P, 4, P]), ALU.add))
                    empty()
                    dve.sem_inc(d_in, 1)
                    m += 1
                    dve.wait_ge(d_out, m)
                    b = job()
                    o(dve.tensor_tensor(inT[:, t, :, :], b4(b), tD, ALU.mult))
                    empty()
                    b = job()
                    o(dve.tensor_tensor(tD, b4(b), tD, ALU.mult))
                    empty()
                    b = job()
                    o(dve.tensor_tensor(LT[:, t, :, :], b4(b), tD, ALU.mult))
                    empty()
                    o(dve.tensor_copy(X[:, t, :, :], bc(ident.unsqueeze(1), [P, 4, P])))
                    o(dve.tensor_copy(XT[:, t, :, :], bc(ident.unsqueeze(1), [P, 4, P])))
                for lv in range(LEVELS):
                    a = C_LVL + (d * LEVELS + lv) * P
                    for t in range(TT):
                        o(dve.tensor_tensor(tB[:, t, :, :], LT[:, t, :, :],
                                            bc(consts[:, a:a + P].unsqueeze(1), [P, 4, P]), ALU.mult))
                        post(gd_op)
                    for t in range(TT):
                        b = job()
                        o(dve.tensor_copy(tU[:, t, :, :], b4(b)))
                        empty()
                        dve.sem_inc(gd_op, 1)
                    for t in range(TT):
                        for dst in (X, XT):
                            b = job()
                            o(dve.tensor_tensor(dst[:, t, :, :], dst[:, t, :, :], b4(b), ALU.subtract))
                            empty()
                A, B = (0, 1) if d == 0 else (1, 0)
                o(dve.tensor_tensor(tB[:, A, :, :], v_tok[:, A, :, :], tok(g_be, A, d), ALU.mult))
                post(gd_op)
                o(dve.tensor_tensor(tB[:, B, :, :], k_tok[:, A, :, :], tok(g_kd, A, d), ALU.mult))
                b = job()
                o(dve.tensor_copy(tU[:, A, :, :], b4(b)))
                empty()
                dve.sem_inc(gd_op, 1)
                b = job()
                o(dve.tensor_copy(X[:, 0, :, :], b4(b)))
                empty()
                dve.sem_inc(gd_op, 1)

                def out_add(dst, b):
                    if d == 0:
                        o(dve.tensor_copy(dst, b4(b)))
                    else:
                        o(dve.tensor_tensor(dst, dst, b4(b), ALU.add))

                b = job()
                out_add(o_acc[:, A, :, :], b)
                empty()
                b = job()
                o(dve.tensor_tensor(tD, b4(b), tok(g_eg, B, d), ALU.mult))
                empty()
                o(dve.tensor_tensor(tD, v_tok[:, B, :, :], tD, ALU.subtract))
                sync()
                o(dve.tensor_tensor(tB[:, B, :, :], tD, tok(g_be, B, d), ALU.mult))
                post(gd_op)
                b = job()
                o(dve.tensor_tensor(tD, b4(b), tok(g_eg, B, d), ALU.mult))
                empty()
                if d == 0:
                    o(dve.tensor_copy(o_acc[:, B, :, :], tD))
                else:
                    o(dve.tensor_tensor(o_acc[:, B, :, :], o_acc[:, B, :, :], tD, ALU.add))
                b = job()
                o(dve.tensor_copy(tU[:, B, :, :], b4(b)))
                empty()
                dve.sem_inc(gd_op, 1)
                b = job()
                o(dve.tensor_tensor(o_acc[:, B, :, :], o_acc[:, B, :, :], b4(b), ALU.add))
                empty()
            o(dve.tensor_tensor(X, o_acc, o_acc, ALU.mult))
            sync()
            o(dve.tensor_reduce(ms[:, 0:8], X.rearrange("p a b c -> p (a b) c"), AX.X, ALU.add))
            sync()
            o(dve.tensor_scalar(ms[:, 0:8], ms[:, 0:8], 1.0 / GD, EPS, ALU.mult, ALU.add))
            post(y_ready)
            norms[0] += 1
            dve.wait_ge(rt_ready, norms[0])
            o(dve.reciprocal(rstd[:, 0:8], rstd[:, 0:8]))
            sync()
            oa = o_acc.rearrange("p a b c -> p (a b) c")
            o(dve.tensor_tensor(oa, oa, bc(rstd[:, 0:8].unsqueeze(2), [P, 8, P]), ALU.mult))
            sync()
            o(dve.tensor_tensor(oa, oa, bc(gn_w[:, :].unsqueeze(1), [P, 8, P]), ALU.mult))
            sync()
            o(dve.tensor_tensor(oa, oa, z.rearrange("p t (h c) -> p (t h) c", h=4), ALU.mult))
            post(y_ready)
            for t in range(TT):
                b = job()
                o(dve.tensor_copy(mixT[:, 4:8, t * P:(t + 1) * P], b4(b)))
                empty()
            post(mix_ready)
            for nn in range(2):
                for t in range(TT):
                    b = job()
                    o(dve.tensor_tensor(g_raw[:, 0:2, :].rearrange("p a b -> p (a b)"), b[:, :],
                                        mod[:, 0, nn * 512:(nn + 1) * 512], ALU.mult))
                    empty()
                    o(dve.tensor_tensor(x[:, t, nn * 512:(nn + 1) * 512], x[:, t, nn * 512:(nn + 1) * 512],
                                        g_raw[:, 0:2, :].rearrange("p a b -> p (a b)"), ALU.add))
                    sync()
            post(x1_ready)
            rms_scale()
            norm_mod(mod[:, 2, :], mod[:, 1, :])
            dve.sem_inc(nw_used, 1)
            to_hT()
            dve.wait_ge(in_route, 16)
            b = job()
            o(dve.tensor_tensor(lg, b[:, 0:72].rearrange("p (t n) -> p t n", t=TT), bc(rb.unsqueeze(1), [P, TT, 36]),
                                ALU.add))
            empty()
            o(dve.tensor_reduce(gmx, lg[:, :, 0:4], AX.X, ALU.max))
            o(dve.memset(acc, 0.0))
            o(dve.memset(G, 0.0))
            o(dve.memset(M, 0.0))
            sync()
            gm4 = bc(gmx.unsqueeze(2), [P, TT, N_GRP])
            o(dve.tensor_tensor(oh4, lg[:, :, 0:4], gm4, ALU.is_equal))
            o(dve.tensor_tensor(e4, lg[:, :, 0:4], gm4, ALU.subtract))
            post(rt_logits)
            o(dve.tensor_tensor(oh4, oh4, bc(consts[:, C_DN4:C_DN4 + N_GRP].unsqueeze(1), [P, TT, N_GRP]), ALU.mult))
            sync()
            o(dve.tensor_reduce(gmx, oh4, AX.X, ALU.max))
            sync()
            o(dve.tensor_tensor(oh4, oh4, gm4, ALU.is_equal))
            sync()
            o(dve.tensor_scalar(pen, oh4, -NEG, NEG, ALU.mult, ALU.add))
            dve.wait_ge(rt_exp, 1)
            o(dve.tensor_reduce(pgt, e4, AX.X, ALU.add))
            sync()
            o(dve.reciprocal(pgt, pgt))
            for t in range(TT):
                o(dve.tensor_tensor(elm[:, t, :].rearrange("p (g e) -> p g e", g=N_GRP),
                                    lg[:, t, 4:36].rearrange("p (g e) -> p g e", g=N_GRP),
                                    bc(pen[:, t, :].unsqueeze(2), [P, N_GRP, EPG]), ALU.add))
            sync()
            for t in range(TT):
                o(dve.max(v8[:, t, :], elm[:, t, :]))
            sync()
            for t in range(TT):
                o(dve.max_index(i8[:, t, :], v8[:, t, :], elm[:, t, :]))
            o(dve.tensor_tensor(gt[:, :, 0:1], v8[:, :, 1:2], v8[:, :, 0:1], ALU.subtract))
            post(rt_logits)
            o(dve.tensor_copy(i8f, i8))
            dve.wait_ge(rt_exp, 2)
            o(dve.tensor_scalar(gt[:, :, 1:2], gt[:, :, 0:1], 1.0, None, ALU.add))
            sync()
            o(dve.reciprocal(gt[:, :, 1:2], gt[:, :, 1:2]))
            sync()
            o(dve.tensor_tensor(gt[:, :, 2:3], gt[:, :, 1:2], pgt.unsqueeze(2), ALU.mult))
            sync()
            o(dve.tensor_tensor(gt[:, :, 3:4], gt[:, :, 2:3], gt[:, :, 0:1], ALU.mult))
            io32 = consts[:, C_IOTA:C_IOTA + N_EXP]
            for t in range(TT):
                o(dve.tensor_scalar(M[:, t, 0:N_EXP], io32, i8f[:, t, 0:1], None, ALU.is_equal))
                o(dve.tensor_scalar(rk[:, t, 0:N_EXP], io32, i8f[:, t, 1:2], None, ALU.is_equal))
            sync()
            for t in range(TT):
                o(dve.tensor_scalar(G[:, t, 0:N_EXP], rk[:, t, 0:N_EXP], gt[:, t, 3:4], None, ALU.mult))
            sync()
            for t in range(TT):
                o(dve.scalar_tensor_tensor(G[:, t, 0:N_EXP], M[:, t, 0:N_EXP], gt[:, t, 2:3], G[:, t, 0:N_EXP],
                                           ALU.mult, ALU.add))
            sync()
            o(dve.tensor_tensor(M[:, :, 0:N_EXP], M[:, :, 0:N_EXP], rk[:, :, 0:N_EXP], ALU.add))
            post(masks_ready)
            b = job()
            o(dve.tensor_tensor(rk, b[:, 0:72].rearrange("p (t n) -> p t n", t=TT), M, ALU.mult))
            o(dve.tensor_reduce(cnt[:, 0:1], b[:, 72:104], AX.X, ALU.max))
            empty()
            o(dve.tensor_scalar(rk, rk, -1.0, None, ALU.add))
            o(dve.tensor_scalar(flag[:, 0:1], cnt[:, 0:1], float(CAP) + 0.5, None, ALU.is_gt))
            post(flag_ready)
            many = dve.value_load(flag[0:1, 0:1], min_val=0, max_val=1)
            with dve.If(many == 0):
                own = Count(dve, f_dve)
                fj = [0]
                io64 = consts[:, C_IOTA:C_IOTA + CAP]

                def f(ins):
                    ins.then_inc(f_dve, 1)
                    own.n += 1

                done = Count(dve, f_done)

                def fjob():
                    done.n += 1
                    done.wait()
                    fj[0] += 1
                    return ps[(fj[0] - 1) % 8]

                def fempty():
                    own.wait()
                    dve.sem_inc(f_free, 1)

                def selection(c, q):
                    for t in range(TT):
                        for u in range(2):
                            f(dve.tensor_scalar(pm[:, t, u * CAP:(u + 1) * CAP], io64, rk4[:, t, c + u:c + u + 1], None,
                                                ALU.is_equal))
                            f(dve.tensor_scalar(pg[:, q, t, u * CAP:(u + 1) * CAP], io64, rk4[:, t, c + u:c + u + 1],
                                                g4[:, t, c + u:c + u + 1], ALU.is_equal, ALU.mult))
                    own.wait()
                    dve.sem_inc(p_ready, 1)

                def rows_in():
                    for g in range(2):
                        b = fjob()
                        f(dve.tensor_copy(xeT[:, 4 * g:4 * g + 4, :], b[:, :].rearrange("p (c n) -> p c n", c=4)))
                        fempty()

                dve.sem_inc(f_free, 8)
                f(dve.tensor_copy(rk4[:, :, 0:2], rk[:, :, 0:2]))
                f(dve.tensor_copy(g4[:, :, 0:2], G[:, :, 0:2]))
                own.wait()
                selection(0, 0)
                rows_in()
                per, first = F_OPS, own.n
                with dve.Fori(0, N_EXP // 4) as i:
                    own.at(i * per + first)
                    done.at(i * 24 + 2)
                    own.wait()
                    f(dve.tensor_copy(rk4[:, :, :], rk[:, :, bass.ds(i * 4 + 2, 4)]))
                    f(dve.tensor_copy(g4[:, :, :], G[:, :, bass.ds(i * 4 + 2, 4)]))
                    own.wait()
                    for p in range(2):
                        selection(2 * p, 1 - p)
                        b = fjob()
                        dve.wait_ge(f_act, i * 2 + (p + 1))
                        dve.sem_inc(f_free, 1)
                        b = fjob()
                        f(dve.tensor_tensor(act_p, sil, b[:, :], ALU.mult))
                        fempty()
                        rows_in()
                        b = fjob()
                        f(dve.tensor_copy(actT.rearrange("p a b -> p (a b)"), b[:, :]))
                        fempty()
                        b = fjob()
                        f(dve.tensor_copy(pgT.rearrange("p a b -> p (a b)"), b[:, 0:TT * P]))
                        fempty()
                        for n2 in range(2):
                            b = fjob()
                            f(dve.tensor_copy(y_sb[:, n2 * 512:(n2 + 1) * 512], b[:, :]))
                            fempty()
                        for t in range(TT):
                            for n2 in range(2):
                                b = fjob()
                                a = acc[:, t, n2 * 512:(n2 + 1) * 512]
                                f(dve.tensor_tensor(a, a, b[:, :], ALU.add))
                                fempty()
                    assert own.n == per, own.n
                    assert done.n == 24
                dve.wait_ge(f_dve, per * (N_EXP // 4) + first)
            with dve.Else():
                dve.sem_inc(s_free, 8)
                own = Count(dve, s_dve)

                def f(ins):
                    ins.then_inc(s_dve, 1)
                    own.n += 1

                per = S_OPS
                with dve.Fori(0, N_EXP // 2) as i:
                    own.at(i * per)
                    f(dve.tensor_copy(g4[:, :, 0:2], G[:, :, bass.ds(i * 2, 2)]))
                    for u in range(2):
                        for c in range(2):
                            dve.wait_ge(s_act, i * 4 + (2 * u + c + 1))
                            dve.sem_inc(s_free, 1)
                        for c in range(2):
                            dve.wait_ge(s_done, i * 16 + (8 * u + 2 + c + 1))
                            f(dve.tensor_tensor(act_d[:, 2 * c:2 * c + 2, :], sil_d[:, 2 * c:2 * c + 2, :],
                                                ps[2 + c][:, :].rearrange("p (a b) -> p a b", a=2), ALU.mult))
                            own.wait()
                            dve.sem_inc(s_free, 1)
                        for t in range(TT):
                            for n2 in range(2):
                                jb = 8 * u + 4 + 2 * t + n2
                                dve.wait_ge(s_done, i * 16 + (jb + 1))
                                a = acc[:, t, n2 * 512:(n2 + 1) * 512]
                                f(dve.scalar_tensor_tensor(a, ps[jb % 8][:, :], g4[:, t, u:u + 1], a,
                                                           ALU.mult, ALU.add))
                                own.wait()
                                dve.sem_inc(s_free, 1)
                    assert own.n == per, own.n
            for t in range(TT):
                o(dve.tensor_tensor(acc[:, t, :], acc[:, t, :], mod[:, 3, :], ALU.mult))
            sync()
            for t in range(TT):
                o(dve.tensor_tensor(x[:, t, :], x[:, t, :], acc[:, t, :], ALU.add))
            sync()
            dve.sem_inc(moe_done, 1)
            rms_scale()
            dve.wait_ge(in_nw2, 32)
            for t in range(TT):
                o(dve.scalar_tensor_tensor(x[:, t, :], x[:, t, :], rstd[:, t:t + 1], nw[:, :], ALU.mult, ALU.mult))
            post(nw_used)

            def norm_weight(m):
                rms_scale()
                dve.wait_ge(in_nw2, m)
                for t in range(TT):
                    o(dve.scalar_tensor_tensor(h_tok[:, t, :], x[:, t, :], rstd[:, t:t + 1], nw[:, :],
                                               ALU.mult, ALU.mult))
                post(h_ready)
                dve.sem_inc(nw_used, 1)
                to_hT()

            norm_weight(48)
            two = lambda b: b[:, :].rearrange("p (a b) -> p a b", a=2)
            for dst in (gq, gk):
                for c in range(2):
                    b = job()
                    o(dve.tensor_copy(dst[0:64, 2 * c:2 * c + 2, :], two(b)[0:64]))
                    empty()
            b = job()
            o(dve.tensor_copy(grT[0:16, :], b[0:16, 0:T]))
            empty()
            for dst in (gv, ggate):
                for t in range(TT):
                    b = job()
                    o(dve.tensor_copy(dst[:, t, :], b[:, :]))
                    empty()
            dve.wait_ge(b2_small, 80)
            for g in range(2):
                b = job()
                for h in (2 * g, 2 * g + 1):
                    o(dve.tensor_scalar(gb_[0:64, h, :], b[0:64, (h % 2) * T:(h % 2 + 1) * T], conv_g[0:64, h:h + 1], None,
                                        ALU.add))
                empty()
            o(dve.tensor_scalar(ge[0:64], gb_[0:64], -1.0, None, ALU.mult))
            sync()
            o(dve.tensor_tensor(ge[0:64], ge[0:64], gb_[0:64], ALU.max))
            post(z_in)
            for dst in (mq, mk, mv):
                for t in range(TT):
                    b = job()
                    o(dve.tensor_copy(dst[:, t, :], b[:, :]))
                    empty()
            dve.wait_ge(z_act, 2)
            o(dve.scalar_tensor_tensor(gb_[0:64], gb_[0:64], 0.0, ge[0:64], ALU.min, ALU.subtract))
            sync()
            o(dve.tensor_scalar(ge[0:64], gb_[0:64], 1.0 / 16.0, None, ALU.mult))
            sync()
            for h in range(LH):
                for c in range(4):
                    o(dve.tensor_tensor_scan(gb_[0:64, h, c * CH:(c + 1) * CH], ones[0:64, 0:CH],
                                             ge[0:64, h, c * CH:(c + 1) * CH], 0.0, ALU.mult, ALU.add))
            post(b_in)
            dve.wait_ge(b_act, 1)
            o(dve.scalar_tensor_tensor(gq[0:64], gq[0:64], LDK ** -0.5, ge[0:64], ALU.mult, ALU.mult))
            o(dve.tensor_copy(g_t.rearrange("p (h c) -> p h c", h=LH)[0:64],
                              ge[0:64].rearrange("p h (c n) -> p h c n", c=4)[:, :, :, CH - 1]))
            o(dve.memset(qz[0:64], 0.0))
            post(b_in)
            for h in range(LH):
                for c in range(4):
                    o(dve.tensor_copy(qz[0:64, h, c, (c % 2) * CH:(c % 2 + 1) * CH], gq[0:64, h, c * CH:(c + 1) * CH]))
            dve.wait_ge(b_act, 2)
            o(dve.tensor_tensor(kin[0:64], gk[0:64], ge[0:64], ALU.mult))
            sync()
            for h in range(LH):
                b4c = gb_[0:64, h, :].rearrange("p (c n) -> p c n", c=4)
                o(dve.tensor_tensor(ge[0:64, h, :].rearrange("p (c n) -> p c n", c=4),
                                    bc(b4c[:, :, CH - 1:CH], [64, 4, CH]), b4c, ALU.subtract))
            post(b_in)
            dve.wait_ge(b_act, 3)
            o(dve.tensor_tensor(gk[0:64], gk[0:64], ge[0:64], ALU.mult))
            post(gla_op)
            for t in range(TT):
                b = job()
                o(dve.tensor_copy(kst[:, t, :, :].rearrange("p a b -> p (a b)"), b[:, 0:256]))
                empty()
            for t in range(TT):
                b = job()
                o(dve.tensor_tensor(AT[:, t, :, :], b4(b), bc(consts[:, C_BLK:C_BLK + P].unsqueeze(1), [P, 4, P]),
                                    ALU.mult))
                empty()
            dec = g_t.rearrange("p (h c) -> p h c", h=LH)
            for c in range(3):
                b = job()
                if c == 0:
                    o(dve.tensor_copy(st[1][0:64], b4(b)[0:64]))
                else:
                    o(dve.tensor_tensor(st[c + 1][0:64], st[c][0:64], bc(dec[0:64, :, c:c + 1], [64, LH, LDV]), ALU.mult))
                    sync()
                    o(dve.tensor_tensor(st[c + 1][0:64], st[c + 1][0:64], b4(b)[0:64], ALU.add))
                empty()
            post(gla_op)
            for t in range(TT):
                b = job()
                o(dve.tensor_copy(y2[:, t, 0:512], b[:, :]))
                empty()
            for t in range(TT):
                o(dve.tensor_tensor(rt[:, t * 512:(t + 1) * 512], y2[:, t, 0:512], y2[:, t, 0:512], ALU.mult))
            sync()
            o(dve.tensor_reduce(ms[:, 0:8], rt.rearrange("p (a b) -> p a b", a=8), AX.X, ALU.add))
            sync()
            o(dve.tensor_scalar(ms[:, 0:8], ms[:, 0:8], 1.0 / LDV, EPS, ALU.mult, ALU.add))
            post(o_in)
            norms[0] += 1
            dve.wait_ge(rt_ready, norms[0])
            o(dve.reciprocal(rstd[:, 0:8], rstd[:, 0:8]))
            sync()
            hd = lambda ap: ap.rearrange("p (h c) -> p h c", h=4)
            for t in range(TT):
                o(dve.tensor_tensor(hd(y2[:, t, 0:512]), hd(y2[:, t, 0:512]),
                                    bc(rstd[:, 4 * t:4 * t + 4].unsqueeze(2), [P, 4, P]), ALU.mult))
            sync()
            for t in range(TT):
                o(dve.tensor_tensor(hd(y2[:, t, 0:512]), hd(y2[:, t, 0:512]),
                                    bc(small[:, 320:448].unsqueeze(1), [P, 4, P]), ALU.mult))
            sync()
            dve.wait_ge(b_act, 4)
            for t in range(TT):
                o(dve.tensor_tensor(y2[:, t, 0:512], y2[:, t, 0:512], ggate[:, t, :], ALU.mult))
            sync()
            h8 = lambda ap: ap.rearrange("p (h c) -> p h c", h=AH)
            for m, (src, wn) in enumerate(((mq, small[:, 448:512]), (mk, mod[:, 0, 0:AD]))):
                for t in range(TT):
                    o(dve.tensor_tensor(rt[:, t * 512:(t + 1) * 512], src[:, t, :], src[:, t, :], ALU.mult))
                sync()
                o(dve.tensor_reduce(g_t2, rt.rearrange("p (a b) -> p a b", a=16), AX.X, ALU.add))
                sync()
                o(dve.tensor_scalar(g_t2, g_t2, 1.0 / AD, EPS, ALU.mult, ALU.add))
                post(a_in)
                dve.wait_ge(a_rt, m + 1)
                o(dve.reciprocal(g_t3, g_t2))
                sync()
                for t in range(TT):
                    o(dve.tensor_tensor(h8(src[:, t, :]), h8(src[:, t, :]),
                                        bc(g_t3[:, 8 * t:8 * t + 8].unsqueeze(2), [P, AH, AD]), ALU.mult))
                sync()
                for t in range(TT):
                    o(dve.tensor_tensor(h8(src[:, t, :]), h8(src[:, t, :]), bc(wn.unsqueeze(1), [P, AH, AD]), ALU.mult))
                sync()
                for t in range(TT):
                    cs = bc(consts[:, C_ROPE + t * 32:C_ROPE + (t + 1) * 32].unsqueeze(1), [P, AH, 32])
                    sn = bc(consts[:, C_ROPE + 64 + t * 32:C_ROPE + 64 + (t + 1) * 32].unsqueeze(1), [P, AH, 32])
                    lo, hi = h8(src[:, t, :])[:, :, 0:32], h8(src[:, t, :])[:, :, 32:64]
                    r4 = rt.rearrange("p (q h c) -> p q h c", q=4, h=AH)
                    o(dve.tensor_tensor(r4[:, 0], lo, cs, ALU.mult))
                    o(dve.tensor_tensor(r4[:, 1], hi, sn, ALU.mult))
                    o(dve.tensor_tensor(r4[:, 2], hi, cs, ALU.mult))
                    o(dve.tensor_tensor(r4[:, 3], lo, sn, ALU.mult))
                    sync()
                    o(dve.tensor_tensor(lo, r4[:, 0], r4[:, 1], ALU.subtract))
                    o(dve.tensor_tensor(hi, r4[:, 2], r4[:, 3], ALU.add))
                    sync()
                dve.sem_inc(gla_op, 1)
                dst = (qT, kT)[m]
                for t in range(TT):
                    for g in range(2):
                        b = job()
                        o(dve.tensor_copy(dst[0:64, 4 * g:4 * g + 4, t * P:(t + 1) * P], b4(b)[0:64]))
                        empty()
            tri = consts[:, C_NEGB:C_NEGB + P]
            for t in range(TT):
                kw = (t + 1) * P
                for g in range(4):
                    b = job()
                    if t:
                        o(dve.tensor_scalar(sc[:, 2 * g:2 * g + 2, 0:P], two(b)[:, :, 0:P], AD ** -0.5, None, ALU.mult))
                    o(dve.scalar_tensor_tensor(sc[:, 2 * g:2 * g + 2, t * P:kw], two(b)[:, :, t * P:kw], AD ** -0.5,
                                               bc(tri.unsqueeze(1), [P, 2, P]), ALU.mult, ALU.add))
                    empty()
                o(dve.tensor_reduce(na_m[:, 0:8], sc[:, :, 0:kw], AX.X, ALU.max))
                sync()
                o(dve.tensor_scalar(na_nm[:, 0:8], na_m[:, 0:8], -1.0, None, ALU.mult))
                post(a_op)
                dve.wait_ge(a_exp, t + 1)
                o(dve.reciprocal(na_r[:, 0:8], na_s[:, 0:8]))
                for g in range(4):
                    b = job()
                    o(dve.tensor_copy(pT[:, 2 * g:2 * g + 2, 0:t + 1, :],
                                      b[:, :].rearrange("p (a k n) -> p a k n", a=2, k=2)[:, :, 0:t + 1, :]))
                    empty()
                b = job()
                o(dve.tensor_tensor(h8(y2[:, t, 512:1024]), h8(b[:, :]), bc(na_r[:, 0:8].unsqueeze(2), [P, AH, AD]),
                                    ALU.mult))
                empty()
            dve.wait_ge(in_nw2, 64)
            for t in range(TT):
                o(dve.tensor_tensor(y2[:, t, :], y2[:, t, :], nw[:, :], ALU.mult))
            post(h_ready)
            dve.sem_inc(nw_used, 1)
            to_hT()
            for nn in range(2):
                for t in range(TT):
                    b = job()
                    o(dve.tensor_tensor(x[:, t, nn * 512:(nn + 1) * 512], x[:, t, nn * 512:(nn + 1) * 512], b[:, :],
                                        ALU.add))
                    empty()
            post(x3_ready)
            norm_weight(80)

            def queries_in(g):
                for c in range(2):
                    b = job()
                    o(dve.tensor_copy(qpT[:, 4 * g + 2 * c:4 * g + 2 * c + 2, :], two(b)))
                    empty()

            def scores_in(g):
                for t in range(TT):
                    b = job()
                    o(dve.tensor_copy(s_all[:, t, 4 * g:4 * g + 4, :], b4(b)))
                    empty()

            def best16(rows, val, ind, src):
                for r in range(rows):
                    o(dve.max(val(r)[:, 0:8], src(r)))
                sync()
                for r in range(rows):
                    o(dve.max_index(ind(r)[:, 0:8], val(r)[:, 0:8], src(r)))
                sync()
                for r in range(rows):
                    o(dve.match_replace(src(r), val(r)[:, 0:8], src(r), NEG))
                sync()
                for r in range(rows):
                    o(dve.max(val(r)[:, 8:16], src(r)))
                sync()
                for r in range(rows):
                    o(dve.max_index(ind(r)[:, 8:16], val(r)[:, 8:16], src(r)))
                sync()

            def route(g):
                best16(4 * TT, lambda r: sv[:, r, :], lambda r: si[:, r, :],
                       lambda r: s_all[:, r // 4, 4 * g + r % 4, :])
                o(dve.tensor_copy(sif, si))
                for r in range(2 * TT):
                    o(dve.tensor_tensor(cand[:, r, :, :], bc(sv[:, 2 * r, :].unsqueeze(2), [P, 16, 16]),
                                        bc(sv[:, 2 * r + 1, :].unsqueeze(1), [P, 16, 16]), ALU.add))
                sync()
                best16(2 * TT, lambda r: tv[:, r, :], lambda r: ti[:, r, :],
                       lambda r: cand[:, r, :, :].rearrange("p a b -> p (a b)"))
                gv3 = gates[:, g % 2, :, :].rearrange("p t (h k) -> p (t h) k", h=2)
                o(dve.tensor_tensor(gv3, tv, bc(tv[:, :, 0:1], [P, 2 * TT, 16]), ALU.subtract))
                post(e_in)
                o(dve.tensor_scalar(tj, ti, 15, None, ALU.bitwise_and))
                sync()
                o(dve.tensor_scalar(ti, ti, 4, None, ALU.logical_shift_right))
                o(dve.tensor_copy(tjf, tj))
                sync()
                o(dve.tensor_copy(tif, ti))
                sync()
                io16 = consts[:, C_IOTA:C_IOTA + 16]
                for half, (pos, dst) in enumerate(((tif, e0), (tjf, e1))):
                    o(dve.tensor_tensor(oh.rearrange("p a b c -> p (a b) c"), bc(io16.unsqueeze(1), [P, 2 * TT * 16, 16]),
                                        bc(pos.rearrange("p a b -> p (a b)").unsqueeze(2), [P, 2 * TT * 16, 16]),
                                        ALU.is_equal))
                    sync()
                    for r in range(2 * TT):
                        o(dve.tensor_tensor(oh[:, r, :, :], oh[:, r, :, :],
                                            bc(sif[:, 2 * r + half, :].unsqueeze(1), [P, 16, 16]), ALU.mult))
                    sync()
                    o(dve.tensor_reduce(dst.rearrange("p a b -> p (a b)"), oh.rearrange("p a b c -> p (a b) c"),
                                        AX.X, ALU.add))
                    sync()
                o(dve.scalar_tensor_tensor(e0, e0, float(PK), e1, ALU.mult, ALU.add))
                sync()
                o(dve.tensor_copy(idx_all[:, g % 2, :, :].rearrange("p t k -> p (t k)"), e0.rearrange("p a b -> p (a b)")))
                post(idx_ready)
                dve.wait_ge(e_act, g + 1)
                o(dve.tensor_reduce(gsum, gv3, AX.X, ALU.add))
                sync()
                o(dve.reciprocal(gsum, gsum))
                sync()
                o(dve.tensor_tensor(gv3, gv3, bc(gsum.unsqueeze(2), [P, 2 * TT, 16]), ALU.mult))
                sync()

            queries_in(0)
            queries_in(1)
            scores_in(0)
            dve.sem_inc(u_free, U_RING)
            route(0)
            queries_in(2)
            scores_in(1)
            queries_in(3)
            scores_in(2)
            scores_in(3)
            o(dve.memset(zeros, 0.0))
            post(zeros_ready)
            for n2 in range(NG):
                if n2:
                    route(n2)
                with dve.Fori(0, 2) as q:
                    for t in range(TT):
                        step = q * TT + (2 * TT * n2 + t)
                        for k in range(16):
                            dve.wait_ge(u_landed[k % U_RING], step * 32 + 16 * (k // U_RING + 1))
                            dve.wait_ge(u_free, step * 16 + (U_RING + k - 1))
                            dve.tensor_tensor_reduce(out=junk[:, k % 2, :], in0=u_ring(k), in1=h_tok[:, t, :], scale=1.0,
                                                     scalar=0.0, op0=ALU.mult, op1=ALU.add,
                                                     accum_out=dots[:, t, k:k + 1]).then_inc(u_free, 1)
                        dve.wait_ge(gelu_done, step + 1)
                        dve.tensor_tensor(w_cur[:, t, :], gel[:, t, :],
                                          gates[:, n2 % 2, t, bass.ds(q * 16, 16)], ALU.mult).then_inc(w_ready, 1)
            dve.wait_ge(p_done, 1)
            for t in range(TT):
                for n2 in range(2):
                    xs = x[:, t, n2 * 512:(n2 + 1) * 512]
                    o(dve.tensor_tensor(xs, xs, ps[2 * t + n2][:, :], ALU.add))
                post(p_taken)


def kernel(**inputs):
    import concourse.bacc as _bacc
    from concourse.bass_utils import run_bass_kernel_spmd as _run

    f = {k: np.asarray(v) for k, v in inputs.items()}
    rows = lambda a: np.ascontiguousarray(a.reshape(1, -1))
    arrays = {
        "x": f["x"][0],
        "c": np.ascontiguousarray(f["c"].reshape(KC, P).T),
        "consts": shape_constants(),
        "window": window_selector(),
        "w_ada": f["w_ada"][0],
        "b_ada": f["b_ada"],
        "norm_mix_w": f["norm_mix_w"],
        "norm_ffn_w": f["norm_ffn_w"],
        "w_in": f["w_in"][0],
        "conv_a_w": np.ascontiguousarray(f["conv_a_w"][0].reshape(3, 2, P).transpose(2, 1, 0).reshape(P, 6)),
        "gdn_conv_w": np.ascontiguousarray(f["gdn_conv_w"][0].reshape(3, 12, P).transpose(2, 1, 0).reshape(P, 36)),
        "gdn_a_log": rows(f["gdn_a_log"]),
        "gdn_dt_bias": rows(f["gdn_dt_bias"]),
        "gdn_norm_w": f["gdn_norm_w"],
        "na_rpb": np.concatenate([f["na_rpb"][0].reshape(NA_H * N_DR, N_DC).T,
                                  np.ones((1, NA_H * N_DR), np.float32)]),
        "w_out": f["w_out"][0],
        "router_w": np.concatenate([f["router_group_w"][0], f["router_expert_w"][0]], axis=1),
        "router_b": np.concatenate([f["router_group_b"], f["router_expert_b"]], axis=1),
        "expert_w1": f["expert_w1"][0],
        "expert_w3": f["expert_w3"][0],
        "expert_w2": f["expert_w2"][0],
        "final_norm_w": rows(f["final_norm_w"]),
        "norm1_w_2": f["norm1_w_2"],
        "w_in_2": f["w_in_2"][0],
        "gla_w_alpha": f["gla_w_alpha_2"][0],
        "gla_b_alpha": np.ascontiguousarray(f["gla_b_alpha_2"][0].reshape(LH, LDK).T),
        "gla_out_norm_w": f["gla_out_norm_w_2"],
        "moba_q_norm_w": f["moba_q_norm_w_2"],
        "moba_k_norm_w": f["moba_k_norm_w_2"],
        "mix_scale": f["mix_scale_2"],
        "w_out_2": f["w_out_2"][0],
        "norm2_w": f["norm2_w_2"],
        "peer_w_query": f["peer_w_query_2"][0],
        "subkeys": np.ascontiguousarray(f["peer_subkeys_2"][0].reshape(16, PK, P).transpose(2, 0, 1)),
        "peer_u": f["peer_u_2"][0],
        "peer_v": f["peer_v_2"][0],
    }
    nc = _bacc.Bacc("TRN2", target_bir_lowering=False, num_devices=1)
    io, feed = {}, {}
    for name, a in arrays.items():
        a = np.ascontiguousarray(a)
        feed[name + "_d"] = a
        io[name] = nc.dram_tensor(name + "_d", a.shape, mybir.dt.from_np(a.dtype), kind="ExternalInput").ap()
    io["out"] = nc.dram_tensor("out_d", (T, D), F32, kind="ExternalOutput").ap()
    two_blocks(nc, io)
    r = _run(nc, [feed], core_ids=[0])
    return r.results[0]["out_d"].reshape(1, T, D)
```

```python
from contextlib import ExitStack

import numpy as np
import concourse.bass as bass
from concourse import mybir

F32 = mybir.dt.float32
U32 = mybir.dt.uint32
ALU = mybir.AluOpType
ACT = mybir.ActivationFunctionType
AX = mybir.AxisListType

P = 128
T = 256
TT = T // P
D = 1024
KC = D // P
EPS = 1e-6
NEG = -1e30
N_MOD = 6 * D // 512
CONV_W = 256
NA_H, NA_DH = 4, 64
ROW_W, N_ROWS = 64, T // 64
NA_KW, NA_KH = 16, 8
N_DR, N_DC = 2 * NA_KH - 1, 2 * NA_KW - 1
GH, GD = 4, 128
LEVELS = 7
W_IN_TILES = 7
N_EXP, N_GRP, EPG = 32, 4, 8
B2_JOB = 190
GD_JOB = 72
GD_JOBS = 8 + 2 + 6 * (LEVELS - 2) + 4 + 7
F_OPS = 2 + 2 * 19
S_OPS = 13
CAP = 64
D_EXP = 512
LH, LDK, LDV, CH = 4, 64, 128, 64
AH, AD = 8, 64
PH, PK, PTOP = 8, 128, 16
U_RING, V_RING = 8, 16
RING = 6

_off = 0


def _take(n):
    global _off
    a = _off
    _off += n
    return a


C_ID = _take(P)
C_UINC = _take(P)
C_LINC = _take(P)
C_NEGF = _take(P)
C_NEGB = _take(P)
C_LVL = _take(2 * LEVELS * P)
C_IOTA = _take(P)
C_BLK = _take(P)
C_ONE = _take(P)
C_DN4 = _take(N_GRP)
C_ROPE = _take(4 * 32)
NCONST = _off


def shape_constants():
    c = np.zeros((P, NCONST), np.float32)
    i = np.arange(P)
    c[:, C_ID:C_ID + P] = np.eye(P)
    le = (i[:, None] <= i[None, :])
    ge = le.T
    c[:, C_UINC:C_UINC + P] = le
    c[:, C_LINC:C_LINC + P] = ge
    c[:, C_NEGF:C_NEGF + P] = np.where(le, 0, NEG)
    c[:, C_NEGB:C_NEGB + P] = np.where(ge, 0, NEG)
    for lv in range(LEVELS):
        same = (i[:, None] >> (lv + 1)) == (i[None, :] >> (lv + 1))
        m = same & (((i[:, None] >> lv) & 1) == 0) & (((i[None, :] >> lv) & 1) == 1)
        c[:, C_LVL + lv * P:C_LVL + (lv + 1) * P] = m
        c[:, C_LVL + (LEVELS + lv) * P:C_LVL + (LEVELS + lv + 1) * P] = m.T
    c[:, C_IOTA:C_IOTA + P] = i[None, :]
    c[:, C_BLK:C_BLK + P] = le & ((i[:, None] // 64) == (i[None, :] // 64))
    c[:, C_ONE:C_ONE + P] = 1.0
    c[:, C_DN4:C_DN4 + N_GRP] = 8 - np.arange(N_GRP)
    inv = (np.float32(10000.0) ** (-np.arange(32, dtype=np.float32) / np.float32(32))).astype(np.float32)
    ang = (np.arange(T, dtype=np.float32)[:, None] * inv[None, :]).astype(np.float32)
    for t in range(TT):
        c[:, C_ROPE + t * 32:C_ROPE + (t + 1) * 32] = np.cos(ang[t * P:(t + 1) * P])
        c[:, C_ROPE + 64 + t * 32:C_ROPE + 64 + (t + 1) * 32] = np.sin(ang[t * P:(t + 1) * P])
    return c


def window_selector():
    col = np.arange(ROW_W)
    start = np.clip(col - NA_KW // 2, 0, ROW_W - NA_KW)
    e = np.zeros((N_DC + 1, ROW_W, ROW_W), np.float32)
    for c in range(ROW_W):
        for k in range(ROW_W):
            if start[c] <= k < start[c] + NA_KW:
                e[k - c + NA_KW - 1, c, k] = 1.0
            else:
                e[N_DC, c, k] = NEG
    return e.reshape(N_DC + 1, ROW_W * ROW_W)


class Count:

    def __init__(self, eng, sem, base=0):
        self.eng, self.sem, self.base, self.n = eng, sem, base, 0

    def at(self, base):
        self.base, self.n = base, 0

    def value(self, more=0):
        return self.base + (self.n + more)

    def wait(self, more=0):
        if isinstance(self.base, int) and self.base + self.n + more <= 0:
            return
        self.eng.wait_ge(self.sem, self.base + (self.n + more))


def two_blocks(nc, io):
    ctx = ExitStack()
    with ctx:
        def sb(name, shape, dt=F32):
            return ctx.enter_context(nc.sbuf_tensor(name, shape, dt))

        def sem(name):
            return ctx.enter_context(nc.semaphore(name))

        ring = sb("ring", [P, RING, 4096])
        x = sb("x", [P, TT, D])
        hT = sb("hT", [P, KC, T])
        mod = sb("mod", [P, 4, D])
        nw = sb("nw", [P, D])
        consts = sb("consts_sb", [P, NCONST])
        tail_w = sb("tail_w", [P, KC, 36])
        small = sb("small", [P, 512])
        WORK = 15664
        work = sb("work", [P, WORK])
        ident = consts[:, C_ID:C_ID + P]
        u_inc = consts[:, C_UINC:C_UINC + P]
        l_inc = consts[:, C_LINC:C_LINC + P]

        def W(at, *shape):
            n = 1
            for s in shape:
                n *= s
            assert at + n <= WORK
            v = work[:, at:at + n]
            if len(shape) == 2:
                v = v.rearrange("p (a b) -> p a b", a=shape[0])
            if len(shape) == 3:
                v = v.rearrange("p (a b c) -> p a b c", a=shape[0], b=shape[1])
            return v

        def half_of(h):
            return slice(64 * (h % 2), 64 * (h % 2) + 64)

        _s = [0]

        def S(n):
            a = _s[0]
            _s[0] += n
            assert _s[0] <= 512
            return small[:, a:a + n]

        sel_w = W(0, 4096)
        bias_rows = W(4096, 4096)
        ab1 = W(9216, 2, D)
        h_tok = W(0, TT, D)
        cond_z = W(14336, KC, 32)
        part = W(14592, 2, 512)
        g_raw = W(0, 12, T)
        g_cv = W(3072, 12, T)
        c3 = W(6144, 6, T)
        z = W(7680, TT, 512)
        gab = W(8704, TT, 16)
        NA0 = 9216
        na_q = W(NA0, 2, T)
        na_k = W(NA0 + 1024, 2, T)
        na_v = W(NA0 + 2048, TT, 256)
        na_bias = W(NA0 + 2560, TT, 4, T)
        na_p = W(NA0 + 4608, 4, T)
        na_pT = W(6144, 4, 2, P)
        na_o = W(8768, 4, NA_DH)
        k_tok = W(0, TT, 4, P)
        v_tok = W(1024, TT, 4, P)
        o_acc = W(2048, TT, 4, P)
        sq = W(NA0, 8, T)
        rn = W(NA0 + 2048, 8, T)
        GD0 = NA0
        LT = W(GD0, TT, 4, P)
        X = W(GD0 + 1024, TT, 4, P)
        XT = W(GD0 + 2048, TT, 4, P)
        inT = W(GD0 + 3072, TT, 4, P)
        tB = W(GD0 + 4096, TT, 4, P)
        tU = W(GD0 + 5120, TT, 4, P)
        tD = W(6144, TT, 4, P)
        acc = W(2048, TT, D)
        xeT = W(4096, KC, P)
        pm = W(5120, TT, P)
        pg = W(5376, 2, TT, P)
        pgT = W(5888, TT, P)
        sil = W(6144, D_EXP)
        act_p = W(6656, D_EXP)
        actT = W(7168, 4, P)
        y_sb = W(9984, D)
        sil_d = W(7936, 4, T)
        act_d = W(8960, 4, T)
        _r = [11008]

        def R(*shape):
            n = int(np.prod(shape))
            a = _r[0]
            _r[0] += n
            return W(a, *shape)

        lg = R(TT, 36)
        rb = R(36)
        gmx = R(TT)
        oh4 = R(TT, N_GRP)
        e4 = R(TT, N_GRP)
        pen = R(TT, N_GRP)
        pgt = R(TT)
        elm = R(TT, N_EXP)
        v8 = R(TT, 8)
        i8 = R(TT, 8).bitcast(U32)
        i8f = R(TT, 8)
        gt = R(TT, 4)
        G = R(TT, 36)
        M = R(TT, 36)
        rk = R(TT, 36)
        cnt = R(36)
        rk4 = R(TT, 4)
        g4 = R(TT, 4)
        flag = R(4).bitcast(mybir.dt.int32)
        y2 = W(0, TT, D)
        gq = W(2048, LH // 2, T)
        gk = W(3072, LH // 2, T)
        gv = W(4096, TT, 512)
        ggate = W(5120, TT, 512)
        gb_ = W(6144, LH // 2, T)
        ge = W(7168, LH // 2, T)
        mq = W(8192, TT, 512)
        mk = W(9216, TT, 512)
        mv = W(10240, TT, 512)
        kin = W(11264, LH // 2, T)
        qz = W(12288, LH // 2, 4, P)
        grT = W(12288, T)
        walpha = W(12544, 256)
        AT = W(14336, TT, LH, P)
        kst = W(6656, TT, LH, LDK)
        st = [None] + [W(7168 + 256 * c, LH // 2, LDV) for c in range(3)]
        mqk = W(8192, 2 * TT, 512)
        rt = W(0, 2 * TT, 512)
        a_ms = W(2048, 2 * TT * AH)
        a_rs = W(2112, 2 * TT * AH)
        qT = hT[:, 0:AH // 2, :]
        kT = mod[:, 1, :].rearrange("p (b n) -> p b n", n=T)
        sc = W(8192, AH, T)
        pT = W(2048, AH, 2, P)
        NG = PH // 2
        qpT = W(2048, 16, T)
        s_all = W(6144, TT, 16 * PK).rearrange("p t (c k) -> p t c k", k=PK)
        subT = W(10240, 16, PK)
        cand = W(12288, 2 * TT, 16, 16)
        oh = W(13312, 2 * TT, 16, 16)
        sv = W(14336, 4 * TT, 16)
        si = W(14464, 4 * TT, 16).bitcast(U32)
        sif = W(14592, 4 * TT, 16)
        tv = W(14720, 2 * TT, 16)
        ti = W(14784, 2 * TT, 16).bitcast(U32)
        tj = W(14848, 2 * TT, 16).bitcast(U32)
        tif = W(14912, 2 * TT, 16)
        tjf = W(14976, 2 * TT, 16)
        e0 = W(15040, 2 * TT, 16)
        e1 = W(15104, 2 * TT, 16)
        gates = W(15168, 2, TT, 32)
        idx_all = W(15296, 2, TT, 32).bitcast(U32)
        idx_cur = W(15424, TT, 16).bitcast(U32)
        dots = W(15456, TT, 16)
        gel = W(15488, TT, 16)
        w_cur = W(15520, TT, 16)
        gsum = W(15552, 2 * TT)
        junk = W(2048, 2, D)
        diag = W(4096, 4, P)
        zeros = W(4608, P)
        mixT = hT
        gn_w = W(9024, P)
        ones = consts[:, C_ONE:C_ONE + P]
        conv_a = S(6)
        conv_g = S(36)
        cT = S(8)
        a_log = S(8)
        dt_b = S(8)
        rpb = small[:, 448:508]

        ms = S(8)
        rstd = S(8)
        g_e = S(8)
        g_t = S(16)
        g_t2 = S(16)
        g_t3 = S(16)
        g_g = S(16)
        g_be = S(16)
        g_c = S(16)
        g_nc = S(16)
        g_tot = S(16)
        g_eg = S(16)
        g_kd = S(16)
        na_m = S(8)
        na_nm = S(8)
        na_s = S(8)
        na_r = S(8)
        ps = [ctx.enter_context(nc.psum_tensor(f"ps{i}", [P, 512], F32)) for i in range(8)]

        scratch_bias = nc.dram_tensor("bias_scratch", [NA_H * N_DR, ROW_W * ROW_W], F32).ap()

        landed = [sem(f"landed{i}") for i in range(RING)]
        w_used = sem("w_used")
        pe_done = sem("pe_done")
        evac = sem("evac")
        dve_n = sem("dve_n")
        act_n = sem("act_n")
        in_start = sem("in_start")
        in_small = sem("in_small")
        in_bias0 = sem("in_bias0")
        in_nw = sem("in_nw")
        nw_used = sem("nw_used")
        in_tail = sem("in_tail")
        in_ada = sem("in_ada")
        bias_out = sem("bias_out")
        bias_in = sem("bias_in")
        tail_used = sem("tail_used")
        cond_act = sem("cond_act")
        cond_ready = sem("cond_ready")
        bias_ready = sem("bias_ready")
        ms_ready = sem("ms_ready")
        rt_ready = sem("rt_ready")
        h_ready = sem("h_ready")
        hT_ready = sem("hT_ready")
        conv_ready = sem("conv_ready")
        silu_ready = sem("silu_ready")
        sq_ready = sem("sq_ready")
        na_sc = sem("na_sc")
        na_exp = sem("na_exp")
        na_out = sem("na_out")
        gab_in = sem("gab_in")
        gab_act = sem("gab_act")
        g_ready = sem("g_ready")
        l2_in = sem("l2_in")
        l2_rt = sem("l2_rt")
        qk_ready = sem("qk_ready")
        d_in = sem("d_in")
        d_out = sem("d_out")
        u_copied = sem("u_copied")
        gd_op = sem("gd_op")
        y_ready = sem("y_ready")
        mix_ready = sem("mix_ready")
        x1_ready = sem("x1_ready")
        out_done = sem("out_done")
        in_route = sem("in_route")
        zeros_ready = sem("zeros_ready")
        gathers = sem("gathers")
        in_nw2 = sem("in_nw2")
        in_tail2 = sem("in_tail2")
        rt_logits = sem("rt_logits")
        rt_exp = sem("rt_exp")
        masks_ready = sem("masks_ready")
        flag_ready = sem("flag_ready")
        f_done = sem("f_done")
        f_free = sem("f_free")
        f_dve = sem("f_dve")
        f_act = sem("f_act")
        p_ready = sem("p_ready")
        s_done = sem("s_done")
        s_free = sem("s_free")
        s_dve = sem("s_dve")
        s_act = sem("s_act")
        moe_done = sem("moe_done")
        b2_small = sem("b2_small")
        z_in = sem("z_in")
        z_act = sem("z_act")
        b_in = sem("b_in")
        b_act = sem("b_act")
        in_nw3 = sem("in_nw3")
        roped = sem("roped")
        v_copied = sem("v_copied")
        gla_op = sem("gla_op")
        o_in = sem("o_in")
        a_in = sem("a_in")
        a_rt = sem("a_rt")
        a_op = sem("a_op")
        a_exp = sem("a_exp")
        x3_ready = sem("x3_ready")
        in_sub = sem("in_sub")
        e_in = sem("e_in")
        e_act = sem("e_act")
        idx_ready = sem("idx_ready")
        idx_copied = sem("idx_copied")
        u_landed = [sem(f"u_landed{i}") for i in range(U_RING)]
        v_landed = [sem(f"v_landed{i}") for i in range(V_RING)]
        u_free = sem("u_free")
        v_free = sem("v_free")
        gelu_done = sem("gelu_done")
        w_ready = sem("w_ready")
        diag_ready = sem("diag_ready")
        p_done = sem("p_done")
        p_taken = sem("p_taken")

        block = ctx.enter_context(nc.Block())

        w_in_v = io["w_in"].rearrange("(k p) n -> p k n", p=P)
        w_ada_v = io["w_ada"].rearrange("(k p) n -> p k n", p=P)
        w_out_v = io["w_out"].rearrange("(k p) n -> p k n", p=P)
        tiles = [w_ada_v[:, :, n * 512:(n + 1) * 512] for n in range(4)]
        tiles += [w_in_v[:, :, n * 512:(n + 1) * 512] for n in range(W_IN_TILES)]
        tiles += [w_ada_v[:, :, n * 512:(n + 1) * 512] for n in range(4, N_MOD)]
        tiles += [w_out_v[:, :, n * 512:(n + 1) * 512] for n in range(2)]

        N_HEAD = len(tiles)
        N_MOE = 3 * N_EXP
        w1_v, w3_v = (io[n].rearrange("e (k p) n -> e p k n", p=P) for n in ("expert_w1", "expert_w3"))
        w2_v = io["expert_w2"].rearrange("e (k p) n -> e p k n", p=P)
        w_in2_v = io["w_in_2"].rearrange("(k p) n -> p k n", p=P)
        w_out2_v = io["w_out_2"].rearrange("(k p) n -> p k n", p=P)
        w_q_v = io["peer_w_query"].rearrange("(k p) n -> p k n", p=P)
        tiles2 = [w_in2_v[:, :, a:a + 512] for a in (1552, 2064, 0, 512, 1024, 2576)]
        tiles2 += [w_out2_v[:, :, n * 512:(n + 1) * 512] for n in range(2)]
        tiles2 += [w_q_v[:, :, n * 512:(n + 1) * 512] for n in range(4)]

        def slot(i, cols=512):
            return ring[:, i % RING, :].rearrange("p (k n) -> p k n", n=cols)

        def u_ring(k):
            return ring[:, 3 + k % U_RING // 4, k % 4 * D:(k % 4 + 1) * D]

        def v_ring(k):
            return ring[:, (5 + k // 4) % RING, k % 4 * D:(k % 4 + 1) * D]

        @block.sync
        def _(sp):
            sp.dma_start(x[:, :, :], io["x"].rearrange("(a p) d -> p a d", p=P)).then_inc(in_start, 16)
            sp.dma_start(cT, io["c"]).then_inc(in_start, 16)
            sp.dma_start(consts[:, :], io["consts"]).then_inc(in_start, 16)
            sp.dma_start(sel_w[0:32, :], io["window"]).then_inc(in_bias0, 16)
            sp.dma_start(rpb[0:N_DC + 1, :], io["na_rpb"]).then_inc(in_bias0, 16)
            sp.dma_start(nw[:, :], io["norm_mix_w"].to_broadcast([P, D])).then_inc(in_nw, 16)
            sp.dma_start(ab1.rearrange("p a d -> p (a d)"), io["b_ada"][:, 0:2 * D].to_broadcast([P, 2 * D]))\
                .then_inc(in_ada, 16)
            for i in range(RING):
                sp.dma_start(slot(i), tiles[i]).then_inc(landed[i], 16)
            sp.dma_start(mod[:, :, :].rearrange("p a d -> p (a d)"), io["b_ada"][:, 2 * D:6 * D].to_broadcast([P, 4 * D]))\
                .then_inc(in_ada, 16)
            sp.dma_start(conv_a, io["conv_a_w"]).then_inc(in_small, 16)
            sp.dma_start(conv_g, io["gdn_conv_w"]).then_inc(in_small, 16)
            sp.dma_start(a_log, io["gdn_a_log"].to_broadcast([P, 8])).then_inc(in_small, 16)
            sp.dma_start(dt_b, io["gdn_dt_bias"].to_broadcast([P, 8])).then_inc(in_small, 16)
            sp.dma_start(tail_w[:, :, 0:16], w_in_v[:, :, 3584:3600]).then_inc(in_tail, 16)
            sp.wait_ge(bias_ready, 1)
            sp.dma_start(scratch_bias, bias_rows[0:NA_H * N_DR, :]).then_inc(bias_out, 16)
            sp.wait_ge(bias_out, 16)
            sp.dma_start(gn_w[:, :], io["gdn_norm_w"].to_broadcast([P, P])).then_inc(in_small, 16)
            for r in range(N_ROWS):
                src = scratch_bias.rearrange("(h a) (c k) -> c h a k", h=NA_H, c=ROW_W)[
                    :, :, NA_KH - 1 - r:NA_KH - 1 - r + N_ROWS, :]
                for h in range(NA_H):
                    dst = na_bias[(r % 2) * ROW_W:(r % 2 + 1) * ROW_W, r // 2, h, :]
                    sp.dma_start(dst.rearrange("p (a k) -> p a k", a=N_ROWS), src[:, h, :, :]).then_inc(bias_in, 16)
            for i in range(RING, len(tiles)):
                sp.wait_ge(w_used, i - RING + 1)
                sp.dma_start(slot(i), tiles[i]).then_inc(landed[i % RING], 16)
            with sp.Fori(0, N_EXP // 2) as i:
                for l in range(6):
                    sp.wait_ge(w_used, i * 6 + (N_HEAD + l - RING + 1))
                    e = i * 2 + l % 2
                    v = (w1_v, w3_v, w2_v)[l // 2]
                    sl = (N_HEAD + l) % RING
                    sp.dma_start(slot(sl, 1024 if l >= 4 else 512), v[e, :, :, :]).then_inc(landed[sl], 16)
            for i in range(len(tiles2)):
                n2 = N_HEAD + N_MOE + i
                sp.wait_ge(w_used, n2 - RING + 1)
                sp.dma_start(slot(n2), tiles2[i]).then_inc(landed[n2 % RING], 16)
            out_v = io["out"].rearrange("(a p) d -> p a d", p=P)
            for t in range(TT):
                sp.wait_ge(p_taken, t + 1)
                sp.dma_start(out_v[:, t, :], x[:, t, :]).then_inc(out_done, 16)
            sp.wait_ge(out_done, 32)

        @block.scalar
        def _(act):
            n = [0]

            def o(ins):
                n[0] += 1
                ins.then_inc(act_n, 1)

            def sync():
                act.wait_ge(act_n, n[0])

            norms = [0]

            def norm_roots():
                norms[0] += 1
                act.wait_ge(ms_ready, norms[0])
                act.activation(rstd[:, 0:TT], ms[:, 0:TT], ACT.Sqrt).then_inc(rt_ready, 1)

            act.wait_ge(in_start, 48)
            act.activation(g_e[:, :], cT, ACT.Silu).then_inc(cond_act, 1)
            norm_roots()
            act.wait_ge(gab_in, 1)
            a2 = g_t.rearrange("p (t c) -> p t c", t=TT)
            o(act.activation(g_t2[:, :], g_t, ACT.Abs))
            sync()
            o(act.activation(g_t3[:, :], g_t2, ACT.Exp, scale=-1.0))
            o(act.activation(g_e[:, :], a_log, ACT.Exp))
            sync()
            o(act.activation(g_t2[:, :], g_t3, ACT.Ln, bias=1.0))
            o(act.activation(g_be.rearrange("p (t c) -> p t c", t=TT), gab[:, :, 8:16], ACT.Sigmoid))
            sync()
            act.sem_inc(gab_act, 1)
            act.wait_ge(conv_ready, 1)
            o(act.activation(g_cv[:, :, :], g_cv[:, :, :], ACT.Silu))
            sync()
            act.sem_inc(silu_ready, 1)
            for t in range(TT):
                act.wait_ge(na_sc, t + 1)
                for h in range(NA_H):
                    o(act.activation(na_p[:, h, :], na_p[:, h, :], ACT.Exp, bias=na_nm[:, h:h + 1],
                                     accum_out=na_s[:, h:h + 1]))
                sync()
                act.sem_inc(na_exp, 1)
            act.wait_ge(na_out, 1)
            o(act.activation(sq[:, :, :], g_cv[:, 0:8, :], ACT.Square))
            sync()
            act.sem_inc(sq_ready, 1)
            for j in range(4):
                act.wait_ge(l2_in, j + 1)
                act.activation(rn[:, 2 * j:2 * j + 2, :], rn[:, 2 * j:2 * j + 2, :], ACT.Sqrt).then_inc(l2_rt, 1)
            o(act.activation(z[:, :, :], z[:, :, :], ACT.Silu))
            act.wait_ge(qk_ready, 1)
            o(act.activation(g_eg[:, :], g_c, ACT.Exp))
            o(act.activation(g_kd[:, :], g_kd, ACT.Exp))
            sync()
            act.sem_inc(gab_act, 1)
            for d in range(2):
                for t in range(TT):
                    act.wait_ge(d_in, 2 * d + t + 1)
                    for h in range(GH):
                        col = t * 8 + d * 4 + h
                        o(act.activation(tD[:, t, h, :], tD[:, t, h, :], ACT.Exp, bias=g_nc[:, col:col + 1]))
                    sync()
                    act.sem_inc(d_out, 1)
                for lv in range(1, LEVELS):
                    for t in range(TT):
                        jb = GD_JOB + GD_JOBS * d + 10 + 6 * (lv - 1) + t
                        act.wait_ge(pe_done, jb + 1)
                        act.activation(tU[:, t, :, :].rearrange("p a b -> p (a b)"), ps[jb % 8][:, :],
                                       ACT.Copy).then_inc(u_copied, 1)
            act.wait_ge(y_ready, 1)
            act.activation(rstd[:, 0:8], ms[:, 0:8], ACT.Sqrt).then_inc(rt_ready, 1)
            norm_roots()
            act.wait_ge(rt_logits, 1)
            act.activation(e4, e4, ACT.Exp).then_inc(rt_exp, 1)
            act.wait_ge(rt_logits, 2)
            act.activation(gt[:, :, 0:1], gt[:, :, 0:1], ACT.Exp).then_inc(rt_exp, 1)
            act.wait_ge(flag_ready, 1)
            many = act.value_load(flag[0:1, 0:1], min_val=0, max_val=1)
            with act.If(many == 0):
                with act.Fori(0, N_EXP // 4) as i:
                    for p in range(2):
                        jb = 2 + 12 * p
                        act.wait_ge(f_done, i * 24 + (jb + 1))
                        act.activation(sil, ps[jb % 8][:, :], ACT.Silu).then_inc(f_act, 1)
            with act.Else():
                with act.Fori(0, N_EXP // 2) as i:
                    for u in range(2):
                        for c in range(2):
                            act.wait_ge(s_done, i * 16 + (8 * u + c + 1))
                            act.activation(sil_d[:, 2 * c:2 * c + 2, :],
                                           ps[c][:, :].rearrange("p (a b) -> p a b", a=2), ACT.Silu).then_inc(s_act, 1)
            norm_roots()
            norm_roots()
            act.wait_ge(a_in, 1)
            act.activation(a_ms, a_ms, ACT.Sqrt).then_inc(a_rt, 1)
            for i, (dst, f) in enumerate(((gv, ACT.Copy), (ggate, ACT.Silu))):
                for t in range(TT):
                    jb = B2_JOB + 7 + 2 * i + t
                    act.wait_ge(pe_done, jb + 1)
                    act.activation(dst[:, t, :], ps[jb % 8][:, :], f).then_inc(v_copied, 1)
            act.wait_ge(z_in, 1)
            act.activation(ge, ge, ACT.Exp, scale=-1.0).then_inc(z_act, 1)
            act.wait_ge(z_act, 1)
            act.activation(ge, ge, ACT.Ln, bias=1.0).then_inc(z_act, 1)
            act.wait_ge(b_in, 1)
            act.activation(ge, gb_, ACT.Exp).then_inc(b_act, 1)
            act.wait_ge(b_in, 2)
            act.activation(ge, gb_, ACT.Exp, scale=-1.0).then_inc(b_act, 1)
            act.wait_ge(b_in, 3)
            act.activation(ge, ge, ACT.Exp).then_inc(b_act, 1)
            for t in range(TT):
                act.wait_ge(a_op, t + 1)
                kw = (t + 1) * P
                for h in range(AH):
                    o(act.activation(sc[:, h, 0:kw], sc[:, h, 0:kw], ACT.Exp, bias=na_nm[:, h:h + 1],
                                     accum_out=na_s[:, h:h + 1]))
                sync()
                act.sem_inc(a_exp, 1)
            act.wait_ge(o_in, 1)
            act.activation(rstd[:, 0:8], ms[:, 0:8], ACT.Sqrt).then_inc(rt_ready, 1)
            norm_roots()
            def exp_gates(g):
                act.wait_ge(e_in, g + 1)
                act.activation(gates[:, g % 2, :, :], gates[:, g % 2, :, :], ACT.Exp).then_inc(e_act, 1)

            exp_gates(0)
            for n2 in range(NG):
                for q in range(2):
                    if q and n2 < NG - 1:
                        exp_gates(n2 + 1)
                    for t in range(TT):
                        step = q * TT + (2 * TT * n2 + t)
                        act.wait_ge(u_free, step * 16 + (U_RING + 16))
                        act.activation(gel[:, t, :], dots[:, t, :], ACT.Gelu).then_inc(gelu_done, 1)
                        act.wait_ge(w_ready, step + 1)
                        for k in range(16):
                            act.wait_ge(v_free, step * 16 + (V_RING + k - 3))
                            act.activation(diag[:, k % 4, :], ident, ACT.Copy,
                                           scale=w_cur[:, t, k:k + 1]).then_inc(diag_ready, 1)

        @block.tensor
        def _(pe):
            j = [0]
            w = [0]

            def bank():
                if j[0] >= 8:
                    pe.wait_ge(evac, j[0] - 7)
                return ps[j[0] % 8]

            def full(ins):
                ins.then_inc(pe_done, 1)
                j[0] += 1

            def emptied():
                pe.wait_ge(evac, j[0])

            def weight_tile():
                i = w[0]
                pe.wait_ge(landed[i % RING], 16 * (i // RING + 1))
                w[0] += 1
                return slot(i)

            def transposes_to_hT():
                for t in range(TT):
                    for g in range(2):
                        b = bank()
                        for c in range(4):
                            k = 4 * g + c
                            last = pe.transpose(b[:, c * P:(c + 1) * P], h_tok[:, t, k * P:(k + 1) * P], ident)
                        full(last)

            def feature_major(b, at, wt, c0, n, last_of_tile=False):
                for k in range(KC):
                    last = pe.matmul(b[0:n, at:at + T], wt[:, k, c0:c0 + n], hT[:, k, :],
                                     start=(k == 0), stop=(k == KC - 1))
                return last

            def token_major(b, at, t, wt, c0, n):
                for k in range(KC):
                    last = pe.matmul(b[:, at:at + n], hT[:, k, t * P:(t + 1) * P], wt[:, k, c0:c0 + n],
                                     start=(k == 0), stop=(k == KC - 1))
                return last

            pe.wait_ge(in_start, 48)
            pe.wait_ge(in_bias0, 32)
            pe.wait_ge(cond_ready, 1)
            for n in range(8):
                full(pe.matmul(bank()[0:60, :], rpb[0:32, :], sel_w[0:32, n * 512:(n + 1) * 512],
                               start=True, stop=True))

            def modulation(tiles_):
                for n in range(tiles_):
                    wt = weight_tile()
                    b = bank()
                    for k in range(KC):
                        q = 32 * (k % 4)
                        last = pe.matmul(b[q:q + 32, :], cond_z[:, k, :], wt[:, k, :], start=(k < 4), stop=(k >= 4),
                                         tile_position=(0, q), skip_group_check=True)
                    full(last)
                    used()
                    emptied()
                    full(pe.matmul(bank()[:, :], ones, part[:, n % 2, :], start=True, stop=True))

            def used():
                pe.wait_ge(pe_done, j[0])
                pe.sem_inc(w_used, 1)

            modulation(4)
            pe.wait_ge(h_ready, 1)
            transposes_to_hT()
            pe.wait_ge(hT_ready, 1)

            wt = weight_tile()
            for c in range(2):
                b = bank()
                feature_major(b, 0, wt, c * 256, P)
                full(feature_major(b, T, wt, c * 256 + P, P))
            used()
            wt = weight_tile()
            b = bank()
            feature_major(b, 0, wt, 0, P)
            full(feature_major(b, T, wt, P, P))
            b = bank()
            feature_major(b, 0, wt, 256, P)
            full(feature_major(b, T, wt, 256 + P, P))
            used()
            wt = weight_tile()
            b = bank()
            feature_major(b, 0, wt, 0, P)
            full(feature_major(b, T, wt, P, P))
            b = bank()
            token_major(b, 0, 0, wt, 256, 256)
            full(token_major(b, 256, 1, wt, 256, 256))
            used()
            pe.wait_ge(in_tail, 16)
            b = bank()
            token_major(b, 0, 0, tail_w, 0, 16)
            full(token_major(b, 16, 1, tail_w, 0, 16))
            pe.wait_ge(pe_done, j[0])
            pe.sem_inc(tail_used, 1)
            for n in range(3):
                wt = weight_tile()
                for c in range(2):
                    b = bank()
                    feature_major(b, 0, wt, c * 256, P)
                    full(feature_major(b, T, wt, c * 256 + P, P))
                used()
            wt = weight_tile()
            for t in range(TT):
                full(token_major(bank(), 0, t, wt, 0, 512))
            used()
            modulation(N_MOD - 4)
            emptied()
            for t in range(TT):
                for g in range(2):
                    b = bank()
                    for h in (g, g + 2):
                        last = pe.matmul(b[:, (h // 2) * T:(h // 2 + 1) * T], na_q[half_of(h), h // 2, t * P:(t + 1) * P],
                                         na_k[half_of(h), h // 2, :], start=True, stop=True)
                    full(last)
                pe.wait_ge(na_exp, t + 1)
                for g in range(2):
                    b = bank()
                    for h in (2 * g, 2 * g + 1):
                        for kt in range(2):
                            last = pe.transpose(b[:, ((h % 2) * 2 + kt) * P:((h % 2) * 2 + kt + 1) * P],
                                                na_p[:, h, kt * P:(kt + 1) * P], ident)
                    full(last)
                emptied()
                b = bank()
                for h in range(NA_H):
                    for kt in range(2):
                        last = pe.matmul(b[:, h * NA_DH:(h + 1) * NA_DH], na_pT[:, h, kt, :],
                                         na_v[:, kt, h * NA_DH:(h + 1) * NA_DH], start=(kt == 0), stop=(kt == 1))
                full(last)
                emptied()
                b = bank()
                for c in range(2):
                    last = pe.transpose(b[:, c * P:(c + 1) * P],
                                        na_o.rearrange("p a b -> p (a b)")[:, c * P:(c + 1) * P], ident)
                full(last)
            pe.wait_ge(sq_ready, 1)
            for c in range(4):
                b = bank()
                full(pe.matmul(b[:, :], ones[:, :], sq[:, 2 * c:2 * c + 2, :].rearrange("p a b -> p (a b)"),
                               start=True, stop=True))
            b = bank()
            pe.wait_ge(g_ready, 1)
            gg = g_g.rearrange("p (t c) -> p t c", t=TT)
            for t in range(TT):
                pe.matmul(b[:, t * 8:t * 8 + 4], u_inc, gg[:, t, 0:4], start=True, stop=True)
                pe.matmul(b[:, t * 8 + 4:t * 8 + 8], l_inc, gg[:, t, 4:8], start=True, stop=True)
                last = pe.matmul(b[:, 16 + t * 8:24 + t * 8], ones[:, :], gg[:, t, :], start=True, stop=True)
            full(last)
            pe.wait_ge(qk_ready, 1)
            for base in (4, 8):
                for t in range(TT):
                    b = bank()
                    for h in range(GH):
                        last = pe.transpose(b[:, h * P:(h + 1) * P], g_cv[:, base + h, t * P:(t + 1) * P], ident)
                    full(last)
            op = [0]

            def operand():
                op[0] += 1
                pe.wait_ge(gd_op, op[0])

            def heads(lhsT, rhs):
                b = bank()
                for h in range(GH):
                    last = pe.matmul(b[:, h * P:(h + 1) * P], lhsT(h), rhs(h), start=True, stop=True)
                full(last)

            gb = g_be.rearrange("p (t c) -> p t c", t=TT)
            assert j[0] == GD_JOB, j[0]
            for d in range(2):
                assert j[0] == GD_JOB + GD_JOBS * d, j[0]
                tri = u_inc if d == 0 else l_inc
                for t in range(TT):
                    heads(lambda h: gg[:, t, d * 4 + h:d * 4 + h + 1].to_broadcast([P, P]), lambda h: tri)
                for t in range(TT):
                    q = lambda h: g_cv[:, h, t * P:(t + 1) * P]
                    k = lambda h: g_cv[:, 4 + h, t * P:(t + 1) * P]
                    heads(k, q)
                    heads(lambda h: gb[:, t, d * 4 + h:d * 4 + h + 1].to_broadcast([P, P]), lambda h: ident)
                    heads(k, k)
                for t in range(TT):
                    operand()
                    b = bank()
                    for h in range(GH):
                        last = pe.transpose(b[:, h * P:(h + 1) * P], tB[:, t, h, :], ident)
                    full(last)
                for lv in range(1, LEVELS):
                    for t in range(TT):
                        operand()
                        heads(lambda h: tB[:, t, h, :], lambda h: X[:, t, h, :])
                    for t in range(TT):
                        pe.wait_ge(u_copied, ((LEVELS - 1) * d + lv - 1) * TT + t + 1)
                        if lv < LEVELS - 1:
                            heads(lambda h: XT[:, t, h, :], lambda h: tU[:, t, h, :])
                        heads(lambda h: tU[:, t, h, :], lambda h: XT[:, t, h, :])
                A, B = (0, 1) if d == 0 else (1, 0)
                operand()
                heads(lambda h: XT[:, A, h, :], lambda h: tB[:, A, h, :])
                operand()
                heads(lambda h: tB[:, B, h, :], lambda h: tU[:, A, h, :])
                heads(lambda h: inT[:, A, h, :], lambda h: tU[:, A, h, :])
                operand()
                heads(lambda h: g_cv[:, 4 + h, B * P:(B + 1) * P], lambda h: X[:, 0, h, :])
                heads(lambda h: g_cv[:, h, B * P:(B + 1) * P], lambda h: X[:, 0, h, :])
                operand()
                heads(lambda h: XT[:, B, h, :], lambda h: tB[:, B, h, :])
                operand()
                heads(lambda h: inT[:, B, h, :], lambda h: tU[:, B, h, :])
            pe.wait_ge(y_ready, 2)
            for t in range(TT):
                heads_b = bank()
                for h in range(GH):
                    last = pe.transpose(heads_b[:, h * P:(h + 1) * P], o_acc[:, t, h, :], ident)
                full(last)
            pe.wait_ge(mix_ready, 1)
            for n in range(2):
                wt = weight_tile()
                for t in range(TT):
                    b = bank()
                    for k in range(KC):
                        last = pe.matmul(b[:, :], mixT[:, k, t * P:(t + 1) * P], wt[:, k, :],
                                         start=(k == 0), stop=(k == KC - 1))
                    full(last)
                used()
            pe.wait_ge(h_ready, 2)
            transposes_to_hT()
            pe.wait_ge(hT_ready, 2)
            pe.wait_ge(in_tail2, 16)
            b = bank()
            token_major(b, 0, 0, tail_w, 0, 36)
            full(token_major(b, 36, 1, tail_w, 0, 36))
            pe.wait_ge(pe_done, j[0])
            pe.sem_inc(tail_used, 1)
            pe.wait_ge(masks_ready, 1)
            b = bank()
            pe.matmul(b[:, 0:36], u_inc, M[:, 0, :], start=True, stop=True)
            pe.matmul(b[:, 36:72], ones, M[:, 0, :], start=True, stop=False)
            pe.matmul(b[:, 36:72], u_inc, M[:, 1, :], start=False, stop=True)
            pe.matmul(b[:, 72:108], ones, M[:, 0, :], start=True, stop=False)
            full(pe.matmul(b[:, 72:108], ones, M[:, 1, :], start=False, stop=True))
            emptied()
            pe.wait_ge(flag_ready, 1)
            many = pe.value_load(flag[0:1, 0:1], min_val=0, max_val=1)
            with pe.If(many == 0):
                done = Count(pe, f_done)

                def fbank():
                    pe.wait_ge(f_free, done.value(1))
                    return ps[(fj[0]) % 8]

                fj = [0]

                def ffull(ins):
                    ins.then_inc(f_done, 1)
                    done.n += 1
                    fj[0] += 1

                def gathered(pair):
                    pe.wait_ge(p_ready, pair + 1)
                    for g in range(2):
                        b = fbank()
                        for c in range(4):
                            k = 4 * g + c
                            for t in range(TT):
                                last = pe.matmul(b[:, c * P:(c + 1) * P], h_tok[:, t, k * P:(k + 1) * P],
                                                 pm[:, t, :], start=(t == 0), stop=(t == TT - 1))
                        ffull(last)

                gathered(0)
                pe.wait_ge(f_free, 8 + 2)
                with pe.Fori(0, N_EXP // 4) as i:
                    done.at(i * 24 + 2)
                    for p in range(2):
                        for r in range(2):
                            b = fbank()
                            for u in range(2):
                                wi = N_HEAD + 6 * p + 2 * r + u
                                pe.wait_ge(landed[wi % RING], i * 32 + 16 * (wi // RING + 1))
                            for k in range(KC):
                                for u in range(2):
                                    last = pe.matmul(b[u * CAP:(u + 1) * CAP, :], xeT[:, k, u * CAP:(u + 1) * CAP],
                                                     slot(N_HEAD + 6 * p + 2 * r + u)[:, k, :],
                                                     start=(k == 0), stop=(k == KC - 1), skip_group_check=True)
                            ffull(last)
                            pe.wait_ge(f_done, done.value())
                            pe.sem_inc(w_used, 2)
                        gathered(i * 2 + (p + 1))
                        pe.wait_ge(f_free, done.value(8 - 2))
                        b = fbank()
                        for c in range(4):
                            last = pe.transpose(b[:, c * P:(c + 1) * P], act_p[:, c * P:(c + 1) * P], ident)
                        ffull(last)
                        b = fbank()
                        for t in range(TT):
                            last = pe.transpose(b[:, t * P:(t + 1) * P], pg[:, p, t, :], ident)
                        ffull(last)
                        pe.wait_ge(f_free, done.value(8 - 1))
                        for n in range(2):
                            b = fbank()
                            for u in range(2):
                                wi = N_HEAD + 6 * p + 4 + u
                                pe.wait_ge(landed[wi % RING], i * 32 + 16 * (wi // RING + 1))
                            for c in range(4):
                                for u in range(2):
                                    last = pe.matmul(b[u * CAP:(u + 1) * CAP, :], actT[:, c, u * CAP:(u + 1) * CAP],
                                                     slot(N_HEAD + 6 * p + 4 + u, 1024)[:, c, n * 512:(n + 1) * 512],
                                                     start=(c == 0), stop=(c == 3), skip_group_check=True)
                            ffull(last)
                        pe.wait_ge(f_done, done.value())
                        pe.sem_inc(w_used, 2)
                        pe.wait_ge(f_free, done.value(8))
                        for t in range(TT):
                            for n in range(2):
                                b = fbank()
                                ffull(pe.matmul(b[:, :], pgT[:, t, :], y_sb[:, n * 512:(n + 1) * 512],
                                                start=True, stop=True))
                pe.wait_ge(f_free, 8 + 2 + 24 * (N_EXP // 4))
            with pe.Else():
                with pe.Fori(0, N_EXP // 2) as i:
                    for u in range(2):
                        for r in range(2):
                            wi = N_HEAD + 2 * r + u
                            pe.wait_ge(landed[wi % RING], i * 16 + 16 * (wi // RING + 1))
                            wt = slot(wi)
                            for c2 in range(2):
                                jb = 8 * u + 2 * r + c2
                                pe.wait_ge(s_free, i * 16 + (jb + 1))
                                b = ps[jb % 8]
                                for c in range(2):
                                    last = feature_major(b, c * T, wt, (2 * c2 + c) * P, P)
                                last.then_inc(s_done, 1)
                        wi = N_HEAD + 4 + u
                        pe.wait_ge(landed[wi % RING], i * 16 + 16 * (wi // RING + 1))
                        wt = slot(wi, 1024)
                        pe.wait_ge(s_free, i * 16 + (8 * u + 4 + 8))
                        for t in range(TT):
                            for n in range(2):
                                jb = 8 * u + 4 + 2 * t + n
                                pe.wait_ge(s_free, i * 16 + (jb + 1))
                                for c in range(4):
                                    last = pe.matmul(ps[jb % 8][:, :], act_d[:, c, t * P:(t + 1) * P],
                                                     wt[:, c, n * 512:(n + 1) * 512], start=(c == 0), stop=(c == 3))
                                last.then_inc(s_done, 1)
                        if u:
                            pe.wait_ge(s_done, i * 16 + (jb + 1))
                            pe.sem_inc(w_used, 6)
                pe.wait_ge(s_free, 8 + 8 * N_EXP)
            w[0] += N_MOE
            pe.wait_ge(h_ready, 3)
            transposes_to_hT()
            pe.wait_ge(hT_ready, 3)
            assert j[0] == B2_JOB, j[0]
            for n in range(2):
                wt = weight_tile()
                for t in range(TT):
                    full(token_major(bank(), 0, t, wt, 0, 512))
                used()
            wt = weight_tile()
            for c in range(2):
                b = bank()
                feature_major(b, 0, wt, c * 256, P)
                full(feature_major(b, T, wt, c * 256 + P, P))
            used()
            pe.wait_ge(in_tail2, 32)
            full(feature_major(bank(), 0, tail_w, 0, 16))
            gr_job = j[0]
            for n in range(2):
                wt = weight_tile()
                for t in range(TT):
                    full(token_major(bank(), 0, t, wt, 0, 512))
                used()
            pe.wait_ge(evac, gr_job)
            pe.wait_ge(b2_small, 80)
            b = bank()
            for g in range(2):
                last = pe.matmul(b[:, g * T:(g + 1) * T], walpha[0:16, g * P:(g + 1) * P], grT[0:16, :],
                                 start=True, stop=True)
            full(last)
            wt = weight_tile()
            for t in range(TT):
                full(token_major(bank(), 0, t, wt, 0, 512))
            used()
            pe.wait_ge(roped, 1)
            for src in (mq, mk):
                for t in range(TT):
                    b = bank()
                    for c in range(4):
                        last = pe.transpose(b[:, c * P:(c + 1) * P], src[:, t, c * P:(c + 1) * P], ident)
                    full(last)
            emptied()

            def scores(t):
                kw = (t + 1) * P
                for g in range(4):
                    b = bank()
                    h0 = 4 * (g // 2) + g % 2
                    for h in (h0, h0 + 2):
                        at = (h - h0) // 2 * T
                        last = pe.matmul(b[:, at:at + kw], qT[half_of(h), h // 2, t * P:(t + 1) * P],
                                         kT[half_of(h), h // 2, 0:kw], start=True, stop=True)
                    full(last)

            def attended(t):
                pe.wait_ge(a_exp, t + 1)
                for g in range(4):
                    b = bank()
                    for h in (2 * g, 2 * g + 1):
                        for kt in range(t + 1):
                            a = ((h % 2) * 2 + kt) * P
                            last = pe.transpose(b[:, a:a + P], sc[:, h, kt * P:(kt + 1) * P], ident)
                    full(last)
                emptied()
                b = bank()
                for h in range(AH):
                    for kt in range(t + 1):
                        last = pe.matmul(b[:, h * AD:(h + 1) * AD], pT[:, h, kt, :], mv[:, kt, h * AD:(h + 1) * AD],
                                         start=(kt == 0), stop=(kt == t))
                full(last)

            scores(0)
            pe.wait_ge(gla_op, 1)
            for p in range(2):
                b = bank()
                for i in range(2 * TT):
                    h, t = p + 2 * (i % 2), i // 2
                    last = pe.transpose(b[:, i * LDK:(i + 1) * LDK], gk[half_of(h), h // 2, t * P:(t + 1) * P],
                                        ident[half_of(h), half_of(h)])
                full(last)
            for p in range(2):
                b = bank()
                for i in range(2 * TT):
                    h, t = p + 2 * (i % 2), i // 2
                    last = pe.matmul(b[:, i * P:(i + 1) * P], kin[half_of(h), h // 2, t * P:(t + 1) * P],
                                     gq[half_of(h), h // 2, t * P:(t + 1) * P], start=True, stop=True)
                full(last)
            emptied()
            for c in range(3):
                b = bank()
                r0 = (c % 2) * CH
                for h in range(LH):
                    last = pe.matmul(b[half_of(h), (h // 2) * LDV:(h // 2 + 1) * LDV], kst[r0:r0 + CH, c // 2, h, :],
                                     gv[r0:r0 + CH, c // 2, h * LDV:(h + 1) * LDV], start=True, stop=True,
                                     tile_position=(r0, 64 * (h % 2)), skip_group_check=True)
                full(last)
            attended(0)
            scores(1)
            pe.wait_ge(gla_op, 2)
            for p in range(2):
                b = bank()
                for i in range(2 * TT):
                    h, t = p + 2 * (i % 2), i // 2
                    out = b[:, i * LDV:(i + 1) * LDV]
                    pe.matmul(out, AT[:, t, h, :], gv[:, t, h * LDV:(h + 1) * LDV], start=True, stop=False)
                    for c in (2 * t, 2 * t + 1):
                        if c:
                            last = pe.matmul(out, qz[half_of(h), h // 2, c, :], st[c][half_of(h), h // 2, :],
                                             start=False, stop=(c == 2 * t + 1))
                full(last)
            attended(1)
            pe.wait_ge(h_ready, 4)
            transposes_to_hT()
            pe.wait_ge(hT_ready, 4)
            for n in range(2):
                wt = weight_tile()
                for t in range(TT):
                    full(token_major(bank(), 0, t, wt, 0, 512))
                used()
            pe.wait_ge(h_ready, 5)
            transposes_to_hT()
            pe.wait_ge(hT_ready, 5)

            def queries():
                wt = weight_tile()
                for c in range(2):
                    b = bank()
                    feature_major(b, 0, wt, c * 256, P)
                    full(feature_major(b, T, wt, c * 256 + P, P))
                used()

            def key_scores(g, behind):
                pe.wait_ge(evac, j[0] - behind)
                for t in range(TT):
                    b = bank()
                    for c in range(4):
                        k = 4 * g + c
                        last = pe.matmul(b[:, c * P:(c + 1) * P], qpT[:, k, t * P:(t + 1) * P], subT[:, k, :],
                                         start=True, stop=True)
                    full(last)

            queries()
            pe.wait_ge(in_sub, 16)
            key_scores(0, 0)
            for g in range(3):
                queries()
            pe.wait_ge(pe_done, j[0])
            pe.sem_inc(v_free, V_RING)
            for g in range(1, 4):
                key_scores(g, 4)
            emptied()
            pe.wait_ge(zeros_ready, 1)
            for n in range(2 * TT):
                pe.matmul(ps[n][:, :], zeros, h_tok[:, 0, 0:512], start=True, stop=False, skip_group_check=True)
            for n2 in range(NG):
                with pe.Fori(0, 2) as q:
                    for t in range(TT):
                        step = q * TT + (2 * TT * n2 + t)
                        for k in range(16):
                            pe.wait_ge(diag_ready, step * 16 + (k + 1))
                            pe.wait_ge(v_landed[k], step * 16 + 16)
                            for n in range(2):
                                last = pe.matmul(ps[2 * t + n][:, :], diag[:, k % 4, :],
                                                 v_ring(k)[:, n * 512:(n + 1) * 512],
                                                 start=False, stop=False, skip_group_check=True)
                            last.then_inc(v_free, 1)
            for n in range(2 * TT):
                last = pe.matmul(ps[n][:, :], zeros, h_tok[:, 0, 0:512], start=False, stop=True, skip_group_check=True)
            last.then_inc(p_done, 1)

        @block.gpsimd
        def _(pool):
            pool.wait_ge(nw_used, 1)
            pool.dma_start(nw[:, :], io["norm_ffn_w"].to_broadcast([P, D])).then_inc(in_nw2, 16)
            pool.wait_ge(tail_used, 1)
            pool.dma_start(tail_w[:, :, :], io["router_w"].rearrange("(k p) n -> p k n", p=P)).then_inc(in_tail2, 16)
            pool.wait_ge(x1_ready, 1)
            pool.dma_start(rb, io["router_b"].to_broadcast([P, 36])).then_inc(in_route, 16)
            pool.wait_ge(nw_used, 2)
            pool.dma_start(nw[:, :], io["final_norm_w"].to_broadcast([P, D])).then_inc(in_nw2, 16)
            pool.dma_start(mod[:, 0, :], io["norm1_w_2"].to_broadcast([P, D])).then_inc(in_nw3, 16)
            pool.wait_ge(tail_used, 2)
            pool.dma_start(tail_w[:, :, 0:16], w_in2_v[:, :, 1536:1552]).then_inc(in_tail2, 16)
            pool.wait_ge(moe_done, 1)
            pool.dma_start(walpha[0:16, :], io["gla_w_alpha"]).then_inc(b2_small, 16)
            pool.dma_start(conv_g[:, 0:2], io["gla_b_alpha"]).then_inc(b2_small, 16)
            pool.dma_start(small[:, 320:448], io["gla_out_norm_w"].to_broadcast([P, P])).then_inc(b2_small, 16)
            pool.dma_start(small[:, 448:512], io["moba_q_norm_w"].to_broadcast([P, AD])).then_inc(b2_small, 16)
            pool.dma_start(mod[:, 3, 0:AD], io["moba_k_norm_w"].to_broadcast([P, AD])).then_inc(b2_small, 16)
            pool.wait_ge(nw_used, 3)
            pool.dma_start(nw[:, :], io["mix_scale"].to_broadcast([P, D])).then_inc(in_nw2, 16)
            pool.wait_ge(nw_used, 4)
            pool.dma_start(mod[:, 0, :], io["norm2_w"].to_broadcast([P, D])).then_inc(in_nw3, 16)
            pool.wait_ge(x3_ready, 1)
            pool.dma_start(subT, io["subkeys"]).then_inc(in_sub, 16)
            for n2 in range(NG):
                pool.wait_ge(idx_ready, n2 + 1)
                with pool.Fori(0, 2) as q:
                    for t in range(TT):
                        step = q * TT + (2 * TT * n2 + t)
                        pool.tensor_copy(idx_cur[:, t, :], idx_all[:, n2 % 2, t, bass.ds(q * 16, 16)])\
                            .then_inc(idx_copied, 1)
                        pool.wait_ge(idx_copied, step + 1)
                        for k in range(16):
                            pool.wait_ge(u_free, step * 16 + (k + 1))
                            pool.sem_inc(gathers, 1)
                            pool.indirect_dma_start(
                                out=u_ring(k), out_offset=None, in_=io["peer_u"],
                                in_offset=bass.IndirectOffsetOnAxis(ap=idx_cur[:, t, k:k + 1], axis=0),
                            ).then_inc(u_landed[k % U_RING], 16)
                        for k in range(16):
                            pool.wait_ge(v_free, step * 16 + (k + 1))
                            pool.sem_inc(gathers, 1)
                            pool.indirect_dma_start(
                                out=v_ring(k), out_offset=None, in_=io["peer_v"],
                                in_offset=bass.IndirectOffsetOnAxis(ap=idx_cur[:, t, k:k + 1], axis=0),
                            ).then_inc(v_landed[k], 16)

        @block.vector
        def _(dve):
            n = [0]
            j = [0]
            norms = [0]

            def o(ins):
                n[0] += 1
                ins.then_inc(dve_n, 1)

            def sync():
                if n[0]:
                    dve.wait_ge(dve_n, n[0])

            def post(s):
                sync()
                dve.sem_inc(s, 1)

            def job():
                dve.wait_ge(pe_done, j[0] + 1)
                return ps[j[0] % 8]

            def empty(*_):
                sync()
                j[0] += 1
                dve.sem_inc(evac, 1)

            def bc(ap, shape):
                return ap.to_broadcast(shape)

            def rms_scale(squares=h_tok):
                for t in range(TT):
                    o(dve.tensor_tensor_reduce(out=squares[:, t, :], in0=x[:, t, :], in1=x[:, t, :], scale=1.0 / D,
                                               scalar=0.0, op0=ALU.mult, op1=ALU.add, accum_out=ms[:, t:t + 1]))
                sync()
                o(dve.tensor_scalar(ms[:, 0:TT], ms[:, 0:TT], EPS, None, ALU.add))
                post(ms_ready)
                norms[0] += 1
                dve.wait_ge(rt_ready, norms[0])
                o(dve.reciprocal(rstd[:, 0:TT], rstd[:, 0:TT]))
                sync()

            def to_hT():
                for t in range(TT):
                    for g in range(2):
                        b = job()
                        o(dve.tensor_copy(hT[:, 4 * g:4 * g + 4, t * P:(t + 1) * P],
                                          b[:, :].rearrange("p (c n) -> p c n", c=4)))
                        empty()
                post(hT_ready)

            def norm_mod(scale, shift):
                for t in range(TT):
                    o(dve.scalar_tensor_tensor(h_tok[:, t, :], x[:, t, :], rstd[:, t:t + 1], scale,
                                               ALU.mult, ALU.mult))
                sync()
                for t in range(TT):
                    o(dve.tensor_tensor(h_tok[:, t, :], h_tok[:, t, :], shift, ALU.add))
                post(h_ready)

            dve.wait_ge(in_bias0, 32)
            dve.wait_ge(in_start, 48)
            dve.wait_ge(cond_act, 1)
            o(dve.memset(cond_z, 0.0))
            sync()
            o(dve.tensor_copy(cond_z[:, :, 0:1], g_e.unsqueeze(2)))
            post(cond_ready)
            rms_scale(hT.rearrange("p (a c) n -> p a (c n)", a=TT))
            for i in range(8):
                b = job()
                o(dve.tensor_copy(bias_rows[0:60, i * 512:(i + 1) * 512], b[0:60, :]))
                empty()
            post(bias_ready)

            def modulation_in(m, dst):
                for i in range(m):
                    b = job()
                    o(dve.tensor_copy(part[:, i % 2, :], b[:, :]))
                    empty()
                    b = job()
                    a = dst[:, i // 2, (i % 2) * 512:(i % 2 + 1) * 512]
                    o(dve.tensor_tensor(a, a, b[:, :], ALU.add))
                    empty()

            dve.wait_ge(in_ada, 32)
            modulation_in(4, ab1)
            dve.wait_ge(in_nw, 16)
            o(dve.scalar_tensor_tensor(ab1[:, 1, :], ab1[:, 1, :], 1.0, nw[:, :], ALU.add, ALU.mult))
            post(nw_used)
            norm_mod(ab1[:, 1, :], ab1[:, 0, :])
            to_hT()
            dve.wait_ge(bias_out, 16)

            for c in range(3):
                b = job()
                o(dve.tensor_copy(c3[:, 2 * c:2 * c + 2, :], b[:, :].rearrange("p (a b) -> p a b", a=2)))
                empty()
            for dst in (na_q, na_k):
                b = job()
                o(dve.tensor_copy(dst, b[:, :].rearrange("p (a b) -> p a b", a=2)))
                empty()
            b = job()
            o(dve.tensor_copy(na_v, b[:, :].rearrange("p (a b) -> p a b", a=2)))
            empty()
            b = job()
            o(dve.tensor_copy(gab, b[:, 0:32].rearrange("p (a b) -> p a b", a=2)))
            empty()
            dve.wait_ge(in_small, 80)
            t3 = lambda ap: ap.rearrange("p (t c) -> p t c", t=TT)
            o(dve.tensor_tensor(t3(g_t), gab[:, :, 0:8], bc(dt_b.unsqueeze(1), [P, TT, 8]), ALU.add))
            post(gab_in)
            for c in range(6):
                b = job()
                o(dve.tensor_copy(g_raw[:, 2 * c:2 * c + 2, :], b[:, :].rearrange("p (a b) -> p a b", a=2)))
                empty()
            for t in range(TT):
                b = job()
                o(dve.tensor_copy(z[:, t, :], b[:, :]))
                empty()

            modulation_in(N_MOD - 4, mod)
            dve.wait_ge(in_nw2, 16)
            o(dve.scalar_tensor_tensor(mod[:, 2, :], mod[:, 2, :], 1.0, nw[:, :], ALU.add, ALU.mult))
            sync()

            def conv(dst, src, taps, m):
                for c in range(m):
                    o(dve.tensor_scalar(dst(c), src(c), taps(c, 1), None, ALU.mult))
                sync()
                for c in range(m):
                    o(dve.scalar_tensor_tensor(dst(c)[:, 1:T], src(c)[:, 0:T - 1], taps(c, 0), dst(c)[:, 1:T],
                                               ALU.mult, ALU.add))
                sync()
                for c in range(m):
                    o(dve.scalar_tensor_tensor(dst(c)[:, 0:T - 1], src(c)[:, 1:T], taps(c, 2), dst(c)[:, 0:T - 1],
                                               ALU.mult, ALU.add))
                sync()

            conv(lambda c: g_cv[:, c, :], lambda c: g_raw[:, c, :],
                 lambda c, i: conv_g[:, 3 * c + i:3 * c + i + 1], 12)
            post(conv_ready)
            o(dve.tensor_tensor(c3[:, 2:4, :], c3[:, 2:4, :], c3[:, 4:6, :], ALU.mult))
            sync()
            conv(lambda c: c3[:, 4 + c, :], lambda c: c3[:, 2 + c, :],
                 lambda c, i: conv_a[:, 3 * c + i:3 * c + i + 1], 2)
            o(dve.tensor_tensor(mixT[:, 0:2, :], c3[:, 4:6, :], c3[:, 0:2, :], ALU.mult))
            dve.wait_ge(gab_act, 1)
            o(dve.scalar_tensor_tensor(g_t2, g_t, 0.0, g_t2, ALU.max, ALU.add))
            sync()
            o(dve.scalar_tensor_tensor(t3(g_g), t3(g_t2), -1.0, bc(g_e.unsqueeze(1), [P, TT, 8]),
                                       ALU.mult, ALU.mult))
            post(g_ready)
            dve.wait_ge(bias_in, 16 * N_ROWS * NA_H)
            for t in range(TT):
                for g in range(2):
                    b = job()
                    o(dve.scalar_tensor_tensor(na_p[:, g:g + 3:2, :], b[:, :].rearrange("p (a b) -> p a b", a=2),
                                               NA_DH ** -0.5, na_bias[:, t, g:g + 3:2, :], ALU.mult, ALU.add))
                    empty()
                o(dve.tensor_reduce(na_m[:, 0:4], na_p[:, :, :], AX.X, ALU.max))
                sync()
                o(dve.tensor_scalar(na_nm[:, 0:4], na_m[:, 0:4], -1.0, None, ALU.mult))
                post(na_sc)
                dve.wait_ge(na_exp, t + 1)
                o(dve.reciprocal(na_r[:, 0:4], na_s[:, 0:4]))
                for g in range(2):
                    b = job()
                    o(dve.tensor_copy(na_pT[:, 2 * g:2 * g + 2, :, :].rearrange("p a b c -> p (a b c)"), b[:, :]))
                    empty()
                b = job()
                o(dve.tensor_tensor(na_o, b[:, 0:256].rearrange("p (a b) -> p a b", a=4),
                                    bc(na_r[:, 0:4].unsqueeze(2), [P, 4, NA_DH]), ALU.mult))
                empty()
                b = job()
                o(dve.tensor_copy(mixT[:, 2:4, t * P:(t + 1) * P], b[:, 0:256].rearrange("p (a b) -> p a b", a=2)))
                empty()
            post(na_out)
            for c in range(4):
                b = job()
                o(dve.tensor_scalar(rn[:, 2 * c:2 * c + 2, :], b[:, :].rearrange("p (a b) -> p a b", a=2),
                                    EPS, None, ALU.add))
                empty()
                dve.sem_inc(l2_in, 1)
            for c in range(4):
                dve.wait_ge(l2_rt, c + 1)
                o(dve.reciprocal(rn[:, 2 * c:2 * c + 2, :], rn[:, 2 * c:2 * c + 2, :]))
            sync()
            o(dve.scalar_tensor_tensor(g_cv[:, 0:4, :], g_cv[:, 0:4, :], GD ** -0.5, rn[:, 0:4, :], ALU.mult, ALU.mult))
            o(dve.tensor_tensor(g_cv[:, 4:8, :], g_cv[:, 4:8, :], rn[:, 4:8, :], ALU.mult))
            b = job()
            o(dve.tensor_copy(g_c, b[:, 0:16]))
            o(dve.tensor_scalar(g_nc, b[:, 0:16], -1.0, None, ALU.mult))
            o(dve.tensor_copy(g_tot, b[:, 16:32]))
            empty()
            o(dve.tensor_tensor(g_kd, g_tot, g_nc, ALU.add))
            post(qk_ready)
            for dst in (k_tok, v_tok):
                for t in range(TT):
                    b = job()
                    o(dve.tensor_copy(dst[:, t, :, :].rearrange("p a b -> p (a b)"), b[:, :]))
                    empty()
            dve.wait_ge(gab_act, 2)
            b4 = lambda b: b[:, :].rearrange("p (a b) -> p a b", a=4)
            tok = lambda ap, t, d: bc(ap[:, t * 8 + d * 4:t * 8 + d * 4 + 4].unsqueeze(2), [P, 4, P])
            m = 0
            for d in range(2):
                neg = consts[:, (C_NEGF if d == 0 else C_NEGB):(C_NEGF if d == 0 else C_NEGB) + P]
                for t in range(TT):
                    b = job()
                    o(dve.tensor_tensor(tD[:, t], b4(b), bc(neg.unsqueeze(1), [P, 4, P]), ALU.add))
                    empty()
                    dve.sem_inc(d_in, 1)

                def level_block(lv, t):
                    a = C_LVL + (d * LEVELS + lv) * P
                    o(dve.tensor_tensor(tB[:, t, :, :], LT[:, t, :, :],
                                        bc(consts[:, a:a + P].unsqueeze(1), [P, 4, P]), ALU.mult))

                for t in range(TT):
                    m += 1
                    dve.wait_ge(d_out, m)
                    b = job()
                    o(dve.tensor_tensor(inT[:, t, :, :], b4(b), tD[:, t], ALU.mult))
                    empty()
                    b = job()
                    o(dve.tensor_tensor(tD[:, t], b4(b), tD[:, t], ALU.mult))
                    empty()
                    b = job()
                    o(dve.tensor_tensor(LT[:, t, :, :], b4(b), tD[:, t], ALU.mult))
                    empty()
                    level_block(0, t)
                    post(gd_op)
                id4 = bc(ident.unsqueeze(1), [P, 4, P])
                for t in range(TT):
                    o(dve.tensor_tensor(XT[:, t, :, :], id4, tB[:, t, :, :], ALU.subtract))
                    b = job()
                    o(dve.tensor_tensor(X[:, t, :, :], id4, b4(b), ALU.subtract))
                    empty()
                    level_block(1, t)
                    post(gd_op)
                for lv in range(1, LEVELS):
                    for t in range(TT):
                        job()
                        if lv < LEVELS - 1:
                            level_block(lv + 1, t)
                        dve.wait_ge(u_copied, ((LEVELS - 1) * d + lv - 1) * TT + t + 1)
                        empty()
                    for t in range(TT):
                        for dst in (X, XT) if lv < LEVELS - 1 else (XT,):
                            b = job()
                            o(dve.tensor_tensor(dst[:, t, :, :], dst[:, t, :, :], b4(b), ALU.subtract))
                            empty()
                        if lv < LEVELS - 1:
                            dve.sem_inc(gd_op, 1)
                A, B = (0, 1) if d == 0 else (1, 0)
                o(dve.tensor_tensor(tB[:, A, :, :], v_tok[:, A, :, :], tok(g_be, A, d), ALU.mult))
                post(gd_op)
                o(dve.tensor_tensor(tB[:, B, :, :], k_tok[:, A, :, :], tok(g_kd, A, d), ALU.mult))
                b = job()
                o(dve.tensor_copy(tU[:, A, :, :], b4(b)))
                empty()
                dve.sem_inc(gd_op, 1)
                b = job()
                o(dve.tensor_copy(X[:, 0, :, :], b4(b)))
                empty()
                dve.sem_inc(gd_op, 1)

                def out_add(dst, b):
                    if d == 0:
                        o(dve.tensor_copy(dst, b4(b)))
                    else:
                        o(dve.tensor_tensor(dst, dst, b4(b), ALU.add))

                b = job()
                out_add(o_acc[:, A, :, :], b)
                empty()
                b = job()
                o(dve.tensor_tensor(tD[:, 0], b4(b), tok(g_eg, B, d), ALU.mult))
                empty()
                o(dve.tensor_tensor(tD[:, 0], v_tok[:, B, :, :], tD[:, 0], ALU.subtract))
                sync()
                o(dve.tensor_tensor(tB[:, B, :, :], tD[:, 0], tok(g_be, B, d), ALU.mult))
                post(gd_op)
                b = job()
                o(dve.tensor_tensor(tD[:, 0], b4(b), tok(g_eg, B, d), ALU.mult))
                empty()
                if d == 0:
                    o(dve.tensor_copy(o_acc[:, B, :, :], tD[:, 0]))
                else:
                    o(dve.tensor_tensor(o_acc[:, B, :, :], o_acc[:, B, :, :], tD[:, 0], ALU.add))
                b = job()
                o(dve.tensor_copy(tU[:, B, :, :], b4(b)))
                empty()
                dve.sem_inc(gd_op, 1)
                b = job()
                o(dve.tensor_tensor(o_acc[:, B, :, :], o_acc[:, B, :, :], b4(b), ALU.add))
                empty()
            o(dve.tensor_tensor(X, o_acc, o_acc, ALU.mult))
            sync()
            o(dve.tensor_reduce(ms[:, 0:8], X.rearrange("p a b c -> p (a b) c"), AX.X, ALU.add))
            sync()
            o(dve.tensor_scalar(ms[:, 0:8], ms[:, 0:8], 1.0 / GD, EPS, ALU.mult, ALU.add))
            post(y_ready)
            norms[0] += 1
            dve.wait_ge(rt_ready, norms[0])
            o(dve.reciprocal(rstd[:, 0:8], rstd[:, 0:8]))
            sync()
            oa = o_acc.rearrange("p a b c -> p (a b) c")
            o(dve.tensor_tensor(oa, oa, bc(rstd[:, 0:8].unsqueeze(2), [P, 8, P]), ALU.mult))
            sync()
            o(dve.tensor_tensor(oa, oa, bc(gn_w[:, :].unsqueeze(1), [P, 8, P]), ALU.mult))
            sync()
            o(dve.tensor_tensor(oa, oa, z.rearrange("p t (h c) -> p (t h) c", h=4), ALU.mult))
            post(y_ready)
            for t in range(TT):
                b = job()
                o(dve.tensor_copy(mixT[:, 4:8, t * P:(t + 1) * P], b4(b)))
                empty()
            post(mix_ready)
            for nn in range(2):
                for t in range(TT):
                    b = job()
                    o(dve.tensor_tensor(g_raw[:, 0:2, :].rearrange("p a b -> p (a b)"), b[:, :],
                                        mod[:, 0, nn * 512:(nn + 1) * 512], ALU.mult))
                    empty()
                    o(dve.tensor_tensor(x[:, t, nn * 512:(nn + 1) * 512], x[:, t, nn * 512:(nn + 1) * 512],
                                        g_raw[:, 0:2, :].rearrange("p a b -> p (a b)"), ALU.add))
                    sync()
            post(x1_ready)
            rms_scale()
            norm_mod(mod[:, 2, :], mod[:, 1, :])
            dve.sem_inc(nw_used, 1)
            to_hT()
            dve.wait_ge(in_route, 16)
            b = job()
            o(dve.tensor_tensor(lg, b[:, 0:72].rearrange("p (t n) -> p t n", t=TT), bc(rb.unsqueeze(1), [P, TT, 36]),
                                ALU.add))
            empty()
            o(dve.tensor_reduce(gmx, lg[:, :, 0:4], AX.X, ALU.max))
            o(dve.memset(acc, 0.0))
            o(dve.memset(G, 0.0))
            o(dve.memset(M, 0.0))
            sync()
            gm4 = bc(gmx.unsqueeze(2), [P, TT, N_GRP])
            o(dve.tensor_tensor(oh4, lg[:, :, 0:4], gm4, ALU.is_equal))
            o(dve.tensor_tensor(e4, lg[:, :, 0:4], gm4, ALU.subtract))
            post(rt_logits)
            o(dve.tensor_tensor(oh4, oh4, bc(consts[:, C_DN4:C_DN4 + N_GRP].unsqueeze(1), [P, TT, N_GRP]), ALU.mult))
            sync()
            o(dve.tensor_reduce(gmx, oh4, AX.X, ALU.max))
            sync()
            o(dve.tensor_tensor(oh4, oh4, gm4, ALU.is_equal))
            sync()
            o(dve.tensor_scalar(pen, oh4, -NEG, NEG, ALU.mult, ALU.add))
            dve.wait_ge(rt_exp, 1)
            o(dve.tensor_reduce(pgt, e4, AX.X, ALU.add))
            sync()
            o(dve.reciprocal(pgt, pgt))
            for t in range(TT):
                o(dve.tensor_tensor(elm[:, t, :].rearrange("p (g e) -> p g e", g=N_GRP),
                                    lg[:, t, 4:36].rearrange("p (g e) -> p g e", g=N_GRP),
                                    bc(pen[:, t, :].unsqueeze(2), [P, N_GRP, EPG]), ALU.add))
            sync()
            for t in range(TT):
                o(dve.max(v8[:, t, :], elm[:, t, :]))
            sync()
            for t in range(TT):
                o(dve.max_index(i8[:, t, :], v8[:, t, :], elm[:, t, :]))
            o(dve.tensor_tensor(gt[:, :, 0:1], v8[:, :, 1:2], v8[:, :, 0:1], ALU.subtract))
            post(rt_logits)
            o(dve.tensor_copy(i8f, i8))
            dve.wait_ge(rt_exp, 2)
            o(dve.tensor_scalar(gt[:, :, 1:2], gt[:, :, 0:1], 1.0, None, ALU.add))
            sync()
            o(dve.reciprocal(gt[:, :, 1:2], gt[:, :, 1:2]))
            sync()
            o(dve.tensor_tensor(gt[:, :, 2:3], gt[:, :, 1:2], pgt.unsqueeze(2), ALU.mult))
            sync()
            o(dve.tensor_tensor(gt[:, :, 3:4], gt[:, :, 2:3], gt[:, :, 0:1], ALU.mult))
            io32 = consts[:, C_IOTA:C_IOTA + N_EXP]
            for t in range(TT):
                o(dve.tensor_scalar(M[:, t, 0:N_EXP], io32, i8f[:, t, 0:1], None, ALU.is_equal))
                o(dve.tensor_scalar(rk[:, t, 0:N_EXP], io32, i8f[:, t, 1:2], None, ALU.is_equal))
            sync()
            for t in range(TT):
                o(dve.tensor_scalar(G[:, t, 0:N_EXP], rk[:, t, 0:N_EXP], gt[:, t, 3:4], None, ALU.mult))
            sync()
            for t in range(TT):
                o(dve.scalar_tensor_tensor(G[:, t, 0:N_EXP], M[:, t, 0:N_EXP], gt[:, t, 2:3], G[:, t, 0:N_EXP],
                                           ALU.mult, ALU.add))
            sync()
            o(dve.tensor_tensor(M[:, :, 0:N_EXP], M[:, :, 0:N_EXP], rk[:, :, 0:N_EXP], ALU.add))
            post(masks_ready)
            b = job()
            o(dve.tensor_tensor(rk, b[:, 0:72].rearrange("p (t n) -> p t n", t=TT), M, ALU.mult))
            o(dve.tensor_reduce(cnt[:, 0:1], b[:, 72:104], AX.X, ALU.max))
            empty()
            o(dve.tensor_scalar(rk, rk, -1.0, None, ALU.add))
            o(dve.tensor_scalar(flag[:, 0:1], cnt[:, 0:1], float(CAP) + 0.5, None, ALU.is_gt))
            post(flag_ready)
            many = dve.value_load(flag[0:1, 0:1], min_val=0, max_val=1)
            with dve.If(many == 0):
                own = Count(dve, f_dve)
                fj = [0]
                io64 = consts[:, C_IOTA:C_IOTA + CAP]

                def f(ins):
                    ins.then_inc(f_dve, 1)
                    own.n += 1

                done = Count(dve, f_done)

                def fjob():
                    done.n += 1
                    done.wait()
                    fj[0] += 1
                    return ps[(fj[0] - 1) % 8]

                def fempty():
                    own.wait()
                    dve.sem_inc(f_free, 1)

                def selection(c, q):
                    for t in range(TT):
                        for u in range(2):
                            f(dve.tensor_scalar(pm[:, t, u * CAP:(u + 1) * CAP], io64, rk4[:, t, c + u:c + u + 1], None,
                                                ALU.is_equal))
                            f(dve.tensor_scalar(pg[:, q, t, u * CAP:(u + 1) * CAP], io64, rk4[:, t, c + u:c + u + 1],
                                                g4[:, t, c + u:c + u + 1], ALU.is_equal, ALU.mult))
                    own.wait()
                    dve.sem_inc(p_ready, 1)

                def rows_in():
                    for g in range(2):
                        b = fjob()
                        f(dve.tensor_copy(xeT[:, 4 * g:4 * g + 4, :], b[:, :].rearrange("p (c n) -> p c n", c=4)))
                        fempty()

                dve.sem_inc(f_free, 8)
                f(dve.tensor_copy(rk4[:, :, 0:2], rk[:, :, 0:2]))
                f(dve.tensor_copy(g4[:, :, 0:2], G[:, :, 0:2]))
                own.wait()
                selection(0, 0)
                rows_in()
                per, first = F_OPS, own.n
                with dve.Fori(0, N_EXP // 4) as i:
                    own.at(i * per + first)
                    done.at(i * 24 + 2)
                    own.wait()
                    f(dve.tensor_copy(rk4[:, :, :], rk[:, :, bass.ds(i * 4 + 2, 4)]))
                    f(dve.tensor_copy(g4[:, :, :], G[:, :, bass.ds(i * 4 + 2, 4)]))
                    own.wait()
                    for p in range(2):
                        selection(2 * p, 1 - p)
                        b = fjob()
                        dve.wait_ge(f_act, i * 2 + (p + 1))
                        dve.sem_inc(f_free, 1)
                        b = fjob()
                        f(dve.tensor_tensor(act_p, sil, b[:, :], ALU.mult))
                        fempty()
                        rows_in()
                        b = fjob()
                        f(dve.tensor_copy(actT.rearrange("p a b -> p (a b)"), b[:, :]))
                        fempty()
                        b = fjob()
                        f(dve.tensor_copy(pgT.rearrange("p a b -> p (a b)"), b[:, 0:TT * P]))
                        fempty()
                        for n2 in range(2):
                            b = fjob()
                            f(dve.tensor_copy(y_sb[:, n2 * 512:(n2 + 1) * 512], b[:, :]))
                            fempty()
                        for t in range(TT):
                            for n2 in range(2):
                                b = fjob()
                                a = acc[:, t, n2 * 512:(n2 + 1) * 512]
                                f(dve.tensor_tensor(a, a, b[:, :], ALU.add))
                                fempty()
                    assert own.n == per, own.n
                    assert done.n == 24
                dve.wait_ge(f_dve, per * (N_EXP // 4) + first)
            with dve.Else():
                dve.sem_inc(s_free, 8)
                own = Count(dve, s_dve)

                def f(ins):
                    ins.then_inc(s_dve, 1)
                    own.n += 1

                per = S_OPS
                with dve.Fori(0, N_EXP // 2) as i:
                    own.at(i * per)
                    f(dve.tensor_copy(g4[:, :, 0:2], G[:, :, bass.ds(i * 2, 2)]))
                    for u in range(2):
                        for c in range(2):
                            dve.wait_ge(s_act, i * 4 + (2 * u + c + 1))
                            dve.sem_inc(s_free, 1)
                        for c in range(2):
                            dve.wait_ge(s_done, i * 16 + (8 * u + 2 + c + 1))
                            f(dve.tensor_tensor(act_d[:, 2 * c:2 * c + 2, :], sil_d[:, 2 * c:2 * c + 2, :],
                                                ps[2 + c][:, :].rearrange("p (a b) -> p a b", a=2), ALU.mult))
                            own.wait()
                            dve.sem_inc(s_free, 1)
                        for t in range(TT):
                            for n2 in range(2):
                                jb = 8 * u + 4 + 2 * t + n2
                                dve.wait_ge(s_done, i * 16 + (jb + 1))
                                a = acc[:, t, n2 * 512:(n2 + 1) * 512]
                                f(dve.scalar_tensor_tensor(a, ps[jb % 8][:, :], g4[:, t, u:u + 1], a,
                                                           ALU.mult, ALU.add))
                                own.wait()
                                dve.sem_inc(s_free, 1)
                    assert own.n == per, own.n
            for t in range(TT):
                o(dve.tensor_tensor(acc[:, t, :], acc[:, t, :], mod[:, 3, :], ALU.mult))
            sync()
            for t in range(TT):
                o(dve.tensor_tensor(x[:, t, :], x[:, t, :], acc[:, t, :], ALU.add))
            sync()
            dve.sem_inc(moe_done, 1)
            rms_scale()
            dve.wait_ge(in_nw2, 32)
            for t in range(TT):
                o(dve.scalar_tensor_tensor(x[:, t, :], x[:, t, :], rstd[:, t:t + 1], nw[:, :], ALU.mult, ALU.mult))
            post(nw_used)

            def norm_weight(m):
                rms_scale()
                dve.wait_ge(in_nw3, m)
                for t in range(TT):
                    o(dve.scalar_tensor_tensor(h_tok[:, t, :], x[:, t, :], rstd[:, t:t + 1], mod[:, 0, :],
                                               ALU.mult, ALU.mult))
                post(h_ready)
                dve.sem_inc(nw_used, 1)
                to_hT()

            norm_weight(16)
            two = lambda b: b[:, :].rearrange("p (a b) -> p a b", a=2)
            h8 = lambda ap: ap.rearrange("p (h c) -> p h c", h=AH)
            for i in range(2 * TT):
                b = job()
                o(dve.tensor_copy(mqk[:, i, :], b[:, :]))
                empty()
            o(dve.tensor_tensor(rt, mqk, mqk, ALU.mult))
            sync()
            o(dve.tensor_reduce(a_ms, rt.rearrange("p i (h c) -> p (i h) c", h=AH), AX.X, ALU.add))
            sync()
            o(dve.tensor_scalar(a_ms, a_ms, 1.0 / AD, EPS, ALU.mult, ALU.add))
            post(a_in)
            dve.wait_ge(a_rt, 1)
            o(dve.reciprocal(a_rs, a_ms))
            sync()
            qk_heads = mqk.rearrange("p i (h c) -> p (i h) c", h=AH)
            o(dve.tensor_tensor(qk_heads, qk_heads, bc(a_rs.unsqueeze(2), [P, 2 * TT * AH, AD]), ALU.mult))
            sync()
            dve.wait_ge(b2_small, 80)
            for m, wn in enumerate((small[:, 448:512], mod[:, 3, 0:AD])):
                half = qk_heads[:, m * TT * AH:(m + 1) * TT * AH, :]
                o(dve.tensor_tensor(half, half, bc(wn.unsqueeze(1), [P, TT * AH, AD]), ALU.mult))
            sync()
            for i in range(2 * TT):
                t = i % TT
                cs = bc(consts[:, C_ROPE + t * 32:C_ROPE + (t + 1) * 32].unsqueeze(1), [P, AH, 32])
                sn = bc(consts[:, C_ROPE + 64 + t * 32:C_ROPE + 64 + (t + 1) * 32].unsqueeze(1), [P, AH, 32])
                lo, hi = h8(mqk[:, i, :])[:, :, 0:32], h8(mqk[:, i, :])[:, :, 32:64]
                r4 = rt[:, 2 * (i % 2):2 * (i % 2) + 2, :].rearrange("p a (q h c) -> p (a q) h c", q=2, h=AH)
                o(dve.tensor_tensor(r4[:, 0], lo, cs, ALU.mult))
                o(dve.tensor_tensor(r4[:, 1], hi, sn, ALU.mult))
                o(dve.tensor_tensor(r4[:, 2], hi, cs, ALU.mult))
                o(dve.tensor_tensor(r4[:, 3], lo, sn, ALU.mult))
                sync()
                o(dve.tensor_tensor(lo, r4[:, 0], r4[:, 1], ALU.subtract))
                o(dve.tensor_tensor(hi, r4[:, 2], r4[:, 3], ALU.add))
            post(roped)
            for dst in (gq, gk):
                b = job()
                o(dve.tensor_copy(dst, two(b)))
                empty()
            b = job()
            o(dve.tensor_copy(grT[0:16, :], b[0:16, 0:T]))
            empty()
            for i in range(2 * TT):
                job()
                dve.wait_ge(v_copied, i + 1)
                empty()
            b = job()
            for g in range(2):
                o(dve.tensor_scalar(gb_[:, g, :], b[:, g * T:(g + 1) * T], conv_g[:, g:g + 1], None, ALU.add))
            empty()
            o(dve.tensor_scalar(ge, gb_, -1.0, None, ALU.mult))
            sync()
            o(dve.tensor_tensor(ge, ge, gb_, ALU.max))
            post(z_in)
            dve.wait_ge(z_act, 2)
            o(dve.scalar_tensor_tensor(gb_, gb_, 0.0, ge, ALU.min, ALU.subtract))
            sync()
            o(dve.tensor_scalar(ge, gb_, 1.0 / 16.0, None, ALU.mult))
            sync()
            for h in range(LH // 2):
                for c in range(4):
                    o(dve.tensor_tensor_scan(gb_[:, h, c * CH:(c + 1) * CH], ones[:, 0:CH],
                                             ge[:, h, c * CH:(c + 1) * CH], 0.0, ALU.mult, ALU.add))
            post(b_in)
            o(dve.memset(qz, 0.0))
            dve.wait_ge(b_act, 1)
            o(dve.scalar_tensor_tensor(gq, gq, LDK ** -0.5, ge, ALU.mult, ALU.mult))
            o(dve.tensor_copy(g_t[:, 0:8].rearrange("p (h c) -> p h c", h=LH // 2),
                              ge.rearrange("p h (c n) -> p h c n", c=4)[:, :, :, CH - 1]))
            post(b_in)
            for t in range(TT):
                b = job()
                o(dve.tensor_copy(mv[:, t, :], b[:, :]))
                empty()
            for dst in (qT, kT):
                for t in range(TT):
                    b = job()
                    o(dve.tensor_copy(dst[:, :, t * P:(t + 1) * P], b4(b)))
                    empty()
            for c in range(4):
                o(dve.tensor_copy(qz[:, :, c, (c % 2) * CH:(c % 2 + 1) * CH], gq[:, :, c * CH:(c + 1) * CH]))
            dve.wait_ge(b_act, 2)
            o(dve.tensor_tensor(kin, gk, ge, ALU.mult))
            sync()
            for h in range(LH // 2):
                b4c = gb_[:, h, :].rearrange("p (c n) -> p c n", c=4)
                o(dve.tensor_tensor(ge[:, h, :].rearrange("p (c n) -> p c n", c=4),
                                    bc(b4c[:, :, CH - 1:CH], [P, 4, CH]), b4c, ALU.subtract))
            post(b_in)
            tri = consts[:, C_NEGB:C_NEGB + P]

            def scores_out(t):
                kw = (t + 1) * P
                for g in range(4):
                    b = job()
                    h0 = 4 * (g // 2) + g % 2
                    if t:
                        o(dve.tensor_scalar(sc[:, h0:h0 + 3:2, 0:P], two(b)[:, :, 0:P], AD ** -0.5, None, ALU.mult))
                    o(dve.scalar_tensor_tensor(sc[:, h0:h0 + 3:2, t * P:kw], two(b)[:, :, t * P:kw], AD ** -0.5,
                                               bc(tri.unsqueeze(1), [P, 2, P]), ALU.mult, ALU.add))
                    empty()
                o(dve.tensor_reduce(na_m[:, 0:8], sc[:, :, 0:kw], AX.X, ALU.max))
                sync()
                o(dve.tensor_scalar(na_nm[:, 0:8], na_m[:, 0:8], -1.0, None, ALU.mult))
                post(a_op)

            def attended_out(t):
                dve.wait_ge(a_exp, t + 1)
                o(dve.reciprocal(na_r[:, 0:8], na_s[:, 0:8]))
                for g in range(4):
                    b = job()
                    o(dve.tensor_copy(pT[:, 2 * g:2 * g + 2, 0:t + 1, :],
                                      b[:, :].rearrange("p (a k n) -> p a k n", a=2, k=2)[:, :, 0:t + 1, :]))
                    empty()
                b = job()
                o(dve.tensor_tensor(h8(y2[:, t, 512:1024]), h8(b[:, :]), bc(na_r[:, 0:8].unsqueeze(2), [P, AH, AD]),
                                    ALU.mult))
                empty()

            scores_out(0)
            dve.wait_ge(b_act, 3)
            o(dve.tensor_tensor(gk, gk, ge, ALU.mult))
            post(gla_op)
            tiles_heads = lambda ap, n: ap.rearrange("p (t h c) -> p t h c", t=TT, c=n)
            for p in range(2):
                b = job()
                for t in range(TT):
                    o(dve.tensor_copy(kst[:, t, p:p + 3:2, :], tiles_heads(b[:, 0:256], LDK)[:, t]))
                empty()
            for p in range(2):
                b = job()
                for t in range(TT):
                    o(dve.tensor_tensor(AT[:, t, p:p + 3:2, :], tiles_heads(b[:, :], P)[:, t],
                                        bc(consts[:, C_BLK:C_BLK + P].unsqueeze(1), [P, 2, P]), ALU.mult))
                empty()
            dec = g_t[:, 0:8].rearrange("p (h c) -> p h c", h=LH // 2)
            for c in range(3):
                b = job()
                if c == 0:
                    o(dve.tensor_copy(st[1], b4(b)[:, 0:2]))
                else:
                    o(dve.tensor_tensor(st[c + 1], st[c], bc(dec[:, :, c:c + 1], [P, LH // 2, LDV]), ALU.mult))
                    sync()
                    o(dve.tensor_tensor(st[c + 1], st[c + 1], b4(b)[:, 0:2], ALU.add))
                empty()
            post(gla_op)
            attended_out(0)
            scores_out(1)
            for p in range(2):
                b = job()
                for t in range(TT):
                    o(dve.tensor_copy(y2[:, t, 0:512].rearrange("p (h c) -> p h c", h=LH)[:, p:p + 3:2, :],
                                      tiles_heads(b[:, :], LDV)[:, t]))
                empty()
            sq_o = W(6656, TT, 512)
            o(dve.tensor_tensor(sq_o, y2[:, :, 0:512], y2[:, :, 0:512], ALU.mult))
            sync()
            o(dve.tensor_reduce(ms[:, 0:8], sq_o.rearrange("p t (h c) -> p (t h) c", h=LH), AX.X, ALU.add))
            sync()
            o(dve.tensor_scalar(ms[:, 0:8], ms[:, 0:8], 1.0 / LDV, EPS, ALU.mult, ALU.add))
            post(o_in)
            norms[0] += 1
            hd = lambda ap: ap.rearrange("p (h c) -> p h c", h=4)
            for t in range(TT):
                o(dve.tensor_tensor(hd(y2[:, t, 0:512]), hd(y2[:, t, 0:512]),
                                    bc(small[:, 320:448].unsqueeze(1), [P, 4, P]), ALU.mult))
            sync()
            o(dve.tensor_tensor(y2[:, :, 0:512], y2[:, :, 0:512], ggate, ALU.mult))
            attended_out(1)
            dve.wait_ge(rt_ready, norms[0])
            o(dve.reciprocal(rstd[:, 0:8], rstd[:, 0:8]))
            sync()
            for t in range(TT):
                o(dve.tensor_tensor(hd(y2[:, t, 0:512]), hd(y2[:, t, 0:512]),
                                    bc(rstd[:, 4 * t:4 * t + 4].unsqueeze(2), [P, 4, P]), ALU.mult))
            sync()
            dve.wait_ge(in_nw2, 48)
            for t in range(TT):
                o(dve.tensor_tensor(y2[:, t, :], y2[:, t, :], nw[:, :], ALU.mult))
            post(h_ready)
            dve.sem_inc(nw_used, 1)
            to_hT()
            for nn in range(2):
                for t in range(TT):
                    b = job()
                    o(dve.tensor_tensor(x[:, t, nn * 512:(nn + 1) * 512], x[:, t, nn * 512:(nn + 1) * 512], b[:, :],
                                        ALU.add))
                    empty()
            post(x3_ready)
            norm_weight(32)

            def queries_in(g):
                for c in range(2):
                    b = job()
                    o(dve.tensor_copy(qpT[:, 4 * g + 2 * c:4 * g + 2 * c + 2, :], two(b)))
                    empty()

            def scores_in(g):
                for t in range(TT):
                    b = job()
                    o(dve.tensor_copy(s_all[:, t, 4 * g:4 * g + 4, :], b4(b)))
                    empty()

            def best16(rows, val, ind, src):
                for r in range(rows):
                    o(dve.max(val(r)[:, 0:8], src(r)))
                sync()
                for r in range(rows):
                    o(dve.max_index(ind(r)[:, 0:8], val(r)[:, 0:8], src(r)))
                sync()
                for r in range(rows):
                    o(dve.match_replace(src(r), val(r)[:, 0:8], src(r), NEG))
                sync()
                for r in range(rows):
                    o(dve.max(val(r)[:, 8:16], src(r)))
                sync()
                for r in range(rows):
                    o(dve.max_index(ind(r)[:, 8:16], val(r)[:, 8:16], src(r)))
                sync()

            def route(g):
                best16(4 * TT, lambda r: sv[:, r, :], lambda r: si[:, r, :],
                       lambda r: s_all[:, r // 4, 4 * g + r % 4, :])
                o(dve.tensor_copy(sif, si))
                for r in range(2 * TT):
                    o(dve.tensor_tensor(cand[:, r, :, :], bc(sv[:, 2 * r, :].unsqueeze(2), [P, 16, 16]),
                                        bc(sv[:, 2 * r + 1, :].unsqueeze(1), [P, 16, 16]), ALU.add))
                sync()
                best16(2 * TT, lambda r: tv[:, r, :], lambda r: ti[:, r, :],
                       lambda r: cand[:, r, :, :].rearrange("p a b -> p (a b)"))
                gv3 = gates[:, g % 2, :, :].rearrange("p t (h k) -> p (t h) k", h=2)
                o(dve.tensor_tensor(gv3, tv, bc(tv[:, :, 0:1], [P, 2 * TT, 16]), ALU.subtract))
                post(e_in)
                o(dve.tensor_scalar(tj, ti, 15, None, ALU.bitwise_and))
                sync()
                o(dve.tensor_scalar(ti, ti, 4, None, ALU.logical_shift_right))
                o(dve.tensor_copy(tjf, tj))
                sync()
                o(dve.tensor_copy(tif, ti))
                sync()
                io16 = consts[:, C_IOTA:C_IOTA + 16]
                for half, (pos, dst) in enumerate(((tif, e0), (tjf, e1))):
                    o(dve.tensor_tensor(oh.rearrange("p a b c -> p (a b) c"), bc(io16.unsqueeze(1), [P, 2 * TT * 16, 16]),
                                        bc(pos.rearrange("p a b -> p (a b)").unsqueeze(2), [P, 2 * TT * 16, 16]),
                                        ALU.is_equal))
                    sync()
                    for r in range(2 * TT):
                        o(dve.tensor_tensor(oh[:, r, :, :], oh[:, r, :, :],
                                            bc(sif[:, 2 * r + half, :].unsqueeze(1), [P, 16, 16]), ALU.mult))
                    sync()
                    o(dve.tensor_reduce(dst.rearrange("p a b -> p (a b)"), oh.rearrange("p a b c -> p (a b) c"),
                                        AX.X, ALU.add))
                    sync()
                o(dve.scalar_tensor_tensor(e0, e0, float(PK), e1, ALU.mult, ALU.add))
                sync()
                o(dve.tensor_copy(idx_all[:, g % 2, :, :].rearrange("p t k -> p (t k)"), e0.rearrange("p a b -> p (a b)")))
                post(idx_ready)
                dve.wait_ge(e_act, g + 1)
                o(dve.tensor_reduce(gsum, gv3, AX.X, ALU.add))
                sync()
                o(dve.reciprocal(gsum, gsum))
                sync()
                o(dve.tensor_tensor(gv3, gv3, bc(gsum.unsqueeze(2), [P, 2 * TT, 16]), ALU.mult))
                sync()

            queries_in(0)
            scores_in(0)
            dve.sem_inc(u_free, U_RING)
            route(0)
            for g in range(1, 4):
                queries_in(g)
            for g in range(1, 4):
                scores_in(g)
            o(dve.memset(zeros, 0.0))
            post(zeros_ready)
            for n2 in range(NG):
                for q in range(2):
                    if q and n2 < NG - 1:
                        route(n2 + 1)
                    for t in range(TT):
                        step = q * TT + (2 * TT * n2 + t)
                        for k in range(16):
                            dve.wait_ge(u_landed[k % U_RING], step * 32 + 16 * (k // U_RING + 1))
                            dve.wait_ge(u_free, step * 16 + (U_RING + k - 1))
                            dve.tensor_tensor_reduce(out=junk[:, k % 2, :], in0=u_ring(k), in1=h_tok[:, t, :], scale=1.0,
                                                     scalar=0.0, op0=ALU.mult, op1=ALU.add,
                                                     accum_out=dots[:, t, k:k + 1]).then_inc(u_free, 1)
                        dve.wait_ge(gelu_done, step + 1)
                        dve.tensor_tensor(w_cur[:, t, :], gel[:, t, :],
                                          gates[:, n2 % 2, t, q * 16:(q + 1) * 16], ALU.mult).then_inc(w_ready, 1)
            dve.wait_ge(p_done, 1)
            for t in range(TT):
                for n2 in range(2):
                    xs = x[:, t, n2 * 512:(n2 + 1) * 512]
                    o(dve.tensor_tensor(xs, xs, ps[2 * t + n2][:, :], ALU.add))
                post(p_taken)


def kernel(**inputs):
    import concourse.bacc as _bacc
    from concourse.bass_utils import run_bass_kernel_spmd as _run

    f = {k: np.asarray(v) for k, v in inputs.items()}
    rows = lambda a: np.ascontiguousarray(a.reshape(1, -1))
    arrays = {
        "x": f["x"][0],
        "c": np.ascontiguousarray(f["c"].reshape(KC, P).T),
        "consts": shape_constants(),
        "window": window_selector(),
        "w_ada": f["w_ada"][0],
        "b_ada": f["b_ada"],
        "norm_mix_w": f["norm_mix_w"],
        "norm_ffn_w": f["norm_ffn_w"],
        "w_in": f["w_in"][0],
        "conv_a_w": np.ascontiguousarray(f["conv_a_w"][0].reshape(3, 2, P).transpose(2, 1, 0).reshape(P, 6)),
        "gdn_conv_w": np.ascontiguousarray(f["gdn_conv_w"][0].reshape(3, 12, P).transpose(2, 1, 0).reshape(P, 36)),
        "gdn_a_log": rows(f["gdn_a_log"]),
        "gdn_dt_bias": rows(f["gdn_dt_bias"]),
        "gdn_norm_w": f["gdn_norm_w"],
        "na_rpb": np.concatenate([f["na_rpb"][0].reshape(NA_H * N_DR, N_DC).T,
                                  np.ones((1, NA_H * N_DR), np.float32)]),
        "w_out": f["w_out"][0],
        "router_w": np.concatenate([f["router_group_w"][0], f["router_expert_w"][0]], axis=1),
        "router_b": np.concatenate([f["router_group_b"], f["router_expert_b"]], axis=1),
        "expert_w1": f["expert_w1"][0],
        "expert_w3": f["expert_w3"][0],
        "expert_w2": f["expert_w2"][0],
        "final_norm_w": rows(f["final_norm_w"]),
        "norm1_w_2": f["norm1_w_2"],
        "w_in_2": f["w_in_2"][0],
        "gla_w_alpha": f["gla_w_alpha_2"][0],
        "gla_b_alpha": np.ascontiguousarray(f["gla_b_alpha_2"][0].reshape(2, P).T),
        "gla_out_norm_w": f["gla_out_norm_w_2"],
        "moba_q_norm_w": f["moba_q_norm_w_2"],
        "moba_k_norm_w": f["moba_k_norm_w_2"],
        "mix_scale": f["mix_scale_2"],
        "w_out_2": f["w_out_2"][0],
        "norm2_w": f["norm2_w_2"],
        "peer_w_query": f["peer_w_query_2"][0],
        "subkeys": np.ascontiguousarray(f["peer_subkeys_2"][0].reshape(16, PK, P).transpose(2, 0, 1)),
        "peer_u": f["peer_u_2"][0],
        "peer_v": f["peer_v_2"][0],
    }
    nc = _bacc.Bacc("TRN2", target_bir_lowering=False, num_devices=1)
    io, feed = {}, {}
    for name, a in arrays.items():
        a = np.ascontiguousarray(a)
        feed[name + "_d"] = a
        io[name] = nc.dram_tensor(name + "_d", a.shape, mybir.dt.from_np(a.dtype), kind="ExternalInput").ap()
    io["out"] = nc.dram_tensor("out_d", (T, D), F32, kind="ExternalOutput").ap()
    two_blocks(nc, io)
    r = _run(nc, [feed], core_ids=[0])
    return r.results[0]["out_d"].reshape(1, T, D)
```
